# Optimizing a Trainium2 kernel written in Bass

```python
import numpy as np
import jax, jax.numpy as jnp
from jax import lax

D_MODEL = 1024
BATCH = 1
SEQ = 512
DEPTH = 1

GRID_W = 64
MIX_WIDTH = D_MODEL
NA_HEADS = 8
NA_WIDTH = MIX_WIDTH // 2
NA_HEAD_DIM = NA_WIDTH // NA_HEADS
NA_WIN_ROWS = 8
NA_WIN_COLS = 16
HG_HEADS = 4
HG_WIDTH = MIX_WIDTH // 4
HG_VAL_DIM = HG_WIDTH // HG_HEADS
HG_KEY_DIM = 64
HG_KWIDTH = HG_HEADS * HG_KEY_DIM
HG_CHUNK = 64
MEM_TOKENS = 256
MEM_HEADS = 4
MEM_WIDTH = MIX_WIDTH // 4
MEM_HEAD_DIM = MEM_WIDTH // MEM_HEADS
IN_SPLITS = (NA_WIDTH, NA_WIDTH, NA_WIDTH,
             HG_KWIDTH, HG_KWIDTH, HG_KWIDTH,
             HG_WIDTH, HG_WIDTH,
             MEM_WIDTH)
IN_WIDTH = sum(IN_SPLITS)
PEER_HEADS = 8
PEER_NKEYS = 128
PEER_TOPK = 16
PEER_QDIM = 256
N_EXPERTS = PEER_NKEYS * PEER_NKEYS
PEER_BLOCK = 128
RMS_EPS = 1e-6

kernel_name = 'hybrid_natten_hgrn2_memxattn_peer_encoder'

def _rms_normalize(x):
    xf = x.astype(jnp.float32)
    return xf * lax.rsqrt(jnp.mean(xf * xf, axis=-1, keepdims=True) + RMS_EPS)

def rmsnorm(x, g):
    return (_rms_normalize(x) * g.astype(jnp.float32)).astype(x.dtype)

def neighbourhood_attention(q, k, v, rpb):
    B, T, H, Dh = q.shape
    rows = T // GRID_W
    wr = min(NA_WIN_ROWS, rows)
    wc = NA_WIN_COLS
    cols = np.arange(GRID_W)
    c0 = np.clip(cols - wc // 2, 0, GRID_W - wc)
    col_idx = c0[:, None] + np.arange(wc)[None, :]
    dc = col_idx - cols[:, None] + (NA_WIN_COLS - 1)
    bias_c = rpb[:, :, dc]
    qg = q.reshape(B, rows, GRID_W, H, Dh)
    kg = k.reshape(B, rows, GRID_W, H, Dh)
    vg = v.reshape(B, rows, GRID_W, H, Dh)
    scale = Dh ** -0.5

    def one_row(r):
        rs = jnp.clip(r - wr // 2, 0, rows - wr)
        kb = lax.dynamic_slice_in_dim(kg, rs, wr, axis=1)
        vb = lax.dynamic_slice_in_dim(vg, rs, wr, axis=1)
        kw = kb[:, :, col_idx]
        vw = vb[:, :, col_idx]
        qr = lax.dynamic_index_in_dim(qg, r, axis=1, keepdims=False)
        dr = rs + jnp.arange(wr) - r + (NA_WIN_ROWS - 1)
        bias = jnp.take(bias_c, dr, axis=1).transpose(0, 2, 1, 3)
        s = jnp.einsum('bqhd,brqjhd->bhqrj', qr, kw) * scale + bias[None].astype(qr.dtype)
        p = jax.nn.softmax(s.reshape(B, H, GRID_W, wr * wc).astype(jnp.float32), axis=-1)
        p = p.reshape(B, H, GRID_W, wr, wc).astype(v.dtype)
        return jnp.einsum('bhqrj,brqjhd->bqhd', p, vw)

    out = lax.map(one_row, jnp.arange(rows))
    return out.transpose(1, 0, 2, 3, 4).reshape(B, T, H * Dh)

def hgrn2_scan(q, k, v, log_f):
    B, T, H, K = q.shape
    V = v.shape[-1]
    n = T // HG_CHUNK

    def to_chunks(a):
        return a.reshape(B, n, HG_CHUNK, H, a.shape[-1]).transpose(1, 0, 2, 3, 4)

    causal_in_chunk = jnp.tril(jnp.ones((HG_CHUNK, HG_CHUNK), dtype=bool))[None, :, :, None, None]

    def step(S, inp):
        qc, kc, vc, lc = inp
        b = jnp.cumsum(lc, axis=1)
        o_inter = jnp.einsum('bthk,bhkv->bthv', qc * jnp.exp(b), S)
        d = b[:, :, None] - b[:, None]
        decay = jnp.exp(jnp.where(causal_in_chunk, d, -jnp.inf))
        A = jnp.einsum('bthk,bshk,btshk->bhts', qc, kc, decay)
        o = o_inter + jnp.einsum('bhts,bshv->bthv', A, vc)
        b_last = b[:, -1]
        S = jnp.exp(b_last)[..., None] * S + jnp.einsum(
            'bshk,bshv->bhkv', kc * jnp.exp(b_last[:, None] - b), vc)
        return S, o

    S0 = jnp.zeros((B, H, K, V), jnp.float32)
    _, o = lax.scan(step, S0, (to_chunks(q), to_chunks(k), to_chunks(v), to_chunks(log_f)))
    return o.transpose(1, 0, 2, 3, 4).reshape(B, T, H, V)

def hgrn2_bidirectional(q, i, f_pre_fwd, f_pre_bwd, lb_fwd, lb_bwd):
    B, T, _ = q.shape
    qh = q.astype(jnp.float32).reshape(B, T, HG_HEADS, HG_KEY_DIM)
    vh = i.astype(jnp.float32).reshape(B, T, HG_HEADS, HG_VAL_DIM)

    def gates(f_pre, lb):
        f = lb + (1.0 - lb) * jax.nn.sigmoid(f_pre.astype(jnp.float32))
        f = f.reshape(B, T, HG_HEADS, HG_KEY_DIM)
        return 1.0 - f, jnp.log(f)

    kf, lf = gates(f_pre_fwd, lb_fwd)
    kb, lbk = gates(f_pre_bwd, lb_bwd)
    o_fwd = hgrn2_scan(qh, kf, vh, lf)
    flip = lambda a: a[:, ::-1]
    o_bwd = flip(hgrn2_scan(flip(qh), flip(kb), flip(vh), flip(lbk)))
    return o_fwd + o_bwd

def memory_cross_attention(mq, mem_n, w_kv):
    B, T, _ = mq.shape
    M = mem_n.shape[1]
    kv = mem_n @ w_kv
    mk, mv = jnp.split(kv, 2, axis=-1)
    qh = mq.reshape(B, T, MEM_HEADS, MEM_HEAD_DIM)
    mk = mk.reshape(B, M, MEM_HEADS, MEM_HEAD_DIM)
    mv = mv.reshape(B, M, MEM_HEADS, MEM_HEAD_DIM)
    s = jnp.einsum('bthd,bmhd->bhtm', qh, mk) * (MEM_HEAD_DIM ** -0.5)
    p = jax.nn.softmax(s.astype(jnp.float32), axis=-1).astype(mv.dtype)
    return jnp.einsum('bhtm,bmhd->bthd', p, mv).reshape(B, T, MEM_WIDTH)

def peer_ffn(h, w_query, sub_keys, u, v):
    B, T, D = h.shape
    qp = (h @ w_query).reshape(B, T, PEER_HEADS, 2, PEER_QDIM // 2)
    s = jnp.einsum('bthcd,hcnd->bthcn', qp, sub_keys).astype(jnp.float32)
    top_s, top_i = lax.top_k(s, PEER_TOPK)
    cand_s = top_s[..., 0, :, None] + top_s[..., 1, None, :]
    cand_i = top_i[..., 0, :, None] * PEER_NKEYS + top_i[..., 1, None, :]
    cand_s = cand_s.reshape(B, T, PEER_HEADS, PEER_TOPK * PEER_TOPK)
    cand_i = cand_i.reshape(B, T, PEER_HEADS, PEER_TOPK * PEER_TOPK)
    best_s, pos = lax.top_k(cand_s, PEER_TOPK)
    eidx = jnp.take_along_axis(cand_i, pos, axis=-1)
    gate = jax.nn.softmax(best_s, axis=-1)
    nb = (B * T) // PEER_BLOCK
    E = PEER_HEADS * PEER_TOPK
    xb = h.reshape(nb, PEER_BLOCK, D)
    ib = eidx.reshape(nb, PEER_BLOCK, E)
    gb = gate.reshape(nb, PEER_BLOCK, E).astype(h.dtype)

    def block(args):
        xt, it, gt = args
        ue = u[it]
        ve = v[it]
        a = jax.nn.gelu(jnp.einsum('nd,ned->ne', xt, ue), approximate=False)
        return jnp.einsum('ne,ned->nd', a * gt, ve)

    return lax.map(block, (xb, ib, gb)).reshape(B, T, D)

def setup_inputs(seed: int = 0) -> dict:
    key = jax.random.key(seed)
    ks = jax.random.split(key, 16)
    nrm = lambda k, shape, scale: jax.random.normal(k, shape, jnp.float32) * scale
    return {
        'x': nrm(ks[0], (BATCH, SEQ, D_MODEL), 1.0),
        'mem': nrm(ks[1], (BATCH, MEM_TOKENS, D_MODEL), 1.0),
        'attn_norm_g': 1.0 + nrm(ks[2], (DEPTH, D_MODEL), 0.02),
        'w_in': nrm(ks[3], (DEPTH, D_MODEL, IN_WIDTH), D_MODEL ** -0.5),
        'na_rpb': nrm(ks[4], (DEPTH, NA_HEADS, 2 * NA_WIN_ROWS - 1, 2 * NA_WIN_COLS - 1), 0.1),
        'hg_lower_bound': nrm(ks[5], (2, DEPTH + 1, HG_KWIDTH), 0.1),
        'hg_out_norm_g': 1.0 + nrm(ks[6], (DEPTH, HG_WIDTH), 0.02),
        'mem_norm_g': 1.0 + nrm(ks[7], (DEPTH, D_MODEL), 0.02),
        'w_mem_kv': nrm(ks[8], (DEPTH, D_MODEL, 2 * MEM_WIDTH), D_MODEL ** -0.5),
        'w_out': nrm(ks[9], (DEPTH, MIX_WIDTH, D_MODEL), MIX_WIDTH ** -0.5),
        'ffn_norm_g': 1.0 + nrm(ks[10], (DEPTH, D_MODEL), 0.02),
        'peer_w_query': nrm(ks[11], (DEPTH, D_MODEL, PEER_HEADS * PEER_QDIM), D_MODEL ** -0.5),
        'peer_sub_keys': nrm(ks[12], (DEPTH, PEER_HEADS, 2, PEER_NKEYS, PEER_QDIM // 2), (PEER_QDIM // 2) ** -0.5),
        'peer_u': nrm(ks[13], (DEPTH, N_EXPERTS, D_MODEL), D_MODEL ** -0.5),
        'peer_v': nrm(ks[14], (DEPTH, N_EXPERTS, D_MODEL), 0.5),
        'final_norm_g': 1.0 + nrm(ks[15], (D_MODEL,), 0.02),
    }

def reference(x, mem, attn_norm_g, w_in, na_rpb, hg_lower_bound, hg_out_norm_g, mem_norm_g,
              w_mem_kv, w_out, ffn_norm_g, peer_w_query, peer_sub_keys, peer_u, peer_v,
              final_norm_g):
    B, T, _ = x.shape
    lb_table = jnp.cumsum(jax.nn.softmax(hg_lower_bound.astype(jnp.float32), axis=1), axis=1)
    offsets = np.cumsum(IN_SPLITS)[:-1].tolist()
    for layer in range(DEPTH):
        h = rmsnorm(x, attn_norm_g[layer])
        z = h @ w_in[layer]
        na_q, na_k, na_v, hg_q, hg_ff, hg_fb, hg_i, hg_g, mem_q = jnp.split(z, offsets, axis=-1)
        shp = (B, T, NA_HEADS, NA_HEAD_DIM)
        na_out = neighbourhood_attention(na_q.reshape(shp), na_k.reshape(shp), na_v.reshape(shp),
                                         na_rpb[layer])
        o = hgrn2_bidirectional(hg_q, hg_i, hg_ff, hg_fb, lb_table[0, layer], lb_table[1, layer])
        o = _rms_normalize(o) * hg_out_norm_g[layer].astype(jnp.float32).reshape(HG_HEADS, HG_VAL_DIM)
        hg_out = (o.reshape(B, T, HG_WIDTH) * jax.nn.silu(hg_g.astype(jnp.float32))).astype(x.dtype)
        mem_out = memory_cross_attention(mem_q, rmsnorm(mem, mem_norm_g[layer]), w_mem_kv[layer])
        mix = jnp.concatenate([na_out, hg_out, mem_out], axis=-1)
        x = x + mix @ w_out[layer]
        h2 = rmsnorm(x, ffn_norm_g[layer])
        x = x + peer_ffn(h2, peer_w_query[layer], peer_sub_keys[layer], peer_u[layer], peer_v[layer])
    return rmsnorm(x, final_norm_g)


_drawn_inputs = setup_inputs


def setup_inputs(seed=0):
    import zlib

    import numpy as np

    out = dict(_drawn_inputs(seed))
    spreads = {}
    factors = {'hg_out_norm_g': 13.135,
     'mem_norm_g': 5.814,
     'final_norm_g': 8.187,
     'na_rpb': 6.743,
     'ffn_norm_g': 3.519}
    for name, (base, spread) in spreads.items():
        noise = np.random.default_rng([zlib.crc32(name.encode()), seed]).standard_normal(out[name].shape)
        drawn = base * np.exp(spread * noise) if base else spread * noise
        out[name] = __import__('jax').numpy.asarray(drawn.astype(out[name].dtype))
    for name, factor in factors.items():
        out[name] = (out[name] * factor).astype(out[name].dtype)
    return out
```

```python
from contextlib import ExitStack

import numpy as np

import concourse.bass as bass
from concourse import mybir

F32 = mybir.dt.float32
F32R = mybir.dt.float32r
U32 = mybir.dt.uint32
ALU = mybir.AluOpType
ACT = mybir.ActivationFunctionType
AX = mybir.AxisListType

P = 128
T, D, MEM = 512, 1024, 256
NT, KD, MT = T // P, D // P, MEM // P
EPS = 1e-6
GRID_W = 64
ROWS = T // GRID_W
NA_HEADS, MEM_HEADS, HG_HEADS, HD = 8, 4, 4, 64
WIN = 16
SCALE = float(HD) ** -0.5
CT_NAQ, CT_NAK, CT_NAV, CT_HGQ, CT_FF, CT_FB, CT_I, CT_G, CT_MQ = 0, 4, 8, 12, 14, 16, 18, 20, 22
N_CT = 24
LEVELS = 7
HPS = 2
PH, NKEYS, TOPK = 8, 128, 16
NEG = -3.0e38
MASKED = -1.0e30
BANKS = 8
BANK = 512


class Tally:

    def __init__(self, sem):
        self.sem, self.n = sem, 0

    def inc(self, ins):
        ins.then_inc(self.sem, 1)
        self.n += 1
        return self.n


def key_tiles(g):
    return list(range(max(0, g - 1), min(NT, g + 2)))


def mix_jobs():
    jobs = [("hT", k, 0, "act" if k % 2 else "dve") for k in range(KD)]
    jobs += [("mT", k, 0, "act" if k % 2 else "dve") for k in range(KD)]
    jobs += [("e", d, hp, "act") for d in range(2) for hp in range(HPS)]
    jobs += [("q", hp, 0, "act") for hp in range(HPS)]
    jobs += [("i", j, 0, "act") for j in range(2)]
    rest = [("mk", 0, 0, "act"), ("mv", 0, 0, "act")] + [("mq", j, 0, "act") for j in range(2)]
    rest += [("naq", j, 0, "act") for j in range(4)] + [("nak", j, 0, "act") for j in range(4)]
    rest += [("nav", j, 0, "act") for j in range(4)] + [("g", j, 0, "act") for j in range(2)]
    steps = []
    for hp in range(HPS):
        for lv in range(LEVELS + 1):
            steps.append([("lev", lv, 2 * hp + s, "dve") for s in range(2)])
        for s in range(2):
            steps.append([("x", 2 * hp + s, m, "act") for m in range(NT)])
        steps[-1].append(("o", hp, 0, "dve"))
    jobs += rest[:3]
    rest = rest[3:]
    for st in steps:
        jobs += st
        if jobs[-1][0] == "nav" or jobs[-1 - len(st)][0] == "nav":
            jobs.append(("navT", jobs[-1 - len(st)][1], 0, "act"))
        if rest:
            jobs.append(rest.pop(0))
    assert not rest
    jobs += [("ms", hp, 0, "act") for hp in range(HPS)]
    return jobs


def evac_counts(jobs):
    count, out = {"act": 0, "dve": 0}, {}
    for n, job in enumerate(jobs):
        count[job[3]] += 1
        out[n] = (job[3], count[job[3]])
    return out


def weight_order():
    order = []
    for job in mix_jobs():
        kind, a, b, _ = job
        if kind == "e":
            order.append(("z", (CT_FF, CT_FB)[a] + b))
        elif kind == "q":
            order.append(("z", CT_HGQ + a))
        elif kind == "i" and a == 0:
            order += [("z", CT_I), ("z", CT_I + 1)]
        elif kind == "mk":
            order += [("kv", 0), ("kv", 1)]
        elif kind == "mv":
            order += [("kv", 2), ("kv", 3)]
        elif kind == "mq":
            order.append(("z", CT_MQ + a))
        elif kind == "naq":
            order.append(("z", CT_NAQ + a))
        elif kind == "nak":
            order.append(("z", CT_NAK + a))
        elif kind == "nav":
            order.append(("z", CT_NAV + a))
        elif kind == "g":
            order.append(("z", CT_G + a))
    return order


def build_mix(nc, dram, keep, psum, dump=None):
    jobs = mix_jobs()
    at = {job[:3]: n for n, job in enumerate(jobs)}
    emptied = evac_counts(jobs)
    weights = weight_order()
    WSLOTS = 6
    RING = 4
    with ExitStack() as ctx:
        def sb(name, shape, dt=F32):
            return ctx.enter_context(nc.sbuf_tensor(name, shape, dt))

        def sem(name):
            return ctx.enter_context(nc.semaphore(name))

        ident, x_sb, hg_out = keep["ident"], keep["x"], keep["hg_out"]
        naq, nak, nav = keep["naq"], keep["nak"], keep["nav"]
        mq, mk, mv = keep["mq"], keep["mk"], keep["mv"]
        xn = sb("xn", [P, NT, D])
        mem_sb = sb("mem_sb", [P, MT, D])
        hT = sb("hT", [P, KD, T])
        mT = sb("mT", [P, KD, MEM])
        wring = sb("wring", [P, WSLOTS, KD, P])
        gain_a = sb("gain_a", [P, KD])
        gain_m = sb("gain_m", [P, KD])
        gain_o = sb("gain_o", [P, HPS])
        bound = sb("bound", [P, 2, HPS, 2])
        lb = sb("lb", [P, 2, HPS])
        lb1 = sb("lb1", [P, 2, HPS])
        lbt = sb("lbt", [P, 2, HPS])
        nvT = sb("nvT", [P, T])
        masks = sb("masks", [P, LEVELS + 1, P])
        halves = sb("halves", [P, P])
        ss = sb("ss", [P, NT + MT])
        std = sb("std", [P, NT + MT])
        rstd = sb("rstd", [P, NT + MT])
        eps = sb("eps", [P, 1])
        q = sb("hgq", [P, HPS, T])
        kk = sb("hgk", [P, 2, HPS, T])
        ksum = sb("ksum", [P, HPS, T])
        v = sb("hgv", [P, NT, HG_HEADS * HD])
        arr = sb("arr", [P, 2, HPS, NT, P + 1])
        ebt = sb("ebt", [P, 2, HPS, NT])
        inter = sb("inter", [P, HPS, 4, T])
        ext = sb("ext", [P, 6, P])
        dec = sb("dec", [P, 2, 2, T])
        qk = xn[:].rearrange("p r (s t) -> p r s t", s=2)
        lf = inter[:, 0, :, :].rearrange("p (d h) t -> p d h t", d=2)
        m_flat = mT[:].rearrange("p k m -> p (k m)")
        gz = m_flat[:, 0:2 * T].rearrange("p (h t) -> p h t", h=HPS)
        tmp = m_flat[:, 2 * T:4 * T].rearrange("p (h t) -> p h t", h=2)
        Am = sb("Am", [P, 2, NT * (T + P)])
        oT = mem_sb[:, 0, :].rearrange("p (h t) -> p h t", h=HPS)
        osq = mem_sb[:, 1, :].rearrange("p (h t) -> p h t", h=HPS)
        orst = hT[:, 0:2, :]
        sil = hT[:, 2:4, :]
        QF, KF, QB, KB = range(4)

        s_const, s_x, s_mem = sem("const_in"), sem("x_in"), sem("mem_in")
        s_w = [sem(f"w_in{i}") for i in range(WSLOTS)]
        s_sq, s_std, s_rstd, s_xn = sem("sumsq"), sem("std"), sem("rstd"), sem("xn_ready")
        pe_done, act_ev, dve_ev = sem("pe_done"), sem("act_emptied"), sem("dve_emptied")
        s_lb, s_gate, s_lf, s_k, s_scan, s_ksum = (sem("lb"), sem("gate"), sem("logf"), sem("k_ready"),
                                                   sem("scan"), sem("ksum"))
        s_dec, s_exp, s_qk = sem("decay_in"), sem("decay_exp"), sem("qk_ready")
        s_ebt, s_idec, s_iexp, s_inter, s_ext = (sem("ebt"), sem("inter_in"), sem("inter_exp"),
                                                 sem("inter_ready"), sem("ext_ready"))
        s_diag, s_osq, s_orst, s_sil, s_fin = (sem("diag"), sem("osq"), sem("orst"), sem("sil"), sem("hg_fin"))
        ev = {"act": act_ev, "dve": dve_ev}
        block = ctx.enter_context(nc.Block())

        def bank(n):
            return psum[:, n % BANKS, :]

        def await_emptied(eng, key):
            who, count = emptied[at[key]]
            eng.wait_ge(ev[who], count)

        def level_step(hp, lv):
            return hp * LEVELS + lv

        def halves_of(ap, lv):
            h = 64 >> lv
            return ap.rearrange("p n (b s j) -> p n b s j", s=2, j=h)

        def mid_of(d, hp, lv):
            h = 64 >> lv
            m = arr[:, d, hp, :, h:P + 1:2 * h]
            return m.unsqueeze(3).to_broadcast([P, NT, P // (2 * h), h])

        n_wjob = {}
        pos = 0
        for job in jobs:
            need = {"e": 1, "q": 1, "mk": 2, "mv": 2, "mq": 1, "naq": 1, "nak": 1, "nav": 1, "g": 1}.get(job[0], 0)
            if job[0] == "i" and job[1] == 0:
                need = 2
            for j in range(need):
                last = {"i": ("i", 1, 0)}.get(job[0], job[:3])
                n_wjob[pos + j] = at[last]
            pos += need

        @block.sync
        def _(sp):
            for i in range(NT):
                sp.dma_start(x_sb[:, i, :], dram["x"][i * P:(i + 1) * P, :]).then_inc(s_x, 16)
            for i in range(MT):
                sp.dma_start(mem_sb[:, i, :], dram["mem"][i * P:(i + 1) * P, :]).then_inc(s_mem, 16)
            for n, (kind, ct) in enumerate(weights):
                if n >= WSLOTS:
                    sp.wait_ge(pe_done, n_wjob[n - WSLOTS] + 1)
                src = dram["w_in"][ct] if kind == "z" else dram["w_kv"][ct]
                sp.dma_start(wring[:, n % WSLOTS, :, :], src).then_inc(s_w[n % WSLOTS], 16)

        consts = [(ident[:], "ident"), (gain_a[:], "attn_norm_g"), (gain_m[:], "mem_norm_g"),
                  (gain_o[:], "hg_out_norm_g"), (bound[:], "hg_lower_bound"), (masks[:], "level_masks"),
                  (halves[:], "head_mean")]

        @block.scalar
        def _(act):
            for dst, name in consts:
                act.dma_start(dst, dram[name]).then_inc(s_const, 16)
            act.wait_ge(s_x, 16 * NT)
            act.wait_ge(s_mem, 16 * MT)
            for i in range(NT + MT):
                src = x_sb[:, i, :] if i < NT else mem_sb[:, i - NT, :]
                dst = xn[:, i, :] if i < NT else hT[:, 2 * (i - NT):2 * (i - NT) + 2, :].rearrange("p a t -> p (a t)")
                act.activation(dst, src, ACT.Square, accum_out=ss[:, i:i + 1]).then_inc(s_sq, 1)
            act.wait_ge(s_sq, NT + MT)
            act.wait_ge(s_rstd, 1)
            act.activation(std[:], ss[:], ACT.Sqrt, bias=eps[:, 0:1], scale=1.0 / D).then_inc(s_std, 1)
            act.wait_ge(s_const, 16 * len(consts))

            def empty(key):
                n = at[key]
                act.wait_ge(pe_done, n + 1)
                src = bank(n)
                kind, a, b = key
                if kind == "hT":
                    return act.activation(hT[:, a, :], src, ACT.Identity, scale=gain_a[:, a:a + 1])
                if kind == "mT":
                    return act.activation(mT[:, a, :], src[:, 0:MEM], ACT.Identity, scale=gain_m[:, a:a + 1])
                if kind == "e":
                    return act.activation(kk[:, a, b, :], src, ACT.Exp, scale=-1.0)
                if kind == "q":
                    return act.copy(q[:, a, :], src)
                if kind == "i":
                    return act.copy(v[:, 2 * a:2 * a + 2, :], src.rearrange("p (n c) -> p n c", n=2))
                if kind == "mk":
                    return act.copy(mk[:], src.rearrange("p (n c) -> p n c", n=2))
                if kind == "mv":
                    return act.copy(mv[:], src.rearrange("p (n c) -> p n c", n=2))
                if kind == "mq":
                    return act.copy(mq[:, a, :], src)
                if kind in ("naq", "nak", "nav"):
                    if kind == "nav" and a:
                        act.wait_ge(pe_done, at[("navT", a - 1, 0)] + 1)
                    dst = {"naq": naq[:, a, :], "nak": nak[:, a, :], "nav": nvT[:]}[kind]
                    return act.copy(dst.rearrange("p (c r) -> p r c", r=ROWS),
                                    src.rearrange("p (r c) -> p r c", r=ROWS))
                if kind == "navT":
                    return act.copy(nav[:, :, a * P:(a + 1) * P], src.rearrange("p (n c) -> p n c", n=NT))
                if kind == "g":
                    return act.copy(gz[:, a, :], src)
                if kind == "x":
                    m = b
                    row = Am[:, a % 2, m * T:(m + 1) * T]
                    if a >= 2:
                        await_emptied(act, ("o", 0, 0))
                    if 0 < m < NT - 1:
                        act.copy(row[:, 0:m * P], src[:, 0:m * P])
                    if m < NT - 1:
                        return act.copy(row[:, (m + 1) * P:], src[:, (m + 1) * P:])
                    return act.copy(row[:, 0:m * P], src[:, 0:m * P])
                if kind == "ms":
                    return act.activation(orst[:, a, :], src, ACT.Sqrt, bias=eps[:, 0:1])

            def log_f():
                act.wait_ge(s_gate, 6)
                act.activation(lf, kk[:], ACT.Ln).then_inc(s_lf, 1)

            def level_exps(hp, lv):
                s = level_step(hp, lv)
                act.wait_ge(s_dec, 4 * (s + 1))
                act.activation(dec[:, s % 2, :, :], dec[:, s % 2, :, :], ACT.Exp).then_inc(s_exp, 1)

            def inter_exps(hp):
                act.wait_ge(s_idec, 2 * (hp + 1))
                if hp == 0:
                    act.activation(ebt[:], arr[:, :, :, :, P], ACT.Exp).then_inc(s_ebt, 1)
                act.activation(inter[:, hp, 1:3, :], inter[:, hp, 1:3, :], ACT.Exp).then_inc(s_iexp, 1)
                act.activation(inter[:, hp, QF, :].rearrange("p (n t) -> p n t", n=NT),
                               arr[:, 0, hp, :, 1:P + 1], ACT.Exp).then_inc(s_iexp, 1)
                act.activation(inter[:, hp, KB, :].rearrange("p (n t) -> p n t", n=NT),
                               arr[:, 1, hp, :, 0:P], ACT.Exp).then_inc(s_iexp, 1)

            act.wait_ge(s_lb, 1)
            act.activation(lbt[:], lbt[:], ACT.Exp).then_inc(s_std, 1)

            for job in jobs:
                if job[3] == "act":
                    empty(job[:3]).then_inc(act_ev, 1)
                if job[:3] == ("i", 1, 0):
                    log_f()
                    level_exps(0, 0)
                if job[0] == "lev" and job[2] % 2 == 1:
                    hp, lv = job[2] // 2, job[1]
                    if lv + 1 < LEVELS:
                        level_exps(hp, lv + 1)
                    elif lv + 1 == LEVELS:
                        inter_exps(hp)
                if job[0] == "x" and job[1] == 1 and job[2] == NT - 1:
                    level_exps(1, 0)
                if job[:3] == ("g", 1, 0):
                    await_emptied(act, ("g", 1, 0))
                    act.activation(sil, gz, ACT.Exp, scale=-1.0).then_inc(s_sil, 1)

        @block.gpsimd
        def _(pool):
            pool.memset(arr[:, :, :, :, 0:1], 0.0).then_inc(s_scan, 1)

            def level_products(hp, lv):
                s = level_step(hp, lv)
                pool.wait_ge(s_exp, s + 1)
                if s >= RING:
                    pool.wait_ge(pe_done, at[("lev", (s - RING) % LEVELS, 2 * ((s - RING) // LEVELS) + 1)] + 1)
                pool.tensor_tensor(qk[:, s % RING, 0, :], q[:, hp, :], dec[:, s % 2, 0, :], ALU.mult).then_inc(s_qk, 1)
                for side in range(2):
                    pick = lambda ap: halves_of(ap.rearrange("p (n t) -> p n t", n=NT), lv)[:, :, :, side, :]
                    pool.tensor_tensor(pick(qk[:, s % RING, 1, :]), pick(kk[:, side, hp, :]),
                                       pick(dec[:, s % 2, 1, :]), ALU.mult).then_inc(s_qk, 1)

            def inter_products(hp):
                pool.wait_ge(s_iexp, 3 * (hp + 1))
                for kind, src in ((QF, q[:, hp, :]), (KF, kk[:, 0, hp, :]), (QB, q[:, hp, :]), (KB, kk[:, 1, hp, :])):
                    pool.tensor_tensor(inter[:, hp, kind, :], inter[:, hp, kind, :], src, ALU.mult).then_inc(s_inter, 1)
                pool.wait_ge(s_inter, 4 * (hp + 1))
                pool.wait_ge(s_ebt, 1)
                if hp:
                    pool.wait_ge(pe_done, at[("x", 1, NT - 1)] + 1)
                qf = inter[:, hp, QF, :].rearrange("p (n t) -> p n t", n=NT)
                qb = inter[:, hp, QB, :].rearrange("p (n t) -> p n t", n=NT)
                pool.tensor_scalar(ext[:, 0, :], qf[:, 2, :], ebt[:, 0, hp, 1:2], None, ALU.mult).then_inc(s_ext, 1)
                pool.tensor_scalar(ext[:, 1, :], qf[:, 3, :], ebt[:, 0, hp, 2:3], None, ALU.mult).then_inc(s_ext, 1)
                pool.tensor_scalar(ext[:, 3, :], qb[:, 0, :], ebt[:, 1, hp, 1:2], None, ALU.mult).then_inc(s_ext, 1)
                pool.tensor_scalar(ext[:, 4, :], qb[:, 1, :], ebt[:, 1, hp, 2:3], None, ALU.mult).then_inc(s_ext, 1)
                pool.wait_ge(s_ext, 6 * hp + 4)
                pool.tensor_scalar(ext[:, 2, :], ext[:, 1, :], ebt[:, 0, hp, 1:2], None, ALU.mult).then_inc(s_ext, 1)
                pool.tensor_scalar(ext[:, 5, :], ext[:, 3, :], ebt[:, 1, hp, 2:3], None, ALU.mult).then_inc(s_ext, 1)

            pool.wait_ge(s_k, 1)
            await_emptied(pool, ("q", 1, 0))
            for hp in range(HPS):
                for lv in range(LEVELS):
                    level_products(hp, lv)
                inter_products(hp)

        @block.vector
        def _(dve):
            dve.memset(eps[:], EPS).then_inc(s_rstd, 1)
            dve.wait_ge(s_std, 1)
            dve.reciprocal(rstd[:], std[:]).then_inc(s_rstd, 1)
            dve.wait_ge(s_rstd, 2)
            for i in range(NT + MT):
                if i < NT:
                    dve.tensor_scalar(xn[:, i, :], x_sb[:, i, :], rstd[:, i:i + 1], None, ALU.mult).then_inc(s_xn, 1)
                else:
                    m = mem_sb[:, i - NT, :]
                    dve.tensor_scalar(m, m, rstd[:, i:i + 1], None, ALU.mult).then_inc(s_xn, 1)
            dve.wait_ge(s_const, 16 * len(consts))
            dve.tensor_tensor(lbt[:], bound[:, :, :, 1], bound[:, :, :, 0], ALU.subtract).then_inc(s_lb, 1)
            dve.wait_ge(s_std, 2)
            dve.tensor_scalar(lb1[:], lbt[:], 1.0, None, ALU.add).then_inc(s_lb, 1)
            dve.wait_ge(s_lb, 2)
            dve.reciprocal(lb[:], lb1[:]).then_inc(s_lb, 1)
            dve.wait_ge(s_lb, 3)
            dve.tensor_scalar(lb1[:], lb[:], -1.0, 1.0, ALU.mult, ALU.add).then_inc(s_lb, 1)

            diag_n = Tally(s_diag)

            def diag(h):
                return Am[:, h % 2, :].rearrange("p (n t) -> p n t", n=NT)[:, :, 0:P]

            def empty(key):
                n = at[key]
                dve.wait_ge(pe_done, n + 1)
                src = bank(n)
                kind, a, b = key
                if kind == "hT":
                    dve.tensor_scalar(hT[:, a, :], src, gain_a[:, a:a + 1], None, ALU.mult).then_inc(dve_ev, 1)
                if kind == "mT":
                    dve.tensor_scalar(mT[:, a, :], src[:, 0:MEM], gain_m[:, a:a + 1], None, ALU.mult).then_inc(dve_ev, 1)
                if kind == "lev":
                    lv, h = a, b
                    mask = masks[:, lv, :].unsqueeze(1).to_broadcast([P, NT, P])
                    s4 = src.rearrange("p (n t) -> p n t", n=NT)
                    if lv == 0:
                        if h >= 2:
                            dve.wait_ge(pe_done, at[("o", 0, 0)] + 1)
                        dve.tensor_tensor(diag(h), s4, mask, ALU.mult).then_inc(dve_ev, 1)
                    else:
                        t4 = tmp[:, h % 2, :].rearrange("p (n t) -> p n t", n=NT)
                        if diag_n.n >= 2:
                            dve.wait_ge(s_diag, diag_n.n - 1)
                        dve.tensor_tensor(t4, s4, mask, ALU.mult).then_inc(dve_ev, 1)
                        dve.wait_ge(dve_ev, emptied[n][1])
                        if diag_n.n >= 2:
                            dve.wait_ge(s_diag, diag_n.n - 1)
                        diag_n.inc(dve.tensor_tensor(diag(h), diag(h), t4, ALU.add))
                if kind == "o":
                    dve.tensor_copy(oT[:, a, :], src).then_inc(dve_ev, 1)
                    dve.wait_ge(dve_ev, emptied[n][1])
                    dve.tensor_tensor(osq[:, a, :], oT[:, a, :], oT[:, a, :], ALU.mult).then_inc(s_osq, 1)

            def decays(hp, lv):
                s = level_step(hp, lv)
                if s >= 2:
                    dve.wait_ge(s_qk, 3 * (s - 1))
                X = [arr[:, d, hp, :, 1 - d:P + 1 - d] for d in range(2)]
                dq = halves_of(dec[:, s % 2, 0, :].rearrange("p (n t) -> p n t", n=NT), lv)
                dk = halves_of(dec[:, s % 2, 1, :].rearrange("p (n t) -> p n t", n=NT), lv)
                xf, xb = halves_of(X[0], lv), halves_of(X[1], lv)
                mf, mb = mid_of(0, hp, lv), mid_of(1, hp, lv)
                for dst, a, b in ((dq[:, :, :, 1, :], xf[:, :, :, 1, :], mf), (dq[:, :, :, 0, :], mb, xb[:, :, :, 0, :]),
                                  (dk[:, :, :, 0, :], mf, xf[:, :, :, 0, :]), (dk[:, :, :, 1, :], xb[:, :, :, 1, :], mb)):
                    dve.tensor_tensor(dst, a, b, ALU.subtract).then_inc(s_dec, 1)

            def inter_decays(hp):
                for kind, d in ((KF, 0), (QB, 1)):
                    tot = arr[:, d, hp, :, P:P + 1].to_broadcast([P, NT, P])
                    dve.tensor_tensor(inter[:, hp, kind, :].rearrange("p (n t) -> p n t", n=NT), tot,
                                      arr[:, d, hp, :, 1 - d:P + 1 - d], ALU.subtract).then_inc(s_idec, 1)

            for job in jobs:
                if job[3] == "dve":
                    empty(job[:3])
                if job[:3] == ("i", 1, 0):
                    await_emptied(dve, ("e", 1, 1))
                    dve.tensor_scalar(kk[:], kk[:], 1.0, None, ALU.add).then_inc(s_gate, 1)
                    dve.wait_ge(s_gate, 1)
                    dve.reciprocal(kk[:], kk[:]).then_inc(s_gate, 1)
                    dve.wait_ge(s_gate, 2)
                    dve.wait_ge(s_lb, 4)
                    for d in range(2):
                        for hp in range(HPS):
                            dve.tensor_scalar(kk[:, d, hp, :], kk[:, d, hp, :], lb1[:, d, hp:hp + 1], lb[:, d, hp:hp + 1],
                                              ALU.mult, ALU.add).then_inc(s_gate, 1)
                    dve.wait_ge(s_gate, 6)
                    dve.wait_ge(s_lf, 1)
                    dve.tensor_scalar(kk[:], kk[:], -1.0, 1.0, ALU.mult, ALU.add).then_inc(s_k, 1)
                    dve.wait_ge(s_scan, 1)
                    for d in range(2):
                        for hp in range(HPS):
                            for n in range(NT):
                                seg = lf[:, d, hp, n * P:(n + 1) * P]
                                dve.tensor_tensor_scan(arr[:, d, hp, n, 1:P + 1], seg, seg, 0.0,
                                                       ALU.add, ALU.bypass).then_inc(s_scan, 1)
                    dve.wait_ge(s_k, 1)
                    dve.tensor_tensor(ksum[:], kk[:, 0, :, :], kk[:, 1, :, :], ALU.add).then_inc(s_ksum, 1)
                    dve.wait_ge(s_scan, 1 + 4 * NT)
                    decays(0, 0)
                if job[0] == "lev" and job[2] % 2 == 0:
                    hp, lv = job[2] // 2, job[1]
                    if lv + 1 < LEVELS:
                        decays(hp, lv + 1)
                    elif lv + 1 == LEVELS:
                        inter_decays(hp)
                        if hp == 0:
                            decays(1, 0)

            def tail_wait(n):
                dve.wait_ge(s_fin, n)
            dve.wait_ge(s_sil, 1)
            dve.tensor_scalar(sil, sil, 1.0, None, ALU.add).then_inc(s_fin, 1)
            tail_wait(1)
            dve.reciprocal(sil, sil).then_inc(s_fin, 1)
            tail_wait(2)
            dve.tensor_tensor(sil, sil, gz, ALU.mult).then_inc(s_fin, 1)
            await_emptied(dve, ("ms", 1, 0))
            dve.reciprocal(orst, orst).then_inc(s_fin, 1)
            tail_wait(4)
            dve.tensor_tensor(oT, oT, orst, ALU.mult).then_inc(s_fin, 1)
            tail_wait(5)
            for hp in range(HPS):
                dve.scalar_tensor_tensor(hg_out[:, hp, :], oT[:, hp, :], gain_o[:, hp:hp + 1], sil[:, hp, :],
                                         ALU.mult, ALU.mult).then_inc(s_fin, 1)

        @block.tensor
        def _(pe):
            wpos = [0]

            def weight_slots(k):
                slots = []
                for _ in range(k):
                    n = wpos[0]
                    pe.wait_ge(s_w[n % WSLOTS], 16 * (n // WSLOTS + 1))
                    slots.append(n % WSLOTS)
                    wpos[0] += 1
                return slots

            def project(out, slot, src, cols):
                for k in range(KD):
                    last = pe.matmul(out, wring[:, slot, k, :], src[:, k, cols], start=(k == 0), stop=(k == KD - 1))
                return last

            def project_natural(out, src, first, count):
                for k in range(KD):
                    last = pe.matmul(out, src(k), wring[:, first:first + count, k, :], start=(k == 0), stop=(k == KD - 1))
                return last

            def run(n, key):
                kind, a, b = key
                out = bank(n)
                if kind == "hT":
                    for i in range(NT):
                        last = pe.transpose(out[:, i * P:(i + 1) * P], xn[:, i, a * P:(a + 1) * P], ident[:])
                elif kind == "mT":
                    for i in range(MT):
                        last = pe.transpose(out[:, i * P:(i + 1) * P], mem_sb[:, i, a * P:(a + 1) * P], ident[:])
                elif kind in ("e", "q", "mq", "naq", "nak", "nav", "g"):
                    last = project(out, weight_slots(1)[0], hT, slice(0, T))
                elif kind == "mk":
                    for j, slot in enumerate(weight_slots(2)):
                        last = project(out[:, j * MEM:(j + 1) * MEM], slot, mT, slice(0, MEM))
                elif kind == "mv":
                    slots = weight_slots(2)
                    for m in range(MT):
                        for j, slot in enumerate(slots):
                            last = project_natural(out[:, m * MEM + j * P:m * MEM + (j + 1) * P],
                                                   lambda k: mT[:, k, m * P:(m + 1) * P], slot, 1)
                elif kind == "i":
                    if a == 0:
                        i_slots.extend(weight_slots(2))
                    for t in range(2):
                        for j, slot in enumerate(i_slots):
                            tok = 2 * a + t
                            last = project_natural(out[:, t * MEM + j * P:t * MEM + (j + 1) * P],
                                                   lambda k: hT[:, k, tok * P:(tok + 1) * P], slot, 1)
                elif kind == "navT":
                    await_emptied(pe, ("nav", a, 0))
                    for t in range(NT):
                        last = pe.transpose(out[:, t * P:(t + 1) * P], nvT[:, t * P:(t + 1) * P], ident[:])
                elif kind == "lev":
                    lv, h = a, b
                    hp, r = h // 2, slice(HD * (h % 2), HD * (h % 2) + HD)
                    if lv < LEVELS:
                        s = level_step(hp, lv)
                        pe.wait_ge(s_qk, 3 * (s + 1))
                        kt, qt = qk[r, s % RING, 1, :], qk[r, s % RING, 0, :]
                    else:
                        pe.wait_ge(s_ksum, 1)
                        kt, qt = ksum[r, hp, :], q[r, hp, :]
                    for t in range(NT):
                        c = slice(t * P, (t + 1) * P)
                        last = pe.matmul(out[:, c], kt[:, c], qt[:, c], start=True, stop=True)
                elif kind == "x":
                    h, m = a, b
                    hp, r = h // 2, slice(HD * (h % 2), HD * (h % 2) + HD)
                    if m == 0:
                        pe.wait_ge(s_ext, 6 * (hp + 1))
                    for t in range(NT):
                        if t == m:
                            continue
                        far = abs(t - m)
                        kt = inter[r, hp, KF if t > m else KB, m * P:(m + 1) * P]
                        if far == 1:
                            qt = inter[r, hp, QF if t > m else QB, t * P:(t + 1) * P]
                        elif far == 2:
                            qt = ext[r, (t - 2) if t > m else (3 + t), :]
                        else:
                            qt = ext[r, 2 if t > m else 5, :]
                        last = pe.matmul(out[:, t * P:(t + 1) * P], kt, qt, start=True, stop=True)
                elif kind == "o":
                    hp = a
                    await_emptied(pe, ("x", 2 * hp + 1, NT - 1))
                    pe.wait_ge(s_diag, 2 * LEVELS * (hp + 1))
                    for s in range(2):
                        h = 2 * hp + s
                        for m in range(NT):
                            last = pe.matmul(out[s * HD:(s + 1) * HD, :], v[:, m, h * HD:(h + 1) * HD],
                                             Am[:, s, m * T:(m + 1) * T], start=(m == 0), stop=(m == NT - 1))
                elif kind == "ms":
                    pe.wait_ge(s_osq, a + 1)
                    last = pe.matmul(out, halves[:], osq[:, a, :], start=True, stop=True)
                return last

            i_slots = []
            pe.wait_ge(s_const, 16 * len(consts))
            pe.wait_ge(s_xn, NT + MT)
            first_z = at[("e", 0, 0)]
            for n, job in enumerate(jobs):
                if n >= BANKS:
                    who, count = emptied[n - BANKS]
                    pe.wait_ge(ev[who], count)
                if n == first_z:
                    await_emptied(pe, ("hT", KD - 1, 0))
                    await_emptied(pe, ("hT", KD - 2, 0))
                if job[:3] == ("mk", 0, 0):
                    await_emptied(pe, ("mT", KD - 1, 0))
                    await_emptied(pe, ("mT", KD - 2, 0))
                run(n, job[:3]).then_inc(pe_done, 1)


def build_attention(nc, dram, keep, psum):
    PAIRS_NA, PAIRS = NA_HEADS // 2, (NA_HEADS + MEM_HEADS) // 2
    UNITS = PAIRS * 2 * NT
    NA_UNITS = PAIRS_NA * 2 * NT
    S_SLOTS, T_SLOTS, T_LAG, V_LAG = 4, 3, 3, 4
    MAXK = 3 * P
    with ExitStack() as ctx:
        def sb(name, shape, dt=F32):
            return ctx.enter_context(nc.sbuf_tensor(name, shape, dt))

        def sem(name):
            return ctx.enter_context(nc.semaphore(name))

        ident, x_sb, hg_out, h2T = keep["ident"], keep["x"], keep["hg_out"], keep["h2T"]
        naq, nak, nav = keep["naq"], keep["nak"], keep["nav"]
        mq, mk, mv = keep["mq"], keep["mk"], keep["mv"]
        mixT = sb("mixT", [P, PAIRS, T])
        bias = sb("bias", [P, NA_HEADS, MAXK])
        wmask = sb("wmask", [P, NT, MAXK])
        bm = sb("bias_masked", [P, 2, NT, MAXK])
        prob = sb("prob", [P, S_SLOTS, MAXK])
        probT = sb("probT", [P, T_SLOTS, MAXK])
        nmax = sb("nmax", [P, UNITS])
        total = sb("total", [P, UNITS])
        inv = sb("inv", [P, UNITS])
        w_out = sb("w_out", [P, KD, D])
        h2 = sb("h2", [P, NT, D])
        ss = sb("ss2", [P, NT])
        std = sb("std2", [P, NT])
        rstd = sb("rstd2", [P, NT])
        eps = sb("eps2", [P, 1])
        gain = sb("gain_f", [P, KD])

        s_in, s_wo = sem("bias_in"), sem("wout_in")
        s_score, s_scaled, s_max, s_exp, s_inv, s_prob = (sem("score"), sem("scaled"), sem("nmax_ready"),
                                                          sem("exp_done"), sem("inv_ready"), sem("prob_ready"))
        s_turned, s_probT, s_pv, s_out, s_bm = (sem("turned"), sem("probT_ready"), sem("pv"), sem("mix_ready"),
                                                sem("bm_ready"))
        s_proj, s_x2, s_sq, s_std, s_rstd, s_h2 = (sem("proj"), sem("x2"), sem("sumsq2"), sem("std2_r"),
                                                   sem("rstd2_r"), sem("h2_ready"))
        s_hT, s_ha, s_hd = sem("h2T_pe"), sem("h2T_act"), sem("h2T_dve")
        block = ctx.enter_context(nc.Block())

        def unit(u):
            pair, side, g = u // (2 * NT), (u // NT) % 2, u % NT
            return pair, side, g, (key_tiles(g) if pair < PAIRS_NA else [0, 1])

        def width(u):
            return P * len(unit(u)[3])

        def rows(side):
            return slice(side * HD, side * HD + HD)

        @block.sync
        def _(sp):
            sp.dma_start(wmask[:], dram["window_masks"]).then_inc(s_in, 16)
            for cq in range(WIN):
                sp.dma_start(bias[cq * ROWS:(cq + 1) * ROWS, :, :],
                             dram["na_rpb"][:, :, (WIN - 1 - cq) * ROWS:(WIN - 1 - cq) * ROWS + MAXK]).then_inc(s_in, 16)
            sp.dma_start(gain[:], dram["ffn_norm_g"]).then_inc(s_in, 16)
            sp.dma_start(w_out[:], dram["w_out"].rearrange("(k p) n -> p k n", p=P)).then_inc(s_wo, 16)

        IN_ALL = 16 * (WIN + 2)

        @block.gpsimd
        def _(pool):
            pool.wait_ge(s_in, IN_ALL)

            def masked_bias(h):
                if h >= 2:
                    pool.wait_ge(s_scaled, NT * (h - 1))
                pool.tensor_tensor(bm[:, h % 2, :, :], wmask[:],
                                   bias[:, h, :].unsqueeze(1).to_broadcast([P, NT, MAXK]), ALU.add).then_inc(s_bm, 1)

            masked_bias(0)
            masked_bias(1)
            for u in range(UNITS):
                w = width(u)
                pool.wait_ge(s_inv, u + 1)
                pool.tensor_scalar(prob[:, u % S_SLOTS, 0:w], prob[:, u % S_SLOTS, 0:w], inv[:, u:u + 1], None,
                                   ALU.mult).then_inc(s_prob, 1)
                if u < NA_UNITS and u % NT == NT - 1 and u // NT + 2 < NA_HEADS:
                    masked_bias(u // NT + 2)

        @block.scalar
        def _(act):
            def exps(u):
                w = width(u)
                act.wait_ge(s_max, u + 1)
                act.activation(prob[:, u % S_SLOTS, 0:w], prob[:, u % S_SLOTS, 0:w], ACT.Exp, bias=nmax[:, u:u + 1],
                               accum_out=total[:, u:u + 1]).then_inc(s_exp, 1)

            def move_probT(u):
                w = width(u)
                act.wait_ge(s_turned, u + 1)
                if u >= T_SLOTS:
                    act.wait_ge(s_pv, u - T_SLOTS + 1)
                act.copy(probT[:, u % T_SLOTS, 0:w], psum[:, 3 + u % 3, 0:w]).then_inc(s_probT, 1)

            for u in range(UNITS + T_LAG):
                if u < UNITS:
                    exps(u)
                if u >= T_LAG:
                    move_probT(u - T_LAG)
            act.wait_ge(s_in, IN_ALL)
            for i in range(NT):
                act.wait_ge(s_x2, 2 * (i + 1) + 1)
                act.activation(h2[:, i, :], x_sb[:, i, :], ACT.Square, accum_out=ss[:, i:i + 1]).then_inc(s_sq, 1)
            act.wait_ge(s_sq, NT)
            act.activation(std[:], ss[:], ACT.Sqrt, bias=eps[:, 0:1], scale=1.0 / D).then_inc(s_std, 1)
            for k in range(0, KD, 2):
                act.wait_ge(s_hT, k + 1)
                act.activation(h2T[:, k, :], psum[:, k, :], ACT.Identity, scale=gain[:, k:k + 1]).then_inc(s_ha, 1)

        @block.vector
        def _(dve):
            dve.memset(eps[:], EPS).then_inc(s_x2, 1)

            def scaled_max(u):
                pair, side, g, keys = unit(u)
                w = width(u)
                dve.wait_ge(s_score, u + 1)
                if u >= S_SLOTS:
                    dve.wait_ge(s_turned, u - S_SLOTS + 1)
                dst = prob[:, u % S_SLOTS, 0:w]
                if pair < PAIRS_NA:
                    h = 2 * pair + side
                    dve.wait_ge(s_bm, h + 1)
                    off = (keys[0] - g + 1) * P
                    dve.scalar_tensor_tensor(dst, psum[:, u % 3, 0:w], SCALE, bm[:, h % 2, g, off:off + w],
                                             ALU.mult, ALU.add).then_inc(s_scaled, 1)
                else:
                    dve.tensor_scalar(dst, psum[:, u % 3, 0:w], SCALE, None, ALU.mult).then_inc(s_scaled, 1)
                dve.wait_ge(s_scaled, u + 1)
                dve.tensor_reduce(nmax[:, u:u + 1], dst, AX.X, ALU.max, negate=True).then_inc(s_max, 1)

            def invert(u):
                dve.wait_ge(s_exp, u + 1)
                dve.reciprocal(inv[:, u:u + 1], total[:, u:u + 1]).then_inc(s_inv, 1)

            def move_out(pair):
                dve.wait_ge(s_pv, 2 * NT * (pair + 1))
                src = psum[:, 6 + pair % 2, :]
                if pair < PAIRS_NA:
                    dve.tensor_copy(mixT[:, pair, :].rearrange("p (r c) -> p r c", r=ROWS),
                                    src.rearrange("p (c r) -> p r c", r=ROWS)).then_inc(s_out, 1)
                else:
                    dve.tensor_copy(mixT[:, pair, :], src).then_inc(s_out, 1)

            for u in range(UNITS + V_LAG + 1):
                if u < UNITS:
                    scaled_max(u)
                if 1 <= u <= UNITS:
                    invert(u - 1)
                done = u - V_LAG
                if done >= 1 and done % (2 * NT) == 0:
                    move_out(done // (2 * NT) - 1)
            for n in range(2 * NT):
                i, half = n // 2, slice((n % 2) * BANK, (n % 2) * BANK + BANK)
                dve.wait_ge(s_proj, n + 1)
                dve.tensor_tensor(x_sb[:, i, half], psum[:, n, :], x_sb[:, i, half], ALU.add).then_inc(s_x2, 1)
            dve.wait_ge(s_std, 1)
            dve.reciprocal(rstd[:], std[:]).then_inc(s_rstd, 1)
            dve.wait_ge(s_rstd, 1)
            for i in range(NT):
                dve.tensor_scalar(h2[:, i, :], x_sb[:, i, :], rstd[:, i:i + 1], None, ALU.mult).then_inc(s_h2, 1)
            for k in range(1, KD, 2):
                dve.wait_ge(s_hT, k + 1)
                dve.tensor_scalar(h2T[:, k, :], psum[:, k, :], gain[:, k:k + 1], None, ALU.mult).then_inc(s_hd, 1)

        @block.tensor
        def _(pe):
            def scores(u):
                pair, side, g, keys = unit(u)
                w, r = width(u), rows(side)
                if u >= 3:
                    pe.wait_ge(s_scaled, u - 2)
                if pair < PAIRS_NA:
                    q, k = naq[r, pair, g * P:(g + 1) * P], nak[r, pair, keys[0] * P:keys[0] * P + w]
                else:
                    q, k = mq[r, pair - PAIRS_NA, g * P:(g + 1) * P], mk[r, pair - PAIRS_NA, :]
                pe.matmul(psum[:, u % 3, 0:w], q, k, start=True, stop=True).then_inc(s_score, 1)

            def turn(u):
                pe.wait_ge(s_prob, u + 1)
                if u >= 3:
                    pe.wait_ge(s_probT, u - 2)
                for j in range(len(unit(u)[3])):
                    last = pe.transpose(psum[:, 3 + u % 3, j * P:(j + 1) * P], prob[:, u % S_SLOTS, j * P:(j + 1) * P], ident[:])
                last.then_inc(s_turned, 1)

            def values(u):
                pair, side, g, keys = unit(u)
                pe.wait_ge(s_probT, u + 1)
                if u % (2 * NT) == 0 and pair >= 2:
                    pe.wait_ge(s_out, pair - 1)
                for j, kt in enumerate(keys):
                    if pair < PAIRS_NA:
                        h = 2 * pair + side
                        v = nav[:, kt, h * HD:(h + 1) * HD]
                    else:
                        h = 2 * (pair - PAIRS_NA) + side
                        v = mv[:, kt, h * HD:(h + 1) * HD]
                    last = pe.matmul(psum[rows(side), 6 + pair % 2, g * P:(g + 1) * P], v, probT[:, u % T_SLOTS, j * P:(j + 1) * P],
                                     start=(j == 0), stop=(j == len(keys) - 1))
                last.then_inc(s_pv, 1)

            for u in range(UNITS + V_LAG):
                if u < UNITS:
                    scores(u)
                if T_LAG <= u < UNITS + T_LAG:
                    turn(u - T_LAG)
                if u >= V_LAG:
                    values(u - V_LAG)
            pe.wait_ge(s_wo, 16)
            pe.wait_ge(s_out, PAIRS)
            pe.wait_ge(s_probT, UNITS)
            for n in range(2 * NT):
                i, half = n // 2, slice((n % 2) * BANK, (n % 2) * BANK + BANK)
                for k in range(KD):
                    src = hg_out[:, k - 4, :] if k in (4, 5) else mixT[:, k if k < 4 else k - 2, :]
                    last = pe.matmul(psum[:, n, :], src[:, i * P:(i + 1) * P], w_out[:, k, half],
                                     start=(k == 0), stop=(k == KD - 1))
                last.then_inc(s_proj, 1)
            pe.wait_ge(s_h2, NT)
            for k in range(KD):
                for i in range(NT):
                    last = pe.transpose(psum[:, k, i * P:(i + 1) * P], h2[:, i, k * P:(k + 1) * P], ident[:])
                last.then_inc(s_hT, 1)


def build_routing(nc, dram, keep, psum):
    HC = 2 * PH
    WSLOTS = 6
    with ExitStack() as ctx:
        def sb(name, shape, dt=F32):
            return ctx.enter_context(nc.sbuf_tensor(name, shape, dt))

        def sem(name):
            return ctx.enter_context(nc.semaphore(name))

        ident, h2T, chosen = keep["ident"], keep["h2T"], keep["chosen"]
        h2hi, h2lo = keep["h2hi"], keep["h2lo"]
        s_hi, s_lo = sem("h2hi_ready"), sem("h2lo_ready")
        wring = sb("wqring", [P, WSLOTS, KD, P])
        keysT = sb("keysT", [P, HC, NKEYS])
        iota = sb("iota3", [P, P])
        query = sb("query", [P, 2, T])
        scores = sb("scores", [P, HC, NT, NKEYS])
        top = sb("top", [P, HC, NT, TOPK])
        top_i = sb("top_i", [P, HC, NT, TOPK], U32)
        top_f = sb("top_f", [P, HC, NT, TOPK])
        sums = sb("sums", [P, 2, NT, TOPK * TOPK])
        best = sb("best", [P, PH, NT, TOPK])
        place = sb("place", [P, PH, NT, TOPK], U32)
        place_ab = sb("place_ab", [P, 2, 2, NT, TOPK], U32)
        ab = sb("ab", [P, 2, 2, NT, TOPK])
        pick = sb("pick", [P, 2, 2, NT, TOPK * TOPK])
        found = sb("found", [P, 3, NT, PH, TOPK])
        gsum = sb("gsum", [P, PH, NT])
        ginv = sb("ginv", [P, PH, NT])

        s_in = sem("keys_in")
        s_w = [sem(f"wq_in{i}") for i in range(WSLOTS)]
        s_q, s_qsb, s_s, s_ssb = sem("query_pe"), sem("query_sb"), sem("scores_pe"), sem("scores_sb")
        s_top, s_ab, s_eq, s_pick, s_red, s_cast = (sem("top_steps"), sem("ab_ready"), sem("eq_ready"),
                                                    sem("pick_ready"), sem("picked"), sem("top_cast"))
        s_gin, s_gexp, s_g, s_turn, s_out = (sem("gate_in"), sem("gate_exp"), sem("gate_steps"), sem("chosen_pe"),
                                             sem("chosen_sb"))
        block = ctx.enter_context(nc.Block())

        @block.sync
        def _(sp):
            for n in range(HC):
                if n >= WSLOTS:
                    sp.wait_ge(s_q, n - WSLOTS + 1)
                sp.dma_start(wring[:, n % WSLOTS, :, :], dram["w_query"][n]).then_inc(s_w[n % WSLOTS], 16)

        @block.scalar
        def _(act):
            act.dma_start(keysT[:], dram["sub_keys"]).then_inc(s_in, 16)
            act.dma_start(iota[:], dram["iota"]).then_inc(s_in, 16)
            for n in range(HC + 1):
                if n < HC:
                    act.wait_ge(s_q, n + 1)
                    if n >= 2:
                        act.wait_ge(s_s, n - 1)
                    act.copy(query[:, n % 2, :], psum[:, n % 2, :]).then_inc(s_qsb, 1)
                if n:
                    act.wait_ge(s_s, n)
                    act.copy(scores[:, n - 1, :, :], psum[:, 2 + (n - 1) % 2, :].rearrange("p (t k) -> p t k", t=NT)).then_inc(s_ssb, 1)
            act.copy(h2hi[:], h2T[:]).then_inc(s_hi, 1)
            act.wait_ge(s_gin, 1)
            act.activation(best[:], best[:], ACT.Exp).then_inc(s_gexp, 1)
            for j in range(3):
                act.wait_ge(s_turn, j + 1)
                act.copy(chosen[:, j, :], psum[:, 4 + j, :]).then_inc(s_out, 1)

        @block.gpsimd
        def _(pool):
            for h in range(PH):
                for c in range(2):
                    dst = pick[:, h % 2, c, :, :].rearrange("p n (s a) -> p n s a", a=TOPK)
                    pool.wait_ge(s_eq, 2 * h + c + 1)
                    pool.tensor_tensor(dst, dst, top_f[:, 2 * h + c, :, :].unsqueeze(2).to_broadcast([P, NT, TOPK, TOPK]),
                                       ALU.mult).then_inc(s_pick, 1)

        @block.vector
        def _(dve):
            steps = Tally(s_top)
            small = iota[:, 0:TOPK].unsqueeze(1).unsqueeze(1).to_broadcast([P, NT, TOPK, TOPK])
            dve.wait_ge(s_in, 32)

            def top16(data, values, places):
                n = len(data)
                lo, hi = slice(0, 8), slice(8, 16)
                back = lambda: dve.wait_ge(s_top, steps.n - n + 1)
                for i in range(n):
                    steps.inc(dve.max(values(i)[:, lo], data[i]))
                for i in range(n):
                    back()
                    steps.inc(dve.max_index(places(i)[:, lo], values(i)[:, lo], data[i]))
                for i in range(n):
                    back()
                    steps.inc(dve.match_replace(data[i], values(i)[:, lo], data[i], NEG))
                for i in range(n):
                    back()
                    steps.inc(dve.max(values(i)[:, hi], data[i]))
                for i in range(n):
                    back()
                    steps.inc(dve.max_index(places(i)[:, hi], values(i)[:, hi], data[i]))

            def reduce_picks(h):
                dve.wait_ge(s_pick, 2 * (h + 1))
                for c in range(2):
                    dve.tensor_reduce(found[:, c, :, h, :], pick[:, h % 2, c, :, :].rearrange("p n (s a) -> p n s a", a=TOPK),
                                      AX.X, ALU.add).then_inc(s_red, 1)

            for n in range(HC):
                h = n // 2
                dve.wait_ge(s_ssb, n + 1)
                top16([scores[:, n, t, :] for t in range(NT)], lambda t: top[:, n, t, :], lambda t: top_i[:, n, t, :])
                dve.wait_ge(s_top, steps.n)
                dve.tensor_copy(top_f[:, n, :, :], top_i[:, n, :, :]).then_inc(s_cast, 1)
                if n % 2:
                    s4 = sums[:, h % 2, :, :].rearrange("p n (a b) -> p n a b", b=TOPK)
                    steps.inc(dve.tensor_tensor(s4, top[:, n - 1, :, :].unsqueeze(3).to_broadcast([P, NT, TOPK, TOPK]),
                                                top[:, n, :, :].unsqueeze(2).to_broadcast([P, NT, TOPK, TOPK]), ALU.add))
                    dve.wait_ge(s_top, steps.n)
                    top16([sums[:, h % 2, t, :] for t in range(NT)], lambda t: best[:, h, t, :], lambda t: place[:, h, t, :])
                    dve.wait_ge(s_top, steps.n)
                    if h >= 2:
                        dve.wait_ge(s_eq, 2 * (h - 1))
                    steps.inc(dve.tensor_scalar(place_ab[:, h % 2, 0, :, :], place[:, h, :, :], 4, None, ALU.logical_shift_right))
                    steps.inc(dve.tensor_scalar(place_ab[:, h % 2, 1, :, :], place[:, h, :, :], 15, None, ALU.bitwise_and))
                    dve.wait_ge(s_top, steps.n)
                    dve.wait_ge(s_cast, n + 1)
                    dve.tensor_copy(ab[:, h % 2, :, :, :], place_ab[:, h % 2, :, :, :]).then_inc(s_ab, 1)
                    dve.wait_ge(s_ab, h + 1)
                    if h >= 2:
                        dve.wait_ge(s_red, 2 * (h - 1))
                    for c in range(2):
                        dst = pick[:, h % 2, c, :, :].rearrange("p n (s a) -> p n s a", a=TOPK)
                        src = ab[:, h % 2, c, :, :].unsqueeze(3).to_broadcast([P, NT, TOPK, TOPK])
                        dve.tensor_tensor(dst, src, small, ALU.is_equal).then_inc(s_eq, 1)
                    if h:
                        reduce_picks(h - 1)
            dve.wait_ge(s_hi, 1)
            dve.tensor_tensor(h2lo[:], h2T[:], h2hi[:].bitcast(F32), ALU.subtract).then_inc(s_lo, 1)
            steps.inc(dve.tensor_copy(gsum[:], best[:, :, :, 0]))
            dve.wait_ge(s_top, steps.n)
            dve.tensor_tensor(best[:], best[:], gsum[:].unsqueeze(3).to_broadcast([P, PH, NT, TOPK]), ALU.subtract).then_inc(s_gin, 1)
            reduce_picks(PH - 1)
            dve.wait_ge(s_gexp, 1)
            dve.tensor_reduce(gsum[:], best[:], AX.X, ALU.add).then_inc(s_g, 1)
            dve.wait_ge(s_g, 1)
            dve.reciprocal(ginv[:], gsum[:]).then_inc(s_g, 1)
            dve.wait_ge(s_g, 2)
            dve.tensor_tensor(found[:, 2, :, :, :].rearrange("p n h s -> p h n s"), best[:],
                              ginv[:].unsqueeze(3).to_broadcast([P, PH, NT, TOPK]), ALU.mult).then_inc(s_g, 1)

        @block.tensor
        def _(pe):
            for n in range(HC + 1):
                if n < HC:
                    pe.wait_ge(s_w[n % WSLOTS], 16 * (n // WSLOTS + 1))
                    if n >= 2:
                        pe.wait_ge(s_qsb, n - 1)
                    for k in range(KD):
                        last = pe.matmul(psum[:, n % 2, :], wring[:, n % WSLOTS, k, :], h2T[:, k, :],
                                         start=(k == 0), stop=(k == KD - 1))
                    last.then_inc(s_q, 1)
                if n:
                    m = n - 1
                    pe.wait_ge(s_in, 32)
                    pe.wait_ge(s_qsb, n)
                    if m >= 2:
                        pe.wait_ge(s_ssb, m - 1)
                    for t in range(NT):
                        last = pe.matmul(psum[:, 2 + m % 2, t * P:(t + 1) * P], query[:, m % 2, t * P:(t + 1) * P],
                                         keysT[:, m, :], start=True, stop=True)
                    last.then_inc(s_s, 1)
            pe.wait_ge(s_red, 2 * PH)
            for j in range(3):
                if j == 2:
                    pe.wait_ge(s_g, 3)
                for t in range(NT):
                    last = pe.transpose(psum[:, 4 + j, t * P:(t + 1) * P], found[:, j, t, :, :].rearrange("p h s -> p (h s)"), ident[:])
                last.then_inc(s_turn, 1)


def build_gates(nc, dram, keep, psum):
    QUADS = 4
    STEP = 4 * QUADS
    CHUNK = 128
    CHUNKS, ITERS = T // CHUNK, T // STEP
    PER = CHUNK // STEP
    with ExitStack() as ctx:
        def sb(name, shape, dt=F32):
            return ctx.enter_context(nc.sbuf_tensor(name, shape, dt))

        def sem(name):
            return ctx.enter_context(nc.semaphore(name))

        chosen, gates = keep["chosen"], keep["gates"]
        iota = sb("iota4", [P, P])
        hot_j = sb("hot_j", [P, QUADS, 4, P])
        hot_i = sb("hot_i", [P, QUADS, 4, P])
        chunk = sb("chunk", [P, 2, P, CHUNK])
        s_in, s_hot, s_prod, s_moved = sem("iota_in"), sem("hot_ready"), sem("gate_prod"), sem("gate_moved")
        s_st = [sem("gates_out0"), sem("gates_out1")]
        block = ctx.enter_context(nc.Block())

        @block.sync
        def _(sp):
            sp.dma_start(iota[:], dram["iota"]).then_inc(s_in, 16)
            for c in range(CHUNKS):
                sp.wait_ge(s_moved, QUADS * PER * (c + 1))
                sp.dma_start(gates[:, :, c * CHUNK:(c + 1) * CHUNK].rearrange("i j t -> j i t"),
                             chunk[:, c % 2, :, :]).then_inc(s_st[c % 2], 16)
            for c in range(2):
                sp.wait_ge(s_st[c], 16 * (CHUNKS // 2))

        @block.vector
        def _(dve):
            def one_hots(it, first):
                for q in range(QUADS):
                    if not first:
                        dve.wait_ge(s_prod, (it - 1) * QUADS + q + 1)
                    for s in range(4):
                        t = it * STEP + q * 4 + s
                        dve.tensor_scalar(hot_j[:, q, s, :], iota[:], chosen[:, 1, bass.ds(t, 1)], None, ALU.is_equal)
                        last = dve.tensor_scalar(hot_i[:, q, s, :], iota[:], chosen[:, 0, bass.ds(t, 1)],
                                                 chosen[:, 2, bass.ds(t, 1)], ALU.is_equal, ALU.mult)
                    last.then_inc(s_hot, 1)

            dve.wait_ge(s_in, 16)
            one_hots(0, True)
            with dve.Fori(1, ITERS) as it:
                one_hots(it, False)

        @block.tensor
        def _(pe):
            def products(it, first):
                for q in range(QUADS):
                    pe.wait_ge(s_hot, it * QUADS + q + 1)
                    if not first:
                        pe.wait_ge(s_moved, (it - 1) * QUADS + q + 1)
                    for s in range(4):
                        last = pe.matmul(psum[:, q, s * P:(s + 1) * P], hot_j[:, q, s, :], hot_i[:, q, s, :],
                                         start=True, stop=True)
                    last.then_inc(s_prod, 1)

            products(0, True)
            with pe.Fori(1, ITERS) as it:
                products(it, False)

        @block.scalar
        def _(act):
            for c in range(CHUNKS):
                if c >= 2:
                    act.wait_ge(s_st[c % 2], 16 * (c // 2))
                with act.Fori(0, PER) as it:
                    for q in range(QUADS):
                        act.wait_ge(s_prod, c * PER * QUADS + it * QUADS + q + 1)
                        act.copy(chunk[:, c % 2, :, bass.ds(it * STEP + q * 4, 4)],
                                 psum[:, q, :].rearrange("p (s i) -> p i s", s=4)).then_inc(s_moved, 1)


def build_experts(nc, dram, keep, psum):
    TILES, E = NKEYS, 4
    GROUPS = TILES // E
    UR, VR, GR, SR = 4, 2, 4, 4
    with ExitStack() as ctx:
        def sb(name, shape, dt=F32):
            return ctx.enter_context(nc.sbuf_tensor(name, shape, dt))

        def sem(name):
            return ctx.enter_context(nc.semaphore(name))

        x_sb, h2hi, h2lo, gates = keep["x"], keep["h2hi"], keep["h2lo"], keep["gates"]
        u_raw = sb("u_raw", [P, UR, KD, P])
        v_raw = sb("v_raw", [P, VR, D])
        g_sb = sb("g_sb", [P, GR, T])
        u_hi = sb("u_hi", [P, 2, KD, P], F32R)
        u_lo = sb("u_lo", [P, 2, KD, P], F32R)
        v_hi = sb("v_hi", [P, 2 * E, D], F32R)
        v_lo = sb("v_lo", [P, 2 * E, D], F32R)
        gel = sb("gel", [P, 2, T])
        wgt = sb("wgt", [P, 2, T])
        w_hi = sb("w_hi", [P, 2 * E, T], F32R)
        w_lo = sb("w_lo", [P, 2 * E, T], F32R)
        fgain = v_raw[:, 0, :]
        ss = sb("ss4", [P, NT])
        std = sb("std4", [P, NT])
        rstd = sb("rstd4", [P, NT])
        eps = sb("eps4", [P, 1])

        s_u = [sem(f"u_in{i}") for i in range(UR)]
        s_v = [sem(f"v_in{i}") for i in range(VR)]
        s_g = [sem(f"g_in{i}") for i in range(GR)]
        s_uhi, s_ulo, s_vhi, s_vlo = sem("u_hi_r"), sem("u_lo_r"), sem("v_hi_r"), sem("v_lo_r")
        s_act, s_gel, s_wgt, s_whi, s_wlo = sem("act_pe"), sem("gel_r"), sem("wgt_r"), sem("w_hi_r"), sem("w_lo_r")
        s_outp, s_acc = sem("out_pe"), sem("acc_r")
        s_fg, s_sq, s_std, s_rstd, s_fin, s_store = (sem("fgain_in"), sem("sumsq4"), sem("std4_r"), sem("rstd4_r"),
                                                     sem("final_r"), sem("stored"))
        block = ctx.enter_context(nc.Block())

        def wait(eng, s, value):
            if not (isinstance(value, int) and value <= 0):
                eng.wait_ge(s, value)

        def over_pairs(eng, body):
            body(0, True, False)
            with eng.Fori(1, GROUPS // 2 - 1) as it:
                body(it * 2, False, False)
            body(GROUPS - 2, False, True)

        @block.sync
        def _(sp):
            def loads(g, first, last):
                for e in range(2 * E):
                    n = g * E + e
                    tile = bass.ds(n, 1) if not isinstance(n, int) else slice(n, n + 1)
                    if not (first and e < UR):
                        sp.wait_ge(s_ulo, n - UR + 1)
                    sp.dma_start(u_raw[:, e % UR, :, :], dram["peer_u"][tile, :, :, :].rearrange("a p k j -> p (a k) j")).then_inc(s_u[e % UR], 16)
                    if not (first and e < VR):
                        sp.wait_ge(s_vlo, n - VR + 1)
                    sp.dma_start(v_raw[:, e % VR, :], dram["peer_v"][tile, :, :].rearrange("a j d -> j (a d)")).then_inc(s_v[e % VR], 16)
                    if not (first and e < GR):
                        sp.wait_ge(s_wgt, n - GR + 1)
                    sp.dma_start(g_sb[:, e % GR, :], gates[tile, :, :].rearrange("a j t -> j (a t)")).then_inc(s_g[e % GR], 16)

            over_pairs(sp, loads)
            sp.wait_ge(s_vlo, TILES)
            sp.dma_start(fgain, dram["final_norm_g"].to_broadcast([P, D])).then_inc(s_fg, 16)
            for i in range(NT):
                sp.wait_ge(s_fin, 2 * i + 2)
                sp.dma_start(dram["out"][i * P:(i + 1) * P, :], x_sb[:, i, :]).then_inc(s_store, 16)
            sp.wait_ge(s_store, 16 * NT)

        def arrived(eng, sems, g, e, slots):
            eng.wait_ge(sems[e % slots], (g * (E // slots) + e // slots + 1) * 16)

        @block.scalar
        def _(act):
            def split_u(g, e, first):
                arrived(act, s_u, g, e, UR)
                if not (first and e < 2):
                    act.wait_ge(s_act, g * E + e - 1)
                act.copy(u_hi[:, e % 2, :, :], u_raw[:, e % UR, :, :]).then_inc(s_uhi, 1)

            def body(g, first, last):
                for e in range(2 * E):
                    n = g * E + e
                    if not (last and e == 2 * E - 1):
                        if e < 2 * E - 1:
                            split_u(g, e + 1, first)
                        else:
                            split_u(g + 2, 0, False)
                    act.wait_ge(s_act, n + 1)
                    if not (first and e < 2):
                        act.wait_ge(s_wgt, n - 1)
                    act.activation(gel[:, e % 2, :], psum[:, e % SR, :], ACT.Gelu).then_inc(s_gel, 1)
                    act.wait_ge(s_wgt, n + 1)
                    if not first:
                        act.wait_ge(s_outp, (g + e // E - 1) * 8)
                    act.copy(w_hi[:, e, :], wgt[:, e % 2, :]).then_inc(s_whi, 1)
                    arrived(act, s_v, g, e, VR)
                    act.copy(v_hi[:, e, :], v_raw[:, e % VR, :]).then_inc(s_vhi, 1)

            split_u(0, 0, True)
            over_pairs(act, body)
            for i in range(NT):
                act.wait_ge(s_acc, GROUPS * 8 - (8 - 2 * (i + 1)))
                act.activation(gel[:].rearrange("p a t -> p (a t)"), x_sb[:, i, :], ACT.Square, accum_out=ss[:, i:i + 1]).then_inc(s_sq, 1)
                act.wait_ge(s_sq, i + 1)
                if i == 0:
                    act.wait_ge(s_rstd, 1)
                act.activation(std[:, i:i + 1], ss[:, i:i + 1], ACT.Sqrt, bias=eps[:, 0:1], scale=1.0 / D).then_inc(s_std, 1)

        @block.vector
        def _(dve):
            dve.memset(eps[:], EPS).then_inc(s_rstd, 1)

            def rest_u(g, e):
                dve.wait_ge(s_uhi, g * E + e + 1)
                dve.tensor_tensor(u_lo[:, e % 2, :, :], u_raw[:, e % UR, :, :], u_hi[:, e % 2, :, :].bitcast(F32),
                                  ALU.subtract).then_inc(s_ulo, 1)

            def accumulate(g):
                for m in range(8):
                    dve.wait_ge(s_outp, g * 8 + m + 1)
                    dst = x_sb[:, m // 2, (m % 2) * BANK:(m % 2 + 1) * BANK]
                    dve.tensor_tensor(dst, psum[:, SR + m % 4, :], dst, ALU.add).then_inc(s_acc, 1)

            def body(g, first, last):
                for e in range(2 * E):
                    n = g * E + e
                    if not (last and e == 2 * E - 1):
                        if e < 2 * E - 1:
                            rest_u(g, e + 1)
                        else:
                            rest_u(g + 2, 0)
                    dve.wait_ge(s_gel, n + 1)
                    arrived(dve, s_g, g, e, GR)
                    if not (first and e < 2):
                        dve.wait_ge(s_wlo, n - 1)
                    dve.tensor_tensor(wgt[:, e % 2, :], gel[:, e % 2, :], g_sb[:, e % GR, :], ALU.mult).then_inc(s_wgt, 1)
                    dve.wait_ge(s_whi, n + 1)
                    dve.tensor_tensor(w_lo[:, e, :], wgt[:, e % 2, :], w_hi[:, e, :].bitcast(F32), ALU.subtract).then_inc(s_wlo, 1)
                    dve.wait_ge(s_vhi, n + 1)
                    dve.tensor_tensor(v_lo[:, e, :], v_raw[:, e % VR, :], v_hi[:, e, :].bitcast(F32), ALU.subtract).then_inc(s_vlo, 1)
                    if e % E == E - 1 and not (first and e < E):
                        accumulate(g + e // E - 1)

            rest_u(0, 0)
            over_pairs(dve, body)
            accumulate(GROUPS - 1)
            dve.wait_ge(s_fg, 16)
            for i in range(NT):
                dve.wait_ge(s_std, i + 1)
                dve.reciprocal(rstd[:, i:i + 1], std[:, i:i + 1]).then_inc(s_rstd, 1)
                dve.wait_ge(s_rstd, i + 2)
                dve.wait_ge(s_acc, GROUPS * 8)
                for half in range(2):
                    c = slice(half * BANK, (half + 1) * BANK)
                    dve.scalar_tensor_tensor(x_sb[:, i, c], x_sb[:, i, c], rstd[:, i:i + 1], fgain[:, c],
                                             ALU.mult, ALU.mult).then_inc(s_fin, 1)

        @block.tensor
        def _(pe):
            def activations(g, e, first):
                n = g * E + e
                pe.wait_ge(s_ulo, n + 1)
                if not (first and e < SR):
                    pe.wait_ge(s_gel, n - SR + 1)
                for k in range(KD):
                    for a, b in ((u_hi, h2hi), (u_hi, h2lo), (u_lo, h2hi)):
                        last = pe.matmul(psum[:, e % SR, :], a[:, e % 2, k, :], b[:, k, :],
                                         start=(k == 0 and a is u_hi and b is h2hi), stop=(k == KD - 1 and a is u_lo))
                last.then_inc(s_act, 1)

            def outputs(g, half, first):
                pe.wait_ge(s_wlo, (g + 1) * E)
                pe.wait_ge(s_vlo, (g + 1) * E)
                for m in range(8):
                    t, c = slice((m // 2) * P, (m // 2 + 1) * P), slice((m % 2) * BANK, (m % 2 + 1) * BANK)
                    if not (first and m < 4):
                        pe.wait_ge(s_acc, g * 8 + m - 3)
                    for e in range(half * E, half * E + E):
                        for a, b in ((w_hi, v_hi), (w_hi, v_lo), (w_lo, v_hi)):
                            last = pe.matmul(psum[:, SR + m % 4, :], a[:, e, t], b[:, e, c],
                                             start=(e == half * E and a is w_hi and b is v_hi),
                                             stop=(e == half * E + E - 1 and a is w_lo))
                    last.then_inc(s_outp, 1)

            def body(g, first, last):
                for half in range(2):
                    for e in range(E):
                        activations(g, half * E + e, first)
                    if not (first and half == 0):
                        outputs(g + half - 1, 1 - half, first and half == 1)

            over_pairs(pe, body)
            outputs(GROUPS - 1, 1, False)


def _level_masks():
    s, t = np.arange(P)[:, None], np.arange(P)[None, :]
    out = np.zeros((P, LEVELS + 1, P), np.float32)
    for lv in range(LEVELS):
        h = 64 >> lv
        out[:, lv] = (s // (2 * h) == t // (2 * h)) & (s // h != t // h)
    out[:, LEVELS] = s == t
    return out


def _window_masks():
    out = np.full((P, NT, 3, P), MASKED, np.float32)
    q = np.arange(P)
    for g in range(NT):
        cq = g * WIN + q // ROWS
        c0 = np.clip(cq - WIN // 2, 0, GRID_W - WIN)
        for j in range(3):
            ck = (g - 1 + j) * WIN + np.arange(P) // ROWS
            inside = (ck[None, :] >= c0[:, None]) & (ck[None, :] < c0[:, None] + WIN)
            out[:, g, j][inside] = 0.0
    return out


def _pairwise_rpb(rpb):
    pad = np.pad(rpb, ((0, 0), (0, 0), (WIN, WIN))).transpose(0, 2, 1)
    return np.stack([pad[:, :, ROWS - 1 - r:2 * ROWS - 1 - r] for r in range(ROWS)]).reshape(ROWS, NA_HEADS, -1)


def _tiles(w):
    return w.reshape(KD, P, -1, P).transpose(2, 1, 0, 3)


def _columns(g):
    return g.reshape(-1, P).T


def build(nc, dram):
    gates = nc.dram_tensor("gates", [NKEYS, NKEYS, T], F32).ap()
    with ExitStack() as ctx:
        def sb(where, name, shape, dt=F32, side=None):
            return where.enter_context(nc.sbuf_tensor(name, shape, dt, side=side))

        psum = ctx.enter_context(nc.psum_tensor("psum", [P, BANKS, BANK], F32))
        keep = {"gates": gates, "ident": sb(ctx, "ident", [P, P]), "x": sb(ctx, "x_sb", [P, NT, D])}
        with ExitStack() as late:
            with ExitStack() as mixing:
                keep["hg_out"] = sb(mixing, "hg_out", [P, HPS, T])
                keep["naq"] = sb(mixing, "naq", [P, 4, T])
                keep["nak"] = sb(mixing, "nak", [P, 4, T])
                keep["nav"] = sb(mixing, "nav", [P, NT, NA_HEADS * HD])
                keep["mq"] = sb(mixing, "mq", [P, 2, T])
                keep["mk"] = sb(mixing, "mk", [P, 2, MEM])
                keep["mv"] = sb(mixing, "mv", [P, MT, MEM_HEADS * HD])
                build_mix(nc, dram, keep, psum)
                keep["h2T"] = sb(late, "h2T", [P, KD, T], side="right")
                build_attention(nc, dram, keep, psum)
            keep["h2hi"] = sb(ctx, "h2hi", [P, KD, T], F32R)
            keep["h2lo"] = sb(ctx, "h2lo", [P, KD, T], F32R)
            routed = ctx.enter_context(ExitStack())
            keep["chosen"] = sb(routed, "chosen", [P, 3, T])
            build_routing(nc, dram, keep, psum)
        build_gates(nc, dram, keep, psum)
        routed.close()
        build_experts(nc, dram, keep, psum)


def kernel(x, mem, attn_norm_g, w_in, na_rpb, hg_lower_bound, hg_out_norm_g, mem_norm_g, w_mem_kv, w_out,
           ffn_norm_g, peer_w_query, peer_sub_keys, peer_u, peer_v, final_norm_g):
    import concourse.bacc as bacc
    from concourse.bass_utils import run_bass_kernel_spmd

    head_mean = np.zeros((P, P), np.float32)
    for s in range(2):
        head_mean[s * HD:(s + 1) * HD, s * HD:(s + 1) * HD] = 1.0 / HD
    a = np.asarray
    arrays = {
        "x": a(x)[0], "mem": a(mem)[0],
        "w_in": _tiles(a(w_in)[0]), "w_kv": _tiles(a(w_mem_kv)[0]), "w_query": _tiles(a(peer_w_query)[0]),
        "attn_norm_g": _columns(a(attn_norm_g)[0]), "mem_norm_g": _columns(a(mem_norm_g)[0]),
        "ffn_norm_g": _columns(a(ffn_norm_g)[0]), "hg_out_norm_g": _columns(a(hg_out_norm_g)[0]),
        "hg_lower_bound": a(hg_lower_bound).reshape(2, 2, HPS, P).transpose(3, 0, 2, 1),
        "na_rpb": _pairwise_rpb(a(na_rpb)[0]), "w_out": a(w_out)[0],
        "sub_keys": a(peer_sub_keys)[0].reshape(2 * PH, NKEYS, P).transpose(2, 0, 1),
        "peer_u": a(peer_u)[0].reshape(NKEYS, NKEYS, KD, P).transpose(0, 3, 2, 1),
        "peer_v": a(peer_v)[0].reshape(NKEYS, NKEYS, D), "final_norm_g": a(final_norm_g).reshape(1, D),
        "ident": np.eye(P, dtype=np.float32), "head_mean": head_mean, "level_masks": _level_masks(),
        "window_masks": _window_masks().reshape(P, NT, 3 * P),
        "iota": np.broadcast_to(np.arange(P, dtype=np.float32), (P, P)),
    }
    arrays = {f"in_{k}": np.ascontiguousarray(v) for k, v in arrays.items()}
    nc = bacc.Bacc("TRN2", target_bir_lowering=False, num_devices=1)
    dram = {k[3:]: nc.dram_tensor(k, v.shape, F32, kind="ExternalInput").ap() for k, v in arrays.items()}
    dram["out"] = nc.dram_tensor("out", (T, D), F32, kind="ExternalOutput").ap()
    build(nc, dram)
    r = run_bass_kernel_spmd(nc, [arrays], core_ids=[0])
    return r.results[0]["out"].reshape(1, T, D)
```

```python
from contextlib import ExitStack

import numpy as np

import concourse.bass as bass
from concourse import mybir

F32 = mybir.dt.float32
F32R = mybir.dt.float32r
U32 = mybir.dt.uint32
ALU = mybir.AluOpType
ACT = mybir.ActivationFunctionType
AX = mybir.AxisListType

P = 128
T, D, MEM = 512, 1024, 256
NT, KD, MT = T // P, D // P, MEM // P
EPS = 1e-6
GRID_W = 64
ROWS = T // GRID_W
NA_HEADS, MEM_HEADS, HG_HEADS, HD = 8, 4, 4, 64
WIN = 16
SCALE = float(HD) ** -0.5
CT_NAQ, CT_NAK, CT_NAV, CT_HGQ, CT_FF, CT_FB, CT_I, CT_G, CT_MQ = 0, 4, 8, 12, 14, 16, 18, 20, 22
N_CT = 24
LEVELS = 7
HPS = 2
PH, NKEYS, TOPK = 8, 128, 16
NEG = -3.0e38
MASKED = -1.0e30
BANKS = 8
BANK = 512
EARLY_ROUTING, EARLY_GATES = 24, 16
EARLY = EARLY_ROUTING + EARLY_GATES
GROUP = 4
USLOTS = 4
CHUNK = 64
CHOSEN_BANKS = (4, 5, 0)
PICK_LAG = 6


class Tally:

    def __init__(self, sem):
        self.sem, self.n = sem, 0

    def inc(self, ins):
        ins.then_inc(self.sem, 1)
        self.n += 1
        return self.n


def key_tiles(g):
    return list(range(max(0, g - 1), min(NT, g + 2)))


def mix_jobs():
    jobs = [("hT", k, 0, "act" if k % 2 else "dve") for k in range(KD)]
    jobs += [("mT", k, 0, "act" if k % 2 else "dve") for k in range(KD)]
    jobs += [("e", d, hp, "act") for d in range(2) for hp in range(HPS)]
    jobs += [("q", hp, 0, "act") for hp in range(HPS)]
    jobs += [("i", j, 0, "act") for j in range(2)]
    rest = [("mk", 0, 0, "act"), ("mv", 0, 0, "act")] + [("mq", j, 0, "act") for j in range(2)]
    rest += [("naq", j, 0, "act") for j in range(4)] + [("nak", j, 0, "act") for j in range(4)]
    rest += [("nav", j, 0, "act") for j in range(4)] + [("g", j, 0, "act") for j in range(2)]
    steps = []
    for hp in range(HPS):
        for lv in range(LEVELS + 1):
            steps.append([("lev", lv, 2 * hp + s, "dve") for s in range(2)])
        for s in range(2):
            steps.append([("x", 2 * hp + s, m, "act") for m in range(NT)])
        steps[-1].append(("o", hp, 0, "dve"))
    jobs += rest[:3]
    rest = rest[3:]
    for st in steps:
        jobs += st
        if jobs[-1][0] == "nav" or jobs[-1 - len(st)][0] == "nav":
            jobs.append(("navT", jobs[-1 - len(st)][1], 0, "act"))
        if rest:
            jobs.append(rest.pop(0))
    assert not rest
    jobs += [("ms", hp, 0, "act") for hp in range(HPS)]
    return jobs


def evac_counts(jobs):
    count, out = {"act": 0, "dve": 0}, {}
    for n, job in enumerate(jobs):
        count[job[3]] += 1
        out[n] = (job[3], count[job[3]])
    return out


def weight_order():
    order = []
    for job in mix_jobs():
        kind, a, b, _ = job
        if kind == "e":
            order.append(("z", (CT_FF, CT_FB)[a] + b))
        elif kind == "q":
            order.append(("z", CT_HGQ + a))
        elif kind == "i" and a == 0:
            order += [("z", CT_I), ("z", CT_I + 1)]
        elif kind == "mk":
            order += [("kv", 0), ("kv", 1)]
        elif kind == "mv":
            order += [("kv", 2), ("kv", 3)]
        elif kind == "mq":
            order.append(("z", CT_MQ + a))
        elif kind == "naq":
            order.append(("z", CT_NAQ + a))
        elif kind == "nak":
            order.append(("z", CT_NAK + a))
        elif kind == "nav":
            order.append(("z", CT_NAV + a))
        elif kind == "g":
            order.append(("z", CT_G + a))
    return order


def build_mix(nc, dram, keep, psum, dump=None):
    jobs = mix_jobs()
    at = {job[:3]: n for n, job in enumerate(jobs)}
    emptied = evac_counts(jobs)
    weights = weight_order()
    WSLOTS = 6
    RING = 4
    with ExitStack() as ctx:
        def sb(name, shape, dt=F32):
            return ctx.enter_context(nc.sbuf_tensor(name, shape, dt))

        def sem(name):
            return ctx.enter_context(nc.semaphore(name))

        ident, x_sb, hg_out = keep["ident"], keep["x"], keep["hg_out"]
        naq, nak, nav = keep["naq"], keep["nak"], keep["nav"]
        mq, mk, mv = keep["mq"], keep["mk"], keep["mv"]
        xn = sb("xn", [P, NT, D])
        mem_sb = sb("mem_sb", [P, MT, D])
        hT = sb("hT", [P, KD, T])
        mT = sb("mT", [P, KD, MEM])
        wring = sb("wring", [P, WSLOTS, KD, P])
        gain_a = sb("gain_a", [P, KD])
        gain_m = sb("gain_m", [P, KD])
        gain_o = sb("gain_o", [P, HPS])
        bound = sb("bound", [P, 2, HPS, 2])
        lb = sb("lb", [P, 2, HPS])
        lb1 = sb("lb1", [P, 2, HPS])
        lbt = sb("lbt", [P, 2, HPS])
        nvT = sb("nvT", [P, T])
        masks = sb("masks", [P, LEVELS + 1, P])
        halves = sb("halves", [P, P])
        ss = sb("ss", [P, NT + MT])
        std = sb("std", [P, NT + MT])
        rstd = sb("rstd", [P, NT + MT])
        eps = sb("eps", [P, 1])
        q = sb("hgq", [P, HPS, T])
        kk = sb("hgk", [P, 2, HPS, T])
        ksum = sb("ksum", [P, HPS, T])
        v = sb("hgv", [P, NT, HG_HEADS * HD])
        arr = sb("arr", [P, 2, HPS, NT, P + 1])
        ebt = sb("ebt", [P, 2, HPS, NT])
        inter = sb("inter", [P, HPS, 4, T])
        ext = sb("ext", [P, 6, P])
        dec = sb("dec", [P, 2, 2, T])
        qk = xn[:].rearrange("p r (s t) -> p r s t", s=2)
        lf = inter[:, 0, :, :].rearrange("p (d h) t -> p d h t", d=2)
        m_flat = mT[:].rearrange("p k m -> p (k m)")
        gz = m_flat[:, 0:2 * T].rearrange("p (h t) -> p h t", h=HPS)
        tmp = m_flat[:, 2 * T:4 * T].rearrange("p (h t) -> p h t", h=2)
        Am = sb("Am", [P, 2, NT * (T + P)])
        oT = mem_sb[:, 0, :].rearrange("p (h t) -> p h t", h=HPS)
        osq = mem_sb[:, 1, :].rearrange("p (h t) -> p h t", h=HPS)
        orst = hT[:, 0:2, :]
        sil = hT[:, 2:4, :]
        QF, KF, QB, KB = range(4)

        s_const, s_x, s_mem = sem("const_in"), sem("x_in"), sem("mem_in")
        s_w = [sem(f"w_in{i}") for i in range(WSLOTS)]
        s_sq, s_std, s_rstd, s_xn = sem("sumsq"), sem("std"), sem("rstd"), sem("xn_ready")
        pe_done, act_ev, dve_ev = sem("pe_done"), sem("act_emptied"), sem("dve_emptied")
        s_lb, s_gate, s_lf, s_k, s_scan, s_ksum = (sem("lb"), sem("gate"), sem("logf"), sem("k_ready"),
                                                   sem("scan"), sem("ksum"))
        s_dec, s_exp, s_qk = sem("decay_in"), sem("decay_exp"), sem("qk_ready")
        s_ebt, s_idec, s_iexp, s_inter, s_ext = (sem("ebt"), sem("inter_in"), sem("inter_exp"),
                                                 sem("inter_ready"), sem("ext_ready"))
        s_diag, s_osq, s_orst, s_sil, s_fin = (sem("diag"), sem("osq"), sem("orst"), sem("sil"), sem("hg_fin"))
        ev = {"act": act_ev, "dve": dve_ev}
        block = ctx.enter_context(nc.Block())

        def bank(n):
            return psum[:, n % BANKS, :]

        def await_emptied(eng, key):
            who, count = emptied[at[key]]
            eng.wait_ge(ev[who], count)

        def level_step(hp, lv):
            return hp * LEVELS + lv

        def halves_of(ap, lv):
            h = 64 >> lv
            return ap.rearrange("p n (b s j) -> p n b s j", s=2, j=h)

        def mid_of(d, hp, lv):
            h = 64 >> lv
            m = arr[:, d, hp, :, h:P + 1:2 * h]
            return m.unsqueeze(3).to_broadcast([P, NT, P // (2 * h), h])

        n_wjob = {}
        pos = 0
        for job in jobs:
            need = {"e": 1, "q": 1, "mk": 2, "mv": 2, "mq": 1, "naq": 1, "nak": 1, "nav": 1, "g": 1}.get(job[0], 0)
            if job[0] == "i" and job[1] == 0:
                need = 2
            for j in range(need):
                last = {"i": ("i", 1, 0)}.get(job[0], job[:3])
                n_wjob[pos + j] = at[last]
            pos += need

        @block.sync
        def _(sp):
            for i in range(NT):
                sp.dma_start(x_sb[:, i, :], dram["x"][i * P:(i + 1) * P, :]).then_inc(s_x, 16)
            for i in range(MT):
                sp.dma_start(mem_sb[:, i, :], dram["mem"][i * P:(i + 1) * P, :]).then_inc(s_mem, 16)
            for n, (kind, ct) in enumerate(weights):
                if n >= WSLOTS:
                    sp.wait_ge(pe_done, n_wjob[n - WSLOTS] + 1)
                src = dram["w_in"][ct] if kind == "z" else dram["w_kv"][ct]
                sp.dma_start(wring[:, n % WSLOTS, :, :], src).then_inc(s_w[n % WSLOTS], 16)

        consts = [(ident[:], "ident"), (gain_a[:], "attn_norm_g"), (gain_m[:], "mem_norm_g"),
                  (gain_o[:], "hg_out_norm_g"), (bound[:], "hg_lower_bound"), (masks[:], "level_masks"),
                  (halves[:], "head_mean")]

        @block.scalar
        def _(act):
            for dst, name in consts:
                act.dma_start(dst, dram[name]).then_inc(s_const, 16)
            act.wait_ge(s_x, 16 * NT)
            act.wait_ge(s_mem, 16 * MT)
            for i in range(NT + MT):
                src = x_sb[:, i, :] if i < NT else mem_sb[:, i - NT, :]
                dst = xn[:, i, :] if i < NT else hT[:, 2 * (i - NT):2 * (i - NT) + 2, :].rearrange("p a t -> p (a t)")
                act.activation(dst, src, ACT.Square, accum_out=ss[:, i:i + 1]).then_inc(s_sq, 1)
            act.wait_ge(s_sq, NT + MT)
            act.wait_ge(s_rstd, 1)
            act.activation(std[:], ss[:], ACT.Sqrt, bias=eps[:, 0:1], scale=1.0 / D).then_inc(s_std, 1)
            act.wait_ge(s_const, 16 * len(consts))

            def empty(key):
                n = at[key]
                act.wait_ge(pe_done, n + 1)
                src = bank(n)
                kind, a, b = key
                if kind == "hT":
                    return act.activation(hT[:, a, :], src, ACT.Identity, scale=gain_a[:, a:a + 1])
                if kind == "mT":
                    return act.activation(mT[:, a, :], src[:, 0:MEM], ACT.Identity, scale=gain_m[:, a:a + 1])
                if kind == "e":
                    return act.activation(kk[:, a, b, :], src, ACT.Exp, scale=-1.0)
                if kind == "q":
                    return act.copy(q[:, a, :], src)
                if kind == "i":
                    return act.copy(v[:, 2 * a:2 * a + 2, :], src.rearrange("p (n c) -> p n c", n=2))
                if kind == "mk":
                    return act.copy(mk[:], src.rearrange("p (n c) -> p n c", n=2))
                if kind == "mv":
                    return act.copy(mv[:], src.rearrange("p (n c) -> p n c", n=2))
                if kind == "mq":
                    return act.copy(mq[:, a, :], src)
                if kind in ("naq", "nak", "nav"):
                    if kind == "nav" and a:
                        act.wait_ge(pe_done, at[("navT", a - 1, 0)] + 1)
                    dst = {"naq": naq[:, a, :], "nak": nak[:, a, :], "nav": nvT[:]}[kind]
                    return act.copy(dst.rearrange("p (c r) -> p r c", r=ROWS),
                                    src.rearrange("p (r c) -> p r c", r=ROWS))
                if kind == "navT":
                    return act.copy(nav[:, :, a * P:(a + 1) * P], src.rearrange("p (n c) -> p n c", n=NT))
                if kind == "g":
                    return act.copy(gz[:, a, :], src)
                if kind == "x":
                    m = b
                    row = Am[:, a % 2, m * T:(m + 1) * T]
                    if a >= 2:
                        await_emptied(act, ("o", 0, 0))
                    if 0 < m < NT - 1:
                        act.copy(row[:, 0:m * P], src[:, 0:m * P])
                    if m < NT - 1:
                        return act.copy(row[:, (m + 1) * P:], src[:, (m + 1) * P:])
                    return act.copy(row[:, 0:m * P], src[:, 0:m * P])
                if kind == "ms":
                    return act.activation(orst[:, a, :], src, ACT.Sqrt, bias=eps[:, 0:1])

            def log_f():
                act.wait_ge(s_gate, 6)
                act.activation(lf, kk[:], ACT.Ln).then_inc(s_lf, 1)

            def level_exps(hp, lv):
                s = level_step(hp, lv)
                act.wait_ge(s_dec, 4 * (s + 1))
                act.activation(dec[:, s % 2, :, :], dec[:, s % 2, :, :], ACT.Exp).then_inc(s_exp, 1)

            def inter_exps(hp):
                act.wait_ge(s_idec, 2 * (hp + 1))
                if hp == 0:
                    act.activation(ebt[:], arr[:, :, :, :, P], ACT.Exp).then_inc(s_ebt, 1)
                act.activation(inter[:, hp, 1:3, :], inter[:, hp, 1:3, :], ACT.Exp).then_inc(s_iexp, 1)
                act.activation(inter[:, hp, QF, :].rearrange("p (n t) -> p n t", n=NT),
                               arr[:, 0, hp, :, 1:P + 1], ACT.Exp).then_inc(s_iexp, 1)
                act.activation(inter[:, hp, KB, :].rearrange("p (n t) -> p n t", n=NT),
                               arr[:, 1, hp, :, 0:P], ACT.Exp).then_inc(s_iexp, 1)

            act.wait_ge(s_lb, 1)
            act.activation(lbt[:], lbt[:], ACT.Exp).then_inc(s_std, 1)

            for job in jobs:
                if job[3] == "act":
                    empty(job[:3]).then_inc(act_ev, 1)
                if job[:3] == ("i", 1, 0):
                    log_f()
                    level_exps(0, 0)
                if job[0] == "lev" and job[2] % 2 == 1:
                    hp, lv = job[2] // 2, job[1]
                    if lv + 1 < LEVELS:
                        level_exps(hp, lv + 1)
                    elif lv + 1 == LEVELS:
                        inter_exps(hp)
                if job[0] == "x" and job[1] == 1 and job[2] == NT - 1:
                    level_exps(1, 0)
                if job[:3] == ("g", 1, 0):
                    await_emptied(act, ("g", 1, 0))
                    act.activation(sil, gz, ACT.Exp, scale=-1.0).then_inc(s_sil, 1)

        @block.gpsimd
        def _(pool):
            pool.memset(arr[:, :, :, :, 0:1], 0.0).then_inc(s_scan, 1)

            def level_products(hp, lv):
                s = level_step(hp, lv)
                pool.wait_ge(s_exp, s + 1)
                if s >= RING:
                    pool.wait_ge(pe_done, at[("lev", (s - RING) % LEVELS, 2 * ((s - RING) // LEVELS) + 1)] + 1)
                pool.tensor_tensor(qk[:, s % RING, 0, :], q[:, hp, :], dec[:, s % 2, 0, :], ALU.mult).then_inc(s_qk, 1)
                for side in range(2):
                    pick = lambda ap: halves_of(ap.rearrange("p (n t) -> p n t", n=NT), lv)[:, :, :, side, :]
                    pool.tensor_tensor(pick(qk[:, s % RING, 1, :]), pick(kk[:, side, hp, :]),
                                       pick(dec[:, s % 2, 1, :]), ALU.mult).then_inc(s_qk, 1)

            def inter_products(hp):
                pool.wait_ge(s_iexp, 3 * (hp + 1))
                for kind, src in ((QF, q[:, hp, :]), (KF, kk[:, 0, hp, :]), (QB, q[:, hp, :]), (KB, kk[:, 1, hp, :])):
                    pool.tensor_tensor(inter[:, hp, kind, :], inter[:, hp, kind, :], src, ALU.mult).then_inc(s_inter, 1)
                pool.wait_ge(s_inter, 4 * (hp + 1))
                pool.wait_ge(s_ebt, 1)
                if hp:
                    pool.wait_ge(pe_done, at[("x", 1, NT - 1)] + 1)
                qf = inter[:, hp, QF, :].rearrange("p (n t) -> p n t", n=NT)
                qb = inter[:, hp, QB, :].rearrange("p (n t) -> p n t", n=NT)
                pool.tensor_scalar(ext[:, 0, :], qf[:, 2, :], ebt[:, 0, hp, 1:2], None, ALU.mult).then_inc(s_ext, 1)
                pool.tensor_scalar(ext[:, 1, :], qf[:, 3, :], ebt[:, 0, hp, 2:3], None, ALU.mult).then_inc(s_ext, 1)
                pool.tensor_scalar(ext[:, 3, :], qb[:, 0, :], ebt[:, 1, hp, 1:2], None, ALU.mult).then_inc(s_ext, 1)
                pool.tensor_scalar(ext[:, 4, :], qb[:, 1, :], ebt[:, 1, hp, 2:3], None, ALU.mult).then_inc(s_ext, 1)
                pool.wait_ge(s_ext, 6 * hp + 4)
                pool.tensor_scalar(ext[:, 2, :], ext[:, 1, :], ebt[:, 0, hp, 1:2], None, ALU.mult).then_inc(s_ext, 1)
                pool.tensor_scalar(ext[:, 5, :], ext[:, 3, :], ebt[:, 1, hp, 2:3], None, ALU.mult).then_inc(s_ext, 1)

            pool.wait_ge(s_k, 1)
            await_emptied(pool, ("q", 1, 0))
            for hp in range(HPS):
                for lv in range(LEVELS):
                    level_products(hp, lv)
                inter_products(hp)

        @block.vector
        def _(dve):
            dve.memset(eps[:], EPS).then_inc(s_rstd, 1)
            dve.wait_ge(s_std, 1)
            dve.reciprocal(rstd[:], std[:]).then_inc(s_rstd, 1)
            dve.wait_ge(s_rstd, 2)
            for i in range(NT + MT):
                if i < NT:
                    dve.tensor_scalar(xn[:, i, :], x_sb[:, i, :], rstd[:, i:i + 1], None, ALU.mult).then_inc(s_xn, 1)
                else:
                    m = mem_sb[:, i - NT, :]
                    dve.tensor_scalar(m, m, rstd[:, i:i + 1], None, ALU.mult).then_inc(s_xn, 1)
            dve.wait_ge(s_const, 16 * len(consts))
            dve.tensor_tensor(lbt[:], bound[:, :, :, 1], bound[:, :, :, 0], ALU.subtract).then_inc(s_lb, 1)
            dve.wait_ge(s_std, 2)
            dve.tensor_scalar(lb1[:], lbt[:], 1.0, None, ALU.add).then_inc(s_lb, 1)
            dve.wait_ge(s_lb, 2)
            dve.reciprocal(lb[:], lb1[:]).then_inc(s_lb, 1)
            dve.wait_ge(s_lb, 3)
            dve.tensor_scalar(lb1[:], lb[:], -1.0, 1.0, ALU.mult, ALU.add).then_inc(s_lb, 1)

            diag_n = Tally(s_diag)

            def diag(h):
                return Am[:, h % 2, :].rearrange("p (n t) -> p n t", n=NT)[:, :, 0:P]

            def empty(key):
                n = at[key]
                dve.wait_ge(pe_done, n + 1)
                src = bank(n)
                kind, a, b = key
                if kind == "hT":
                    dve.tensor_scalar(hT[:, a, :], src, gain_a[:, a:a + 1], None, ALU.mult).then_inc(dve_ev, 1)
                if kind == "mT":
                    dve.tensor_scalar(mT[:, a, :], src[:, 0:MEM], gain_m[:, a:a + 1], None, ALU.mult).then_inc(dve_ev, 1)
                if kind == "lev":
                    lv, h = a, b
                    mask = masks[:, lv, :].unsqueeze(1).to_broadcast([P, NT, P])
                    s4 = src.rearrange("p (n t) -> p n t", n=NT)
                    if lv == 0:
                        if h >= 2:
                            dve.wait_ge(pe_done, at[("o", 0, 0)] + 1)
                        dve.tensor_tensor(diag(h), s4, mask, ALU.mult).then_inc(dve_ev, 1)
                    else:
                        t4 = tmp[:, h % 2, :].rearrange("p (n t) -> p n t", n=NT)
                        if diag_n.n >= 2:
                            dve.wait_ge(s_diag, diag_n.n - 1)
                        dve.tensor_tensor(t4, s4, mask, ALU.mult).then_inc(dve_ev, 1)
                        dve.wait_ge(dve_ev, emptied[n][1])
                        if diag_n.n >= 2:
                            dve.wait_ge(s_diag, diag_n.n - 1)
                        diag_n.inc(dve.tensor_tensor(diag(h), diag(h), t4, ALU.add))
                if kind == "o":
                    dve.tensor_copy(oT[:, a, :], src).then_inc(dve_ev, 1)
                    dve.wait_ge(dve_ev, emptied[n][1])
                    dve.tensor_tensor(osq[:, a, :], oT[:, a, :], oT[:, a, :], ALU.mult).then_inc(s_osq, 1)

            def decays(hp, lv):
                s = level_step(hp, lv)
                if s >= 2:
                    dve.wait_ge(s_qk, 3 * (s - 1))
                X = [arr[:, d, hp, :, 1 - d:P + 1 - d] for d in range(2)]
                dq = halves_of(dec[:, s % 2, 0, :].rearrange("p (n t) -> p n t", n=NT), lv)
                dk = halves_of(dec[:, s % 2, 1, :].rearrange("p (n t) -> p n t", n=NT), lv)
                xf, xb = halves_of(X[0], lv), halves_of(X[1], lv)
                mf, mb = mid_of(0, hp, lv), mid_of(1, hp, lv)
                for dst, a, b in ((dq[:, :, :, 1, :], xf[:, :, :, 1, :], mf), (dq[:, :, :, 0, :], mb, xb[:, :, :, 0, :]),
                                  (dk[:, :, :, 0, :], mf, xf[:, :, :, 0, :]), (dk[:, :, :, 1, :], xb[:, :, :, 1, :], mb)):
                    dve.tensor_tensor(dst, a, b, ALU.subtract).then_inc(s_dec, 1)

            def inter_decays(hp):
                for kind, d in ((KF, 0), (QB, 1)):
                    tot = arr[:, d, hp, :, P:P + 1].to_broadcast([P, NT, P])
                    dve.tensor_tensor(inter[:, hp, kind, :].rearrange("p (n t) -> p n t", n=NT), tot,
                                      arr[:, d, hp, :, 1 - d:P + 1 - d], ALU.subtract).then_inc(s_idec, 1)

            for job in jobs:
                if job[3] == "dve":
                    empty(job[:3])
                if job[:3] == ("i", 1, 0):
                    await_emptied(dve, ("e", 1, 1))
                    dve.tensor_scalar(kk[:], kk[:], 1.0, None, ALU.add).then_inc(s_gate, 1)
                    dve.wait_ge(s_gate, 1)
                    dve.reciprocal(kk[:], kk[:]).then_inc(s_gate, 1)
                    dve.wait_ge(s_gate, 2)
                    dve.wait_ge(s_lb, 4)
                    for d in range(2):
                        for hp in range(HPS):
                            dve.tensor_scalar(kk[:, d, hp, :], kk[:, d, hp, :], lb1[:, d, hp:hp + 1], lb[:, d, hp:hp + 1],
                                              ALU.mult, ALU.add).then_inc(s_gate, 1)
                    dve.wait_ge(s_gate, 6)
                    dve.wait_ge(s_lf, 1)
                    dve.tensor_scalar(kk[:], kk[:], -1.0, 1.0, ALU.mult, ALU.add).then_inc(s_k, 1)
                    dve.wait_ge(s_scan, 1)
                    for d in range(2):
                        for hp in range(HPS):
                            for n in range(NT):
                                seg = lf[:, d, hp, n * P:(n + 1) * P]
                                dve.tensor_tensor_scan(arr[:, d, hp, n, 1:P + 1], seg, seg, 0.0,
                                                       ALU.add, ALU.bypass).then_inc(s_scan, 1)
                    dve.wait_ge(s_k, 1)
                    dve.tensor_tensor(ksum[:], kk[:, 0, :, :], kk[:, 1, :, :], ALU.add).then_inc(s_ksum, 1)
                    dve.wait_ge(s_scan, 1 + 4 * NT)
                    decays(0, 0)
                if job[0] == "lev" and job[2] % 2 == 0:
                    hp, lv = job[2] // 2, job[1]
                    if lv + 1 < LEVELS:
                        decays(hp, lv + 1)
                    elif lv + 1 == LEVELS:
                        inter_decays(hp)
                        if hp == 0:
                            decays(1, 0)

            def tail_wait(n):
                dve.wait_ge(s_fin, n)
            dve.wait_ge(s_sil, 1)
            dve.tensor_scalar(sil, sil, 1.0, None, ALU.add).then_inc(s_fin, 1)
            tail_wait(1)
            dve.reciprocal(sil, sil).then_inc(s_fin, 1)
            tail_wait(2)
            dve.tensor_tensor(sil, sil, gz, ALU.mult).then_inc(s_fin, 1)
            await_emptied(dve, ("ms", 1, 0))
            dve.reciprocal(orst, orst).then_inc(s_fin, 1)
            tail_wait(4)
            dve.tensor_tensor(oT, oT, orst, ALU.mult).then_inc(s_fin, 1)
            tail_wait(5)
            for hp in range(HPS):
                dve.scalar_tensor_tensor(hg_out[:, hp, :], oT[:, hp, :], gain_o[:, hp:hp + 1], sil[:, hp, :],
                                         ALU.mult, ALU.mult).then_inc(s_fin, 1)

        @block.tensor
        def _(pe):
            wpos = [0]

            def weight_slots(k):
                slots = []
                for _ in range(k):
                    n = wpos[0]
                    pe.wait_ge(s_w[n % WSLOTS], 16 * (n // WSLOTS + 1))
                    slots.append(n % WSLOTS)
                    wpos[0] += 1
                return slots

            def project(out, slot, src, cols):
                for k in range(KD):
                    last = pe.matmul(out, wring[:, slot, k, :], src[:, k, cols], start=(k == 0), stop=(k == KD - 1))
                return last

            def project_natural(out, src, first, count):
                for k in range(KD):
                    last = pe.matmul(out, src(k), wring[:, first:first + count, k, :], start=(k == 0), stop=(k == KD - 1))
                return last

            def run(n, key):
                kind, a, b = key
                out = bank(n)
                if kind == "hT":
                    for i in range(NT):
                        last = pe.transpose(out[:, i * P:(i + 1) * P], xn[:, i, a * P:(a + 1) * P], ident[:])
                elif kind == "mT":
                    for i in range(MT):
                        last = pe.transpose(out[:, i * P:(i + 1) * P], mem_sb[:, i, a * P:(a + 1) * P], ident[:])
                elif kind in ("e", "q", "mq", "naq", "nak", "nav", "g"):
                    last = project(out, weight_slots(1)[0], hT, slice(0, T))
                elif kind == "mk":
                    for j, slot in enumerate(weight_slots(2)):
                        last = project(out[:, j * MEM:(j + 1) * MEM], slot, mT, slice(0, MEM))
                elif kind == "mv":
                    slots = weight_slots(2)
                    for m in range(MT):
                        for j, slot in enumerate(slots):
                            last = project_natural(out[:, m * MEM + j * P:m * MEM + (j + 1) * P],
                                                   lambda k: mT[:, k, m * P:(m + 1) * P], slot, 1)
                elif kind == "i":
                    if a == 0:
                        i_slots.extend(weight_slots(2))
                    for t in range(2):
                        for j, slot in enumerate(i_slots):
                            tok = 2 * a + t
                            last = project_natural(out[:, t * MEM + j * P:t * MEM + (j + 1) * P],
                                                   lambda k: hT[:, k, tok * P:(tok + 1) * P], slot, 1)
                elif kind == "navT":
                    await_emptied(pe, ("nav", a, 0))
                    for t in range(NT):
                        last = pe.transpose(out[:, t * P:(t + 1) * P], nvT[:, t * P:(t + 1) * P], ident[:])
                elif kind == "lev":
                    lv, h = a, b
                    hp, r = h // 2, slice(HD * (h % 2), HD * (h % 2) + HD)
                    if lv < LEVELS:
                        s = level_step(hp, lv)
                        pe.wait_ge(s_qk, 3 * (s + 1))
                        kt, qt = qk[r, s % RING, 1, :], qk[r, s % RING, 0, :]
                    else:
                        pe.wait_ge(s_ksum, 1)
                        kt, qt = ksum[r, hp, :], q[r, hp, :]
                    for t in range(NT):
                        c = slice(t * P, (t + 1) * P)
                        last = pe.matmul(out[:, c], kt[:, c], qt[:, c], start=True, stop=True)
                elif kind == "x":
                    h, m = a, b
                    hp, r = h // 2, slice(HD * (h % 2), HD * (h % 2) + HD)
                    if m == 0:
                        pe.wait_ge(s_ext, 6 * (hp + 1))
                    for t in range(NT):
                        if t == m:
                            continue
                        far = abs(t - m)
                        kt = inter[r, hp, KF if t > m else KB, m * P:(m + 1) * P]
                        if far == 1:
                            qt = inter[r, hp, QF if t > m else QB, t * P:(t + 1) * P]
                        elif far == 2:
                            qt = ext[r, (t - 2) if t > m else (3 + t), :]
                        else:
                            qt = ext[r, 2 if t > m else 5, :]
                        last = pe.matmul(out[:, t * P:(t + 1) * P], kt, qt, start=True, stop=True)
                elif kind == "o":
                    hp = a
                    await_emptied(pe, ("x", 2 * hp + 1, NT - 1))
                    pe.wait_ge(s_diag, 2 * LEVELS * (hp + 1))
                    for s in range(2):
                        h = 2 * hp + s
                        for m in range(NT):
                            last = pe.matmul(out[s * HD:(s + 1) * HD, :], v[:, m, h * HD:(h + 1) * HD],
                                             Am[:, s, m * T:(m + 1) * T], start=(m == 0), stop=(m == NT - 1))
                elif kind == "ms":
                    pe.wait_ge(s_osq, a + 1)
                    last = pe.matmul(out, halves[:], osq[:, a, :], start=True, stop=True)
                return last

            i_slots = []
            pe.wait_ge(s_const, 16 * len(consts))
            pe.wait_ge(s_xn, NT + MT)
            first_z = at[("e", 0, 0)]
            for n, job in enumerate(jobs):
                if n >= BANKS:
                    who, count = emptied[n - BANKS]
                    pe.wait_ge(ev[who], count)
                if n == first_z:
                    await_emptied(pe, ("hT", KD - 1, 0))
                    await_emptied(pe, ("hT", KD - 2, 0))
                if job[:3] == ("mk", 0, 0):
                    await_emptied(pe, ("mT", KD - 1, 0))
                    await_emptied(pe, ("mT", KD - 2, 0))
                run(n, job[:3]).then_inc(pe_done, 1)


def build_attention(nc, dram, keep, psum):
    PAIRS_NA, PAIRS = NA_HEADS // 2, (NA_HEADS + MEM_HEADS) // 2
    UNITS = PAIRS * 2 * NT
    NA_UNITS = PAIRS_NA * 2 * NT
    S_SLOTS, T_SLOTS, T_LAG, V_LAG = 4, 3, 3, 4
    MAXK = 3 * P
    with ExitStack() as ctx:
        def sb(name, shape, dt=F32):
            return ctx.enter_context(nc.sbuf_tensor(name, shape, dt))

        def sem(name):
            return ctx.enter_context(nc.semaphore(name))

        ident, x_sb, hg_out = keep["ident"], keep["x"], keep["hg_out"]
        h2hi, h2lo = keep["h2hi"], keep["h2lo"]
        naq, nak, nav = keep["naq"], keep["nak"], keep["nav"]
        mq, mk, mv = keep["mq"], keep["mk"], keep["mv"]
        mixT = sb("mixT", [P, PAIRS, T])
        bias = sb("bias", [P, NA_HEADS, MAXK])
        wmask = sb("wmask", [P, NT, MAXK])
        bm = sb("bias_masked", [P, 2, NT, MAXK])
        prob = sb("prob", [P, S_SLOTS, MAXK])
        probT = sb("probT", [P, T_SLOTS, MAXK])
        nmax = sb("nmax", [P, UNITS])
        total = sb("total", [P, UNITS])
        inv = sb("inv", [P, UNITS])
        w_out = sb("w_out", [P, KD, D])
        h2 = sb("h2", [P, NT, D])
        ss = sb("ss2", [P, NT])
        std = sb("std2", [P, NT])
        rstd = sb("rstd2", [P, NT])
        eps = sb("eps2", [P, 1])
        gain = sb("gain_f", [P, KD])

        s_in, s_wo = sem("bias_in"), sem("wout_in")
        s_score, s_scaled, s_max, s_exp, s_inv, s_prob = (sem("score"), sem("scaled"), sem("nmax_ready"),
                                                          sem("exp_done"), sem("inv_ready"), sem("prob_ready"))
        s_turned, s_probT, s_pv, s_out, s_bm = (sem("turned"), sem("probT_ready"), sem("pv"), sem("mix_ready"),
                                                sem("bm_ready"))
        s_proj, s_x2, s_sq, s_std, s_rstd, s_h2 = (sem("proj"), sem("x2"), sem("sumsq2"), sem("std2_r"),
                                                   sem("rstd2_r"), sem("h2_ready"))
        s_hT, s_hi, s_lo = sem("h2T_pe"), sem("h2hi_r"), sem("h2lo_r")
        block = ctx.enter_context(nc.Block())

        def unit(u):
            pair, side, g = u // (2 * NT), (u // NT) % 2, u % NT
            return pair, side, g, (key_tiles(g) if pair < PAIRS_NA else [0, 1])

        def width(u):
            return P * len(unit(u)[3])

        def rows(side):
            return slice(side * HD, side * HD + HD)

        @block.sync
        def _(sp):
            sp.dma_start(wmask[:], dram["window_masks"]).then_inc(s_in, 16)
            for cq in range(WIN):
                sp.dma_start(bias[cq * ROWS:(cq + 1) * ROWS, :, :],
                             dram["na_rpb"][:, :, (WIN - 1 - cq) * ROWS:(WIN - 1 - cq) * ROWS + MAXK]).then_inc(s_in, 16)
            sp.dma_start(gain[:], dram["ffn_norm_g"]).then_inc(s_in, 16)
            sp.dma_start(w_out[:], dram["w_out"].rearrange("(k p) n -> p k n", p=P)).then_inc(s_wo, 16)

        IN_ALL = 16 * (WIN + 2)

        @block.gpsimd
        def _(pool):
            pool.wait_ge(s_in, IN_ALL)

            def masked_bias(h):
                if h >= 2:
                    pool.wait_ge(s_scaled, NT * (h - 1))
                pool.tensor_tensor(bm[:, h % 2, :, :], wmask[:],
                                   bias[:, h, :].unsqueeze(1).to_broadcast([P, NT, MAXK]), ALU.add).then_inc(s_bm, 1)

            masked_bias(0)
            masked_bias(1)
            for u in range(UNITS):
                w = width(u)
                pool.wait_ge(s_inv, u + 1)
                pool.tensor_scalar(prob[:, u % S_SLOTS, 0:w], prob[:, u % S_SLOTS, 0:w], inv[:, u:u + 1], None,
                                   ALU.mult).then_inc(s_prob, 1)
                if u < NA_UNITS and u % NT == NT - 1 and u // NT + 2 < NA_HEADS:
                    masked_bias(u // NT + 2)

        @block.scalar
        def _(act):
            def exps(u):
                w = width(u)
                act.wait_ge(s_max, u + 1)
                act.activation(prob[:, u % S_SLOTS, 0:w], prob[:, u % S_SLOTS, 0:w], ACT.Exp, bias=nmax[:, u:u + 1],
                               accum_out=total[:, u:u + 1]).then_inc(s_exp, 1)

            def move_probT(u):
                w = width(u)
                act.wait_ge(s_turned, u + 1)
                if u >= T_SLOTS:
                    act.wait_ge(s_pv, u - T_SLOTS + 1)
                act.copy(probT[:, u % T_SLOTS, 0:w], psum[:, 3 + u % 3, 0:w]).then_inc(s_probT, 1)

            for u in range(UNITS + T_LAG):
                if u < UNITS:
                    exps(u)
                if u >= T_LAG:
                    move_probT(u - T_LAG)
            act.wait_ge(s_in, IN_ALL)
            for i in range(NT):
                act.wait_ge(s_x2, 2 * (i + 1) + 1)
                act.activation(h2[:, i, :], x_sb[:, i, :], ACT.Square, accum_out=ss[:, i:i + 1]).then_inc(s_sq, 1)
            act.wait_ge(s_sq, NT)
            act.activation(std[:], ss[:], ACT.Sqrt, bias=eps[:, 0:1], scale=1.0 / D).then_inc(s_std, 1)
            for k in range(KD):
                act.wait_ge(s_hT, k + 1)
                act.activation(h2hi[:, k, :], psum[:, k, :], ACT.Identity, scale=gain[:, k:k + 1]).then_inc(s_hi, 1)

        @block.vector
        def _(dve):
            dve.memset(eps[:], EPS).then_inc(s_x2, 1)

            def scaled_max(u):
                pair, side, g, keys = unit(u)
                w = width(u)
                dve.wait_ge(s_score, u + 1)
                if u >= S_SLOTS:
                    dve.wait_ge(s_turned, u - S_SLOTS + 1)
                dst = prob[:, u % S_SLOTS, 0:w]
                if pair < PAIRS_NA:
                    h = 2 * pair + side
                    dve.wait_ge(s_bm, h + 1)
                    off = (keys[0] - g + 1) * P
                    dve.scalar_tensor_tensor(dst, psum[:, u % 3, 0:w], SCALE, bm[:, h % 2, g, off:off + w],
                                             ALU.mult, ALU.add).then_inc(s_scaled, 1)
                else:
                    dve.tensor_scalar(dst, psum[:, u % 3, 0:w], SCALE, None, ALU.mult).then_inc(s_scaled, 1)
                dve.wait_ge(s_scaled, u + 1)
                dve.tensor_reduce(nmax[:, u:u + 1], dst, AX.X, ALU.max, negate=True).then_inc(s_max, 1)

            def invert(u):
                dve.wait_ge(s_exp, u + 1)
                dve.reciprocal(inv[:, u:u + 1], total[:, u:u + 1]).then_inc(s_inv, 1)

            def move_out(pair):
                dve.wait_ge(s_pv, 2 * NT * (pair + 1))
                src = psum[:, 6 + pair % 2, :]
                if pair < PAIRS_NA:
                    dve.tensor_copy(mixT[:, pair, :].rearrange("p (r c) -> p r c", r=ROWS),
                                    src.rearrange("p (c r) -> p r c", r=ROWS)).then_inc(s_out, 1)
                else:
                    dve.tensor_copy(mixT[:, pair, :], src).then_inc(s_out, 1)

            for u in range(UNITS + V_LAG + 1):
                if u < UNITS:
                    scaled_max(u)
                if 1 <= u <= UNITS:
                    invert(u - 1)
                done = u - V_LAG
                if done >= 1 and done % (2 * NT) == 0:
                    move_out(done // (2 * NT) - 1)
            for n in range(2 * NT):
                i, half = n // 2, slice((n % 2) * BANK, (n % 2) * BANK + BANK)
                dve.wait_ge(s_proj, n + 1)
                dve.tensor_tensor(x_sb[:, i, half], psum[:, n, :], x_sb[:, i, half], ALU.add).then_inc(s_x2, 1)
            dve.wait_ge(s_std, 1)
            dve.reciprocal(rstd[:], std[:]).then_inc(s_rstd, 1)
            dve.wait_ge(s_rstd, 1)
            for i in range(NT):
                dve.tensor_scalar(h2[:, i, :], x_sb[:, i, :], rstd[:, i:i + 1], None, ALU.mult).then_inc(s_h2, 1)
            for k in range(KD):
                dve.wait_ge(s_hi, k + 1)
                dve.scalar_tensor_tensor(h2lo[:, k, :], psum[:, k, :], gain[:, k:k + 1], h2hi[:, k, :].bitcast(F32),
                                         ALU.mult, ALU.subtract).then_inc(s_lo, 1)

        @block.tensor
        def _(pe):
            def scores(u):
                pair, side, g, keys = unit(u)
                w, r = width(u), rows(side)
                if u >= 3:
                    pe.wait_ge(s_scaled, u - 2)
                if pair < PAIRS_NA:
                    q, k = naq[r, pair, g * P:(g + 1) * P], nak[r, pair, keys[0] * P:keys[0] * P + w]
                else:
                    q, k = mq[r, pair - PAIRS_NA, g * P:(g + 1) * P], mk[r, pair - PAIRS_NA, :]
                pe.matmul(psum[:, u % 3, 0:w], q, k, start=True, stop=True).then_inc(s_score, 1)

            def turn(u):
                pe.wait_ge(s_prob, u + 1)
                if u >= 3:
                    pe.wait_ge(s_probT, u - 2)
                for j in range(len(unit(u)[3])):
                    last = pe.transpose(psum[:, 3 + u % 3, j * P:(j + 1) * P], prob[:, u % S_SLOTS, j * P:(j + 1) * P], ident[:])
                last.then_inc(s_turned, 1)

            def values(u):
                pair, side, g, keys = unit(u)
                pe.wait_ge(s_probT, u + 1)
                if u % (2 * NT) == 0 and pair >= 2:
                    pe.wait_ge(s_out, pair - 1)
                for j, kt in enumerate(keys):
                    if pair < PAIRS_NA:
                        h = 2 * pair + side
                        v = nav[:, kt, h * HD:(h + 1) * HD]
                    else:
                        h = 2 * (pair - PAIRS_NA) + side
                        v = mv[:, kt, h * HD:(h + 1) * HD]
                    last = pe.matmul(psum[rows(side), 6 + pair % 2, g * P:(g + 1) * P], v, probT[:, u % T_SLOTS, j * P:(j + 1) * P],
                                     start=(j == 0), stop=(j == len(keys) - 1))
                last.then_inc(s_pv, 1)

            for u in range(UNITS + V_LAG):
                if u < UNITS:
                    scores(u)
                if T_LAG <= u < UNITS + T_LAG:
                    turn(u - T_LAG)
                if u >= V_LAG:
                    values(u - V_LAG)
            pe.wait_ge(s_wo, 16)
            pe.wait_ge(s_out, PAIRS)
            pe.wait_ge(s_probT, UNITS)
            for n in range(2 * NT):
                i, half = n // 2, slice((n % 2) * BANK, (n % 2) * BANK + BANK)
                for k in range(KD):
                    src = hg_out[:, k - 4, :] if k in (4, 5) else mixT[:, k if k < 4 else k - 2, :]
                    last = pe.matmul(psum[:, n, :], src[:, i * P:(i + 1) * P], w_out[:, k, half],
                                     start=(k == 0), stop=(k == KD - 1))
                last.then_inc(s_proj, 1)
            pe.wait_ge(s_h2, NT)
            for k in range(KD):
                for i in range(NT):
                    last = pe.transpose(psum[:, k, i * P:(i + 1) * P], h2[:, i, k * P:(k + 1) * P], ident[:])
                last.then_inc(s_hT, 1)


def build_routing(nc, dram, keep, psum):
    HC = 2 * PH
    WSLOTS, SSLOTS = 3, 4
    with ExitStack() as ctx:
        def sb(name, shape, dt=F32):
            return ctx.enter_context(nc.sbuf_tensor(name, shape, dt))

        def sem(name):
            return ctx.enter_context(nc.semaphore(name))

        ident, chosen, acts = keep["ident"], keep["chosen"], keep["acts"]
        h2hi, h2lo = keep["h2hi"], keep["h2lo"]
        w_raw = sb("wq_raw", [P, WSLOTS, KD, P])
        w_hi = sb("wq_hi", [P, 2, KD, P], F32R)
        w_lo = sb("wq_lo", [P, 2, KD, P], F32R)
        u_raw = sb("u_raw3", [P, USLOTS, KD, P])
        u_hi = sb("u_hi3", [P, 2, KD, P], F32R)
        u_lo = sb("u_lo3", [P, 2, KD, P], F32R)
        gel = sb("gel3", [P, 2, T])
        keysT = sb("keysT", [P, HC, NKEYS])
        iota = sb("iota3", [P, P])
        query = sb("query", [P, 2, T])
        scores = sb("scores", [P, SSLOTS, NT, NKEYS])
        top = sb("top", [P, HC, NT, TOPK])
        top_i = sb("top_i", [P, HC, NT, TOPK], U32)
        top_f = sb("top_f", [P, HC, NT, TOPK])
        sums = sb("sums", [P, 2, NT, TOPK * TOPK])
        best = sb("best", [P, PH, NT, TOPK])
        place = sb("place", [P, PH, NT, TOPK], U32)
        place_ab = sb("place_ab", [P, 2, 2, NT, TOPK], U32)
        ab = sb("ab", [P, 2, 2, NT, TOPK])
        pick = sb("pick", [P, 2, 2, NT, TOPK * TOPK])
        found = sb("found", [P, 3, NT, PH, TOPK])
        gsum = sb("gsum", [P, PH, NT])
        ginv = sb("ginv", [P, PH, NT])

        s_in = sem("keys_in")
        s_w = [sem(f"wq_in{i}") for i in range(WSLOTS)]
        s_whi, s_wlo = sem("wq_hi_r"), sem("wq_lo_r")
        s_u = [sem(f"u3_in{i}") for i in range(USLOTS)]
        s_uhi, s_ulo, s_act, s_gel = sem("u3_hi_r"), sem("u3_lo_r"), sem("act3_pe"), sem("gel3_r")
        s_ast = [sem("acts3_out0"), sem("acts3_out1")]
        s_q, s_qsb, s_s, s_ssb = sem("query_pe"), sem("query_sb"), sem("scores_pe"), sem("scores_sb")
        s_top, s_ab, s_eq, s_pick, s_red, s_cast = (sem("top_steps"), sem("ab_ready"), sem("eq_ready"),
                                                    sem("pick_ready"), sem("picked"), sem("top_cast"))
        s_gin, s_gexp, s_g, s_turn, s_out = (sem("gate_in"), sem("gate_exp"), sem("gate_steps"), sem("chosen_pe"),
                                             sem("chosen_sb"))
        block = ctx.enter_context(nc.Block())

        @block.sync
        def _(sp):
            for n in range(EARLY_ROUTING + 4):
                if n < HC:
                    if n >= WSLOTS:
                        sp.wait_ge(s_wlo, n - WSLOTS + 1)
                    sp.dma_start(w_raw[:, n % WSLOTS, :, :], dram["w_query"][n]).then_inc(s_w[n % WSLOTS], 16)
                if n < EARLY_ROUTING:
                    if n >= USLOTS:
                        sp.wait_ge(s_ulo, n - USLOTS + 1)
                    sp.dma_start(u_raw[:, n % USLOTS, :, :], dram["peer_u"][2 * GROUP + n]).then_inc(s_u[n % USLOTS], 16)
                if n >= 4:
                    m = n - 4
                    sp.wait_ge(s_gel, m + 1)
                    sp.dma_start(acts[m], gel[:, m % 2, :]).then_inc(s_ast[m % 2], 16)
            for i in range(2):
                sp.wait_ge(s_ast[i], 16 * (EARLY_ROUTING // 2))

        @block.scalar
        def _(act):
            def split_w(n):
                act.wait_ge(s_w[n % WSLOTS], 16 * (n // WSLOTS + 1))
                if n >= 2:
                    act.wait_ge(s_q, n - 1)
                act.copy(w_hi[:, n % 2, :, :], w_raw[:, n % WSLOTS, :, :]).then_inc(s_whi, 1)

            def split_u(n):
                act.wait_ge(s_u[n % USLOTS], 16 * (n // USLOTS + 1))
                if n >= 2:
                    act.wait_ge(s_act, n - 1)
                act.copy(u_hi[:, n % 2, :, :], u_raw[:, n % USLOTS, :, :]).then_inc(s_uhi, 1)

            act.dma_start(keysT[:], dram["sub_keys"]).then_inc(s_in, 16)
            act.dma_start(iota[:], dram["iota"]).then_inc(s_in, 16)
            split_w(0)
            split_w(1)
            split_u(0)
            for n in range(EARLY_ROUTING + 1):
                if n < HC:
                    act.wait_ge(s_q, n + 1)
                    if n >= 2:
                        act.wait_ge(s_s, n - 1)
                    act.copy(query[:, n % 2, :], psum[:, n % 2, :]).then_inc(s_qsb, 1)
                    if n + 2 < HC:
                        split_w(n + 2)
                if n + 1 < EARLY_ROUTING:
                    split_u(n + 1)
                if 1 <= n <= HC:
                    act.wait_ge(s_s, n)
                    if n > SSLOTS:
                        act.wait_ge(s_cast, n - SSLOTS)
                    act.copy(scores[:, (n - 1) % SSLOTS, :, :],
                             psum[:, 2 + (n - 1) % 2, :].rearrange("p (t k) -> p t k", t=NT)).then_inc(s_ssb, 1)
                if n:
                    m = n - 1
                    act.wait_ge(s_act, m + 1)
                    if m >= 2:
                        act.wait_ge(s_ast[m % 2], 16 * (m // 2))
                    act.activation(gel[:, m % 2, :], psum[:, 6 + m % 2, :], ACT.Gelu).then_inc(s_gel, 1)
            act.wait_ge(s_gin, 1)
            act.activation(best[:], best[:], ACT.Exp).then_inc(s_gexp, 1)
            for j in range(3):
                act.wait_ge(s_turn, j + 1)
                act.copy(chosen[:, j, :], psum[:, CHOSEN_BANKS[j], :]).then_inc(s_out, 1)

        @block.gpsimd
        def _(pool):
            def rest_w(n):
                if n >= 2:
                    pool.wait_ge(s_q, n - 1)
                pool.wait_ge(s_whi, n + 1)
                pool.tensor_tensor(w_lo[:, n % 2, :, :], w_raw[:, n % WSLOTS, :, :], w_hi[:, n % 2, :, :].bitcast(F32),
                                   ALU.subtract).then_inc(s_wlo, 1)

            def rest_u(n):
                if n >= 2:
                    pool.wait_ge(s_act, n - 1)
                pool.wait_ge(s_uhi, n + 1)
                pool.tensor_tensor(u_lo[:, n % 2, :, :], u_raw[:, n % USLOTS, :, :], u_hi[:, n % 2, :, :].bitcast(F32),
                                   ALU.subtract).then_inc(s_ulo, 1)

            def key_numbers(h):
                for c in range(2):
                    dst = pick[:, h % 2, c, :, :].rearrange("p n (s a) -> p n s a", a=TOPK)
                    pool.wait_ge(s_eq, 2 * h + c + 1)
                    pool.wait_ge(s_cast, 2 * h + c + 1)
                    pool.tensor_tensor(dst, dst, top_f[:, 2 * h + c, :, :].unsqueeze(2).to_broadcast([P, NT, TOPK, TOPK]),
                                       ALU.mult).then_inc(s_pick, 1)

            rest_w(0)
            rest_w(1)
            rest_u(0)
            for n in range(EARLY_ROUTING):
                if n + 2 < HC:
                    rest_w(n + 2)
                if n + 1 < EARLY_ROUTING:
                    rest_u(n + 1)
                if n >= PICK_LAG and n % 2 == PICK_LAG % 2 and (n - PICK_LAG) // 2 < PH - 1:
                    key_numbers((n - PICK_LAG) // 2)
            key_numbers(PH - 1)

        @block.vector
        def _(dve):
            steps = Tally(s_top)
            small = iota[:, 0:TOPK].unsqueeze(1).unsqueeze(1).to_broadcast([P, NT, TOPK, TOPK])
            dve.wait_ge(s_in, 32)

            def top16(data, values, places):
                n = len(data)
                lo, hi = slice(0, 8), slice(8, 16)
                back = lambda: dve.wait_ge(s_top, steps.n - n + 1)
                for i in range(n):
                    steps.inc(dve.max(values(i)[:, lo], data[i]))
                for i in range(n):
                    back()
                    steps.inc(dve.max_index(places(i)[:, lo], values(i)[:, lo], data[i]))
                for i in range(n):
                    back()
                    steps.inc(dve.match_replace(data[i], values(i)[:, lo], data[i], NEG))
                for i in range(n):
                    back()
                    steps.inc(dve.max(values(i)[:, hi], data[i]))
                for i in range(n):
                    back()
                    steps.inc(dve.max_index(places(i)[:, hi], values(i)[:, hi], data[i]))

            def reduce_picks(h):
                dve.wait_ge(s_pick, 2 * (h + 1))
                for c in range(2):
                    dve.tensor_reduce(found[:, c, :, h, :], pick[:, h % 2, c, :, :].rearrange("p n (s a) -> p n s a", a=TOPK),
                                      AX.X, ALU.add).then_inc(s_red, 1)

            for n in range(HC):
                h = n // 2
                dve.wait_ge(s_ssb, n + 1)
                top16([scores[:, n % SSLOTS, t, :] for t in range(NT)], lambda t: top[:, n, t, :], lambda t: top_i[:, n, t, :])
                dve.wait_ge(s_top, steps.n)
                dve.tensor_copy(top_f[:, n, :, :], top_i[:, n, :, :]).then_inc(s_cast, 1)
                if n % 2:
                    s4 = sums[:, h % 2, :, :].rearrange("p n (a b) -> p n a b", b=TOPK)
                    steps.inc(dve.tensor_tensor(s4, top[:, n - 1, :, :].unsqueeze(3).to_broadcast([P, NT, TOPK, TOPK]),
                                                top[:, n, :, :].unsqueeze(2).to_broadcast([P, NT, TOPK, TOPK]), ALU.add))
                    dve.wait_ge(s_top, steps.n)
                    top16([sums[:, h % 2, t, :] for t in range(NT)], lambda t: best[:, h, t, :], lambda t: place[:, h, t, :])
                    dve.wait_ge(s_top, steps.n)
                    if h >= 2:
                        dve.wait_ge(s_eq, 2 * (h - 1))
                    steps.inc(dve.tensor_scalar(place_ab[:, h % 2, 0, :, :], place[:, h, :, :], 4, None, ALU.logical_shift_right))
                    steps.inc(dve.tensor_scalar(place_ab[:, h % 2, 1, :, :], place[:, h, :, :], 15, None, ALU.bitwise_and))
                    dve.wait_ge(s_top, steps.n)
                    dve.wait_ge(s_cast, n + 1)
                    dve.tensor_copy(ab[:, h % 2, :, :, :], place_ab[:, h % 2, :, :, :]).then_inc(s_ab, 1)
                    dve.wait_ge(s_ab, h + 1)
                    if h >= 2:
                        dve.wait_ge(s_red, 2 * (h - 1))
                    for c in range(2):
                        dst = pick[:, h % 2, c, :, :].rearrange("p n (s a) -> p n s a", a=TOPK)
                        src = ab[:, h % 2, c, :, :].unsqueeze(3).to_broadcast([P, NT, TOPK, TOPK])
                        dve.tensor_tensor(dst, src, small, ALU.is_equal).then_inc(s_eq, 1)
                    if h:
                        reduce_picks(h - 1)
            steps.inc(dve.tensor_copy(gsum[:], best[:, :, :, 0]))
            dve.wait_ge(s_top, steps.n)
            dve.tensor_tensor(best[:], best[:], gsum[:].unsqueeze(3).to_broadcast([P, PH, NT, TOPK]), ALU.subtract).then_inc(s_gin, 1)
            reduce_picks(PH - 1)
            dve.wait_ge(s_gexp, 1)
            dve.tensor_reduce(gsum[:], best[:], AX.X, ALU.add).then_inc(s_g, 1)
            dve.wait_ge(s_g, 1)
            dve.reciprocal(ginv[:], gsum[:]).then_inc(s_g, 1)
            dve.wait_ge(s_g, 2)
            dve.tensor_tensor(found[:, 2, :, :, :].rearrange("p n h s -> p h n s"), best[:],
                              ginv[:].unsqueeze(3).to_broadcast([P, PH, NT, TOPK]), ALU.mult).then_inc(s_g, 1)

        @block.tensor
        def _(pe):
            for n in range(EARLY_ROUTING):
                if n < HC:
                    pe.wait_ge(s_wlo, n + 1)
                    if n >= 2:
                        pe.wait_ge(s_qsb, n - 1)
                    for k in range(KD):
                        for a, b in ((w_hi, h2hi), (w_hi, h2lo), (w_lo, h2hi)):
                            last = pe.matmul(psum[:, n % 2, :], a[:, n % 2, k, :], b[:, k, :],
                                             start=(k == 0 and a is w_hi and b is h2hi), stop=(k == KD - 1 and a is w_lo))
                    last.then_inc(s_q, 1)
                if 1 <= n <= HC:
                    m = n - 1
                    pe.wait_ge(s_in, 32)
                    pe.wait_ge(s_qsb, n)
                    if m >= 2:
                        pe.wait_ge(s_ssb, m - 1)
                    for t in range(NT):
                        last = pe.matmul(psum[:, 2 + m % 2, t * P:(t + 1) * P], query[:, m % 2, t * P:(t + 1) * P],
                                         keysT[:, m, :], start=True, stop=True)
                    last.then_inc(s_s, 1)
                pe.wait_ge(s_ulo, n + 1)
                if n >= 2:
                    pe.wait_ge(s_gel, n - 1)
                for k in range(KD):
                    for a, b in ((u_hi, h2hi), (u_hi, h2lo), (u_lo, h2hi)):
                        last = pe.matmul(psum[:, 6 + n % 2, :], a[:, n % 2, k, :], b[:, k, :],
                                         start=(k == 0 and a is u_hi and b is h2hi), stop=(k == KD - 1 and a is u_lo))
                last.then_inc(s_act, 1)
            pe.wait_ge(s_red, 2 * PH)
            for j in range(3):
                if j == 2:
                    pe.wait_ge(s_g, 3)
                for t in range(NT):
                    last = pe.transpose(psum[:, CHOSEN_BANKS[j], t * P:(t + 1) * P],
                                        found[:, j, t, :, :].rearrange("p h s -> p (h s)"), ident[:])
                last.then_inc(s_turn, 1)


def build_gates(nc, dram, keep, psum):
    BATCH, BATCHES = 16, 2 * CHUNK // 16
    QUADS = BATCH // 4
    HALF = BATCHES // 2
    ITERS = T // (2 * CHUNK)
    PER = BATCHES // 2
    assert EARLY_GATES == PER * ITERS and PER == USLOTS
    with ExitStack() as ctx:
        def sb(name, shape, dt=F32):
            return ctx.enter_context(nc.sbuf_tensor(name, shape, dt))

        def sem(name):
            return ctx.enter_context(nc.semaphore(name))

        chosen, gates, acts, h2hi, h2lo = keep["chosen"], keep["gates"], keep["acts"], keep["h2hi"], keep["h2lo"]
        iota = sb("iota4", [P, P])
        hot_j = sb("hot_j", [P, 2, BATCH, P])
        hot_i = sb("hot_i", [P, 2, BATCH, P])
        chunk = sb("chunk", [P, 2, P, CHUNK])
        u_raw = sb("u_raw4", [P, USLOTS, KD, P])
        u_hi = sb("u_hi4", [P, 2, KD, P], F32R)
        u_lo = sb("u_lo4", [P, 2, KD, P], F32R)
        gel = sb("gel4", [P, 2, T])
        s_in, s_hot_i, s_gated, s_hot_j = sem("iota_in"), sem("hot_i_r"), sem("gated_r"), sem("hot_j_r")
        s_prod, s_moved = sem("gate_prod"), sem("gate_moved")
        s_st = keep["gates_out"]
        s_u = [sem(f"u4_in{i}") for i in range(USLOTS)]
        s_uhi, s_ulo, s_act, s_gel = sem("u4_hi_r"), sem("u4_lo_r"), sem("act4_pe"), sem("gel4_r")
        s_ast = [sem("acts4_out0"), sem("acts4_out1")]
        block = ctx.enter_context(nc.Block())

        def wait(eng, s, value):
            if not (isinstance(value, int) and value <= 0):
                eng.wait_ge(s, value)

        def over_chunks(eng, body):
            body(0)
            with eng.Fori(1, ITERS) as it:
                body(it)

        @block.sync
        def _(sp):
            def load(first, e):
                m = first + e
                wait(sp, s_ulo, m - USLOTS + 1)
                tile = bass.ds(2 * GROUP + EARLY_ROUTING + m, 1)
                sp.dma_start(u_raw[:, e % USLOTS, :, :],
                             dram["peer_u"][tile, :, :, :].rearrange("a p k j -> p (a k) j")).then_inc(s_u[e % USLOTS], 16)

            def store(first, e):
                m = first + e
                wait(sp, s_gel, m + 1)
                tile = bass.ds(EARLY_ROUTING + m, 1)
                sp.dma_start(acts[tile, :, :].rearrange("a j t -> j (a t)"), gel[:, e % 2, :]).then_inc(s_ast[e % 2], 16)

            sp.dma_start(iota[:], dram["iota"]).then_inc(s_in, 16)
            for e in range(USLOTS):
                load(0, e)

            with sp.Fori(0, ITERS - 1) as it:
                for e in range(PER):
                    store(it * PER, e)
                    load(it * PER + USLOTS, e)
            for e in range(PER):
                store(EARLY_GATES - PER, e)
            for i in range(2):
                sp.wait_ge(s_ast[i], 16 * (EARLY_GATES // 2))

        @block.vector
        def _(dve):
            def one_hots(eng_it, b):
                batch = eng_it * BATCHES + b
                wait(dve, s_prod, (batch - 1) * QUADS)
                tokens = bass.ds(batch * BATCH, BATCH)
                for hot, row, ready in ((hot_i, 0, s_hot_i), (hot_j, 1, s_hot_j)):
                    dve.tensor_tensor(hot[:, b % 2, :, :], iota[:].unsqueeze(1).to_broadcast([P, BATCH, P]),
                                      chosen[:, row, tokens].unsqueeze(2).to_broadcast([P, BATCH, P]),
                                      ALU.is_equal).then_inc(ready, 1)

            def rest_u(first, e):
                m = first + e
                wait(dve, s_act, m - 1)
                dve.wait_ge(s_uhi, m + 1)
                dve.tensor_tensor(u_lo[:, e % 2, :, :], u_raw[:, e % USLOTS, :, :], u_hi[:, e % 2, :, :].bitcast(F32),
                                  ALU.subtract).then_inc(s_ulo, 1)

            def body(it):
                for b in range(BATCHES):
                    one_hots(it, b)
                    if b % 2:
                        rest_u(it * PER, b // 2)

            dve.wait_ge(s_in, 16)
            over_chunks(dve, body)

        @block.gpsimd
        def _(pool):
            with pool.Fori(0, ITERS) as it:
                for b in range(BATCHES):
                    batch = it * BATCHES + b
                    pool.wait_ge(s_hot_i, batch + 1)
                    pool.tensor_tensor(hot_i[:, b % 2, :, :], hot_i[:, b % 2, :, :],
                                       chosen[:, 2, bass.ds(batch * BATCH, BATCH)].unsqueeze(2).to_broadcast([P, BATCH, P]),
                                       ALU.mult).then_inc(s_gated, 1)

        @block.tensor
        def _(pe):
            def activations(first, e):
                m = first + e
                pe.wait_ge(s_ulo, m + 1)
                wait(pe, s_gel, m - 1)
                for k in range(KD):
                    for a, b in ((u_hi, h2hi), (u_hi, h2lo), (u_lo, h2hi)):
                        last = pe.matmul(psum[:, 6 + e % 2, :], a[:, e % 2, k, :], b[:, k, :],
                                         start=(k == 0 and a is u_hi and b is h2hi), stop=(k == KD - 1 and a is u_lo))
                last.then_inc(s_act, 1)

            def body(it):
                for b in range(BATCHES):
                    batch = it * BATCHES + b
                    pe.wait_ge(s_gated, batch + 1)
                    pe.wait_ge(s_hot_j, batch + 1)
                    for q in range(QUADS):
                        wait(pe, s_moved, (batch - 1) * QUADS + q + 1)
                        for s in range(4):
                            last = pe.matmul(psum[:, q, s * P:(s + 1) * P], hot_j[:, b % 2, q * 4 + s, :],
                                             hot_i[:, b % 2, q * 4 + s, :], start=True, stop=True)
                        last.then_inc(s_prod, 1)
                    if b % 2:
                        activations(it * PER, b // 2)

            over_chunks(pe, body)

        @block.scalar
        def _(act):
            def split_u(turn, e):
                m = turn * USLOTS + e
                act.wait_ge(s_u[e % USLOTS], 16 * (turn + e // USLOTS + 1))
                wait(act, s_act, m - 1)
                act.copy(u_hi[:, e % 2, :, :], u_raw[:, e % USLOTS, :, :]).then_inc(s_uhi, 1)

            def gelu(turn, e):
                m = turn * USLOTS + e
                act.wait_ge(s_act, m + 1)
                wait(act, s_ast[e % 2], (turn * (USLOTS // 2) + e // 2) * 16)
                act.activation(gel[:, e % 2, :], psum[:, 6 + e % 2, :], ACT.Gelu).then_inc(s_gel, 1)

            def body(it, more=True):
                for b in range(BATCHES):
                    batch, half = it * BATCHES + b, b // HALF
                    if b % HALF == 0:
                        wait(act, s_st[half], it * 16)
                    for q in range(QUADS):
                        act.wait_ge(s_prod, batch * QUADS + q + 1)
                        start = (b % HALF) * BATCH + q * 4
                        act.copy(chunk[:, half, :, start:start + 4],
                                 psum[:, q, :].rearrange("p (s i) -> p i s", s=4)).then_inc(s_moved, 1)
                    if b % 2:
                        e = b // 2
                        if e:
                            gelu(it, e - 1)
                        elif not (isinstance(it, int) and it == 0):
                            gelu(it - 1, USLOTS - 1)
                        if e + 1 < PER:
                            split_u(it, e + 1)
                        elif more:
                            split_u(it + 1, 0)
                    if b % HALF == HALF - 1:
                        act.wait_ge(s_moved, (batch + 1) * QUADS)
                        act.dma_start(gates[bass.ds(it * 2 + half, 1), :, :, :].rearrange("c j i t -> j (c i) t"),
                                      chunk[:, half, :, :]).then_inc(s_st[half], 16)

            split_u(0, 0)
            body(0)
            with act.Fori(1, ITERS - 1) as it:
                body(it)
            body(ITERS - 1, more=False)
            gelu(ITERS - 1, USLOTS - 1)


def build_experts(nc, dram, keep, psum):
    TILES, E = NKEYS, GROUP
    GROUPS = TILES // E
    PAIRS, EARLY_PAIRS = GROUPS // 2, EARLY // (2 * E)
    UR, VR, GR, SR = 4, 2, 4, 4
    with ExitStack() as ctx:
        def sb(name, shape, dt=F32):
            return ctx.enter_context(nc.sbuf_tensor(name, shape, dt))

        def sem(name):
            return ctx.enter_context(nc.semaphore(name))

        x_sb, h2hi, h2lo, gates, acts = keep["x"], keep["h2hi"], keep["h2lo"], keep["gates"], keep["acts"]
        s_gates = keep["gates_out"]
        u_raw = sb("u_raw", [P, UR, KD, P])
        u_hi = sb("u_hi", [P, 2, KD, P], F32R)
        u_lo = sb("u_lo", [P, 2, KD, P], F32R)
        gel = sb("gel", [P, 2, T])
        eps = sb("eps4", [P, 1])
        v_raw = sb("v_raw", [P, VR, D])
        g_sb = sb("g_sb", [P, GR, T])
        v_hi = sb("v_hi", [P, 2 * E, D], F32R)
        v_lo = sb("v_lo", [P, 2 * E, D], F32R)
        wgt = sb("wgt", [P, 2, T])
        w_hi = sb("w_hi", [P, 2 * E, T], F32R)
        w_lo = sb("w_lo", [P, 2 * E, T], F32R)
        fgain = v_raw[:, 0, :]
        ss = sb("ss4", [P, NT])
        std = sb("std4", [P, NT])
        rstd = sb("rstd4", [P, NT])

        s_u = [sem(f"u_in{i}") for i in range(UR)]
        s_v = [sem(f"v_in{i}") for i in range(VR)]
        s_g = [sem(f"g_in{i}") for i in range(GR)]
        s_uhi, s_ulo, s_vhi, s_vlo = sem("u_hi_r"), sem("u_lo_r"), sem("v_hi_r"), sem("v_lo_r")
        s_act, s_gel, s_wgt, s_whi, s_wlo = sem("act_pe"), sem("gel_r"), sem("wgt_r"), sem("w_hi_r"), sem("w_lo_r")
        s_outp, s_acc = sem("out_pe"), sem("acc_r")
        s_fg, s_sq, s_std, s_rstd, s_fin, s_store = (sem("fgain_in"), sem("sumsq4"), sem("std4_r"), sem("rstd4_r"),
                                                     sem("final_r"), sem("stored"))
        block = ctx.enter_context(nc.Block())

        def wait(eng, s, value):
            if not (isinstance(value, int) and value <= 0):
                eng.wait_ge(s, value)

        def over_pairs(eng, body):
            body(0, "first")
            with eng.Fori(1, 1 + EARLY_PAIRS) as it:
                body(it * 2, "early")
            body((1 + EARLY_PAIRS) * 2, "again")
            with eng.Fori(2 + EARLY_PAIRS, PAIRS - 1) as it:
                body(it * 2, "own")
            body((PAIRS - 1) * 2, "last")

        def own(g, e, kind):
            return g * E + e - (0 if kind == "first" else EARLY)

        @block.sync
        def _(sp):
            def load_u(g, e, kind):
                n = g * E + e
                tile = bass.ds(n, 1)
                wait(sp, s_wgt, n - UR + 1)
                if kind == "early":
                    sp.dma_start(u_raw[:, e % UR, 0:T // P, :],
                                 acts[bass.ds(n - 2 * E, 1), :, :].rearrange("a j (b c) -> j (a b) c", c=P)).then_inc(s_u[e % UR], 16)
                else:
                    sp.dma_start(u_raw[:, e % UR, :, :],
                                 dram["peer_u"][tile, :, :, :].rearrange("a p k j -> p (a k) j")).then_inc(s_u[e % UR], 16)

            def load_g(g, e):
                n = g * E + e
                wait(sp, s_wgt, n - GR + 1)
                sp.dma_start(g_sb[:, e % GR, :].rearrange("p (c t) -> p c t", t=CHUNK),
                             gates[:, :, bass.ds(n, 1), :].rearrange("c j a t -> j c (a t)")).then_inc(s_g[e % GR], 16)

            def loads(g, kind):
                ahead = UR if kind == "first" else 0
                for e in range(ahead):
                    load_u(g, e, kind)
                if kind == "first":
                    for s in s_gates:
                        sp.wait_ge(s, 16 * (T // (2 * CHUNK)))
                for e in range(2 * E):
                    if e >= ahead:
                        load_u(g, e, kind)
                    load_g(g, e)

            over_pairs(sp, loads)
            sp.wait_ge(s_vlo, TILES)
            sp.dma_start(fgain, dram["final_norm_g"].to_broadcast([P, D])).then_inc(s_fg, 16)
            for i in range(NT):
                sp.wait_ge(s_fin, 2 * i + 2)
                sp.dma_start(dram["out"][i * P:(i + 1) * P, :], x_sb[:, i, :]).then_inc(s_store, 16)
            sp.wait_ge(s_store, 16 * NT)

        @block.gpsimd
        def _(pool):
            for s in s_gates:
                pool.wait_ge(s, 16 * (T // (2 * CHUNK)))
            for n in range(VR):
                pool.dma_start(v_raw[:, n, :], dram["peer_v"][n]).then_inc(s_v[n], 16)
            with pool.Fori(1, TILES // VR) as it:
                for e in range(VR):
                    n = it * VR + e
                    pool.wait_ge(s_vlo, n - VR + 1)
                    pool.dma_start(v_raw[:, e, :], dram["peer_v"][bass.ds(n, 1), :, :].rearrange("a j d -> j (a d)")).then_inc(s_v[e], 16)

        def arrived(eng, sems, g, e, slots):
            eng.wait_ge(sems[e % slots], (g * (E // slots) + e // slots + 1) * 16)

        def look_ahead(split, g, e, kind):
            if e < 2 * E - 2:
                split(g, e + 2, kind)
            elif kind in ("again", "own"):
                split(g + 2, e + 2 - 2 * E, kind)

        @block.scalar
        def _(act):
            def split_u(g, e, kind):
                arrived(act, s_u, g, e, UR)
                wait(act, s_act, own(g, e, kind) - 1)
                act.copy(u_hi[:, e % 2, :, :], u_raw[:, e % UR, :, :]).then_inc(s_uhi, 1)

            def body(g, kind):
                if kind in ("first", "again"):
                    split_u(g, 0, kind)
                    split_u(g, 1, kind)
                for half in range(2):
                    for e in range(half * E, half * E + E):
                        n = g * E + e
                        if kind != "early":
                            act.wait_ge(s_act, own(g, e, kind) + 1)
                            look_ahead(split_u, g, e, kind)
                            wait(act, s_wgt, n - 1)
                            act.activation(gel[:, e % 2, :], psum[:, e % SR, :], ACT.Gelu).then_inc(s_gel, 1)
                        act.wait_ge(s_wgt, n + 1)
                        wait(act, s_outp, (g + half - 1) * 8)
                        act.copy(w_hi[:, e, :], wgt[:, e % 2, :]).then_inc(s_whi, 1)
                    for e in range(half * E, half * E + E):
                        arrived(act, s_v, g, e, VR)
                        act.copy(v_hi[:, e, :], v_raw[:, e % VR, :]).then_inc(s_vhi, 1)

            over_pairs(act, body)
            for i in range(NT):
                act.wait_ge(s_acc, GROUPS * 8 - (8 - 2 * (i + 1)))
                act.activation(gel[:].rearrange("p a t -> p (a t)"), x_sb[:, i, :], ACT.Square, accum_out=ss[:, i:i + 1]).then_inc(s_sq, 1)
                act.wait_ge(s_sq, i + 1)
                if i == 0:
                    act.wait_ge(s_rstd, 1)
                act.activation(std[:, i:i + 1], ss[:, i:i + 1], ACT.Sqrt, bias=eps[:, 0:1], scale=1.0 / D).then_inc(s_std, 1)

        @block.vector
        def _(dve):
            dve.memset(eps[:], EPS).then_inc(s_rstd, 1)

            def rest_u(g, e, kind):
                dve.wait_ge(s_uhi, own(g, e, kind) + 1)
                dve.tensor_tensor(u_lo[:, e % 2, :, :], u_raw[:, e % UR, :, :], u_hi[:, e % 2, :, :].bitcast(F32),
                                  ALU.subtract).then_inc(s_ulo, 1)

            def rest_v(g, e):
                dve.wait_ge(s_vhi, g * E + e + 1)
                dve.tensor_tensor(v_lo[:, e, :], v_raw[:, e % VR, :], v_hi[:, e, :].bitcast(F32), ALU.subtract).then_inc(s_vlo, 1)

            def accumulate(g, m):
                dve.wait_ge(s_outp, g * 8 + m + 1)
                dst = x_sb[:, m // 2, (m % 2) * BANK:(m % 2 + 1) * BANK]
                dve.tensor_tensor(dst, psum[:, SR + m % 4, :], dst, ALU.add).then_inc(s_acc, 1)

            def body(g, kind):
                if kind in ("first", "again"):
                    rest_u(g, 0, kind)
                    rest_u(g, 1, kind)
                for half in range(2):
                    for e in range(half * E, half * E + E):
                        n = g * E + e
                        if kind == "early":
                            arrived(dve, s_u, g, e, UR)
                            activated = u_raw[:, e % UR, 0:T // P, :].rearrange("p a b -> p (a b)")
                        else:
                            look_ahead(rest_u, g, e, kind)
                            dve.wait_ge(s_gel, own(g, e, kind) + 1)
                            activated = gel[:, e % 2, :]
                        arrived(dve, s_g, g, e, GR)
                        wait(dve, s_wlo, n - 1)
                        dve.tensor_tensor(wgt[:, e % 2, :], activated, g_sb[:, e % GR, :], ALU.mult).then_inc(s_wgt, 1)
                        dve.wait_ge(s_whi, n + 1)
                        dve.tensor_tensor(w_lo[:, e, :], wgt[:, e % 2, :], w_hi[:, e, :].bitcast(F32), ALU.subtract).then_inc(s_wlo, 1)
                    for m in range(8):
                        if m % 2 == 0:
                            rest_v(g, half * E + m // 2)
                        if not (kind == "first" and half == 0):
                            accumulate(g + half - 1, m)

            over_pairs(dve, body)
            for m in range(8):
                accumulate(GROUPS - 1, m)
            dve.wait_ge(s_fg, 16)
            for i in range(NT):
                dve.wait_ge(s_std, i + 1)
                dve.reciprocal(rstd[:, i:i + 1], std[:, i:i + 1]).then_inc(s_rstd, 1)
                dve.wait_ge(s_rstd, i + 2)
                dve.wait_ge(s_acc, GROUPS * 8)
                for half in range(2):
                    c = slice(half * BANK, (half + 1) * BANK)
                    dve.scalar_tensor_tensor(x_sb[:, i, c], x_sb[:, i, c], rstd[:, i:i + 1], fgain[:, c],
                                             ALU.mult, ALU.mult).then_inc(s_fin, 1)

        @block.tensor
        def _(pe):
            def activations(g, e, kind):
                pe.wait_ge(s_ulo, own(g, e, kind) + 1)
                wait(pe, s_gel, own(g, e, kind) - SR + 1)
                for k in range(KD):
                    for a, b in ((u_hi, h2hi), (u_hi, h2lo), (u_lo, h2hi)):
                        last = pe.matmul(psum[:, e % SR, :], a[:, e % 2, k, :], b[:, k, :],
                                         start=(k == 0 and a is u_hi and b is h2hi), stop=(k == KD - 1 and a is u_lo))
                last.then_inc(s_act, 1)

            def outputs(g, half):
                pe.wait_ge(s_wlo, (g + 1) * E)
                pe.wait_ge(s_vlo, (g + 1) * E)
                for m in range(8):
                    t, c = slice((m // 2) * P, (m // 2 + 1) * P), slice((m % 2) * BANK, (m % 2 + 1) * BANK)
                    wait(pe, s_acc, g * 8 + m - 3)
                    for e in range(half * E, half * E + E):
                        for a, b in ((w_hi, v_hi), (w_hi, v_lo), (w_lo, v_hi)):
                            last = pe.matmul(psum[:, SR + m % 4, :], a[:, e, t], b[:, e, c],
                                             start=(e == half * E and a is w_hi and b is v_hi),
                                             stop=(e == half * E + E - 1 and a is w_lo))
                    last.then_inc(s_outp, 1)

            def body(g, kind):
                for half in range(2):
                    if kind != "early":
                        for e in range(E):
                            activations(g, half * E + e, kind)
                    if not (kind == "first" and half == 0):
                        outputs(g + half - 1, 1 - half)

            over_pairs(pe, body)
            outputs(GROUPS - 1, 1)


def _level_masks():
    s, t = np.arange(P)[:, None], np.arange(P)[None, :]
    out = np.zeros((P, LEVELS + 1, P), np.float32)
    for lv in range(LEVELS):
        h = 64 >> lv
        out[:, lv] = (s // (2 * h) == t // (2 * h)) & (s // h != t // h)
    out[:, LEVELS] = s == t
    return out


def _window_masks():
    out = np.full((P, NT, 3, P), MASKED, np.float32)
    q = np.arange(P)
    for g in range(NT):
        cq = g * WIN + q // ROWS
        c0 = np.clip(cq - WIN // 2, 0, GRID_W - WIN)
        for j in range(3):
            ck = (g - 1 + j) * WIN + np.arange(P) // ROWS
            inside = (ck[None, :] >= c0[:, None]) & (ck[None, :] < c0[:, None] + WIN)
            out[:, g, j][inside] = 0.0
    return out


def _pairwise_rpb(rpb):
    pad = np.pad(rpb, ((0, 0), (0, 0), (WIN, WIN))).transpose(0, 2, 1)
    return np.stack([pad[:, :, ROWS - 1 - r:2 * ROWS - 1 - r] for r in range(ROWS)]).reshape(ROWS, NA_HEADS, -1)


def _tiles(w):
    return w.reshape(KD, P, -1, P).transpose(2, 1, 0, 3)


def _columns(g):
    return g.reshape(-1, P).T


def build(nc, dram):
    gates = nc.dram_tensor("gates", [T // CHUNK, NKEYS, NKEYS, CHUNK], F32).ap()
    acts = nc.dram_tensor("acts", [EARLY, NKEYS, T], F32).ap()
    with ExitStack() as ctx:
        def sb(where, name, shape, dt=F32, side=None):
            return where.enter_context(nc.sbuf_tensor(name, shape, dt, side=side))

        psum = ctx.enter_context(nc.psum_tensor("psum", [P, BANKS, BANK], F32))
        keep = {"gates": gates, "acts": acts, "ident": sb(ctx, "ident", [P, P]), "x": sb(ctx, "x_sb", [P, NT, D])}
        keep["gates_out"] = [ctx.enter_context(nc.semaphore(f"gates_out{i}")) for i in range(2)]
        with ExitStack() as mixing:
            keep["hg_out"] = sb(mixing, "hg_out", [P, HPS, T])
            keep["naq"] = sb(mixing, "naq", [P, 4, T])
            keep["nak"] = sb(mixing, "nak", [P, 4, T])
            keep["nav"] = sb(mixing, "nav", [P, NT, NA_HEADS * HD])
            keep["mq"] = sb(mixing, "mq", [P, 2, T])
            keep["mk"] = sb(mixing, "mk", [P, 2, MEM])
            keep["mv"] = sb(mixing, "mv", [P, MT, MEM_HEADS * HD])
            build_mix(nc, dram, keep, psum)
            keep["h2hi"] = sb(ctx, "h2hi", [P, KD, T], F32R, side="right")
            keep["h2lo"] = sb(ctx, "h2lo", [P, KD, T], F32R, side="right")
            build_attention(nc, dram, keep, psum)
        with ExitStack() as routed:
            keep["chosen"] = sb(routed, "chosen", [P, 3, T])
            build_routing(nc, dram, keep, psum)
            build_gates(nc, dram, keep, psum)
        build_experts(nc, dram, keep, psum)


def kernel(x, mem, attn_norm_g, w_in, na_rpb, hg_lower_bound, hg_out_norm_g, mem_norm_g, w_mem_kv, w_out,
           ffn_norm_g, peer_w_query, peer_sub_keys, peer_u, peer_v, final_norm_g):
    import concourse.bacc as bacc
    from concourse.bass_utils import run_bass_kernel_spmd

    head_mean = np.zeros((P, P), np.float32)
    for s in range(2):
        head_mean[s * HD:(s + 1) * HD, s * HD:(s + 1) * HD] = 1.0 / HD
    a = np.asarray
    arrays = {
        "x": a(x)[0], "mem": a(mem)[0],
        "w_in": _tiles(a(w_in)[0]), "w_kv": _tiles(a(w_mem_kv)[0]), "w_query": _tiles(a(peer_w_query)[0]),
        "attn_norm_g": _columns(a(attn_norm_g)[0]), "mem_norm_g": _columns(a(mem_norm_g)[0]),
        "ffn_norm_g": _columns(a(ffn_norm_g)[0]), "hg_out_norm_g": _columns(a(hg_out_norm_g)[0]),
        "hg_lower_bound": a(hg_lower_bound).reshape(2, 2, HPS, P).transpose(3, 0, 2, 1),
        "na_rpb": _pairwise_rpb(a(na_rpb)[0]), "w_out": a(w_out)[0],
        "sub_keys": a(peer_sub_keys)[0].reshape(2 * PH, NKEYS, P).transpose(2, 0, 1),
        "peer_u": a(peer_u)[0].reshape(NKEYS, NKEYS, KD, P).transpose(0, 3, 2, 1),
        "peer_v": a(peer_v)[0].reshape(NKEYS, NKEYS, D), "final_norm_g": a(final_norm_g).reshape(1, D),
        "ident": np.eye(P, dtype=np.float32), "head_mean": head_mean, "level_masks": _level_masks(),
        "window_masks": _window_masks().reshape(P, NT, 3 * P),
        "iota": np.broadcast_to(np.arange(P, dtype=np.float32), (P, P)),
    }
    arrays = {f"in_{k}": np.ascontiguousarray(v) for k, v in arrays.items()}
    nc = bacc.Bacc("TRN2", target_bir_lowering=False, num_devices=1)
    dram = {k[3:]: nc.dram_tensor(k, v.shape, F32, kind="ExternalInput").ap() for k, v in arrays.items()}
    dram["out"] = nc.dram_tensor("out", (T, D), F32, kind="ExternalOutput").ap()
    build(nc, dram)
    r = run_bass_kernel_spmd(nc, [arrays], core_ids=[0])
    return r.results[0]["out"].reshape(1, T, D)
```

```python
from contextlib import ExitStack

import numpy as np

import concourse.bass as bass
from concourse import mybir

F32 = mybir.dt.float32
F32R = mybir.dt.float32r
U32 = mybir.dt.uint32
ALU = mybir.AluOpType
ACT = mybir.ActivationFunctionType
AX = mybir.AxisListType

P = 128
T, D, MEM = 512, 1024, 256
NT, KD, MT = T // P, D // P, MEM // P
EPS = 1e-6
GRID_W = 64
ROWS = T // GRID_W
NA_HEADS, MEM_HEADS, HG_HEADS, HD = 8, 4, 4, 64
WIN = 16
MAXK = 3 * P
RING_SLOTS = 4
FILL_FIRST = 3
SCALE = float(HD) ** -0.5
CT_NAQ, CT_NAK, CT_NAV, CT_HGQ, CT_FF, CT_FB, CT_I, CT_G, CT_MQ = 0, 4, 8, 12, 14, 16, 18, 20, 22
LEVELS = 7
HPS = 2
PH, NKEYS, TOPK = 8, 128, 16
NEG = -3.0e38
MASKED = -1.0e30
BANKS = 8
BANK = 512
EARLY_ROUTING, EARLY_GATES = 24, 16
EARLY = EARLY_ROUTING + EARLY_GATES
GROUP = 4
USLOTS = 4
CHUNK = 64
CHOSEN_BANKS = (4, 5, 0)
PICK_LAG = 6


class Tally:

    def __init__(self, sem):
        self.sem, self.n = sem, 0

    def inc(self, ins):
        ins.then_inc(self.sem, 1)
        self.n += 1
        return self.n


def key_tiles(g):
    return list(range(max(0, g - 1), min(NT, g + 2)))


def mix_jobs():
    jobs = [("hT", k, 0, "dve") for k in range(KD)]
    jobs += [("mT", k, 0, "act" if k % 2 else "dve") for k in range(KD)]
    jobs += [("e", d, hp, "act") for d in range(2) for hp in range(HPS)]
    for j in range(2):
        jobs += [("iz", j, 0, "act"), ("q", j, 0, "act"), ("iT", j, 0, "act")]
    rest = [("mk", 0, 0, "act"), ("mv", 0, 0, "act")] + [("mq", j, 0, "act") for j in range(2)]
    rest += [("naq", j, 0, "act") for j in range(4)] + [("nak", j, 0, "act") for j in range(4)]
    rest += [("nav", j, 0, "act") for j in range(4)] + [("g", j, 0, "act") for j in range(2)]
    steps = []
    for hp in range(HPS):
        for lv in range(LEVELS + 1):
            steps.append([("lev", lv, 2 * hp + s, "dve") for s in range(2)])
        for s in range(2):
            steps.append([("x", 2 * hp + s, m, "act") for m in range(NT)])
        steps[-1].append(("o", hp, 0, "dve"))
    jobs += rest[:FILL_FIRST]
    rest = rest[FILL_FIRST:]
    for st in steps:
        jobs += st
        if jobs[-1][0] == "nav" or jobs[-1 - len(st)][0] == "nav":
            jobs.append(("navT", jobs[-1 - len(st)][1], 0, "act"))
        if rest:
            jobs.append(rest.pop(0))
    assert not rest
    jobs.insert(jobs.index(("x", 2 * HPS - 1, 0, "act")), ("ms", 0, 0, "act"))
    jobs.append(("ms", 1, 0, "act"))
    return jobs


def evac_counts(jobs):
    count, out = {"act": 0, "dve": 0}, {}
    for n, job in enumerate(jobs):
        count[job[3]] += 1
        out[n] = (job[3], count[job[3]])
    return out


def weight_order():
    order = []
    for job in mix_jobs():
        kind, a, b, _ = job
        if kind == "e":
            order.append(("z", (CT_FF, CT_FB)[a] + b))
        elif kind == "q":
            order.append(("z", CT_HGQ + a))
        elif kind == "iz":
            order.append(("z", CT_I + a))
        elif kind == "mk":
            order += [("kv", 0), ("kv", 1)]
        elif kind == "mv":
            order += [("kv", 2), ("kv", 3)]
        elif kind == "mq":
            order.append(("z", CT_MQ + a))
        elif kind == "naq":
            order.append(("z", CT_NAQ + a))
        elif kind == "nak":
            order.append(("z", CT_NAK + a))
        elif kind == "nav":
            order.append(("z", CT_NAV + a))
        elif kind == "g":
            order.append(("z", CT_G + a))
    return order


def bias_table(keep):
    return keep["ring"][:, 0:NA_HEADS * MAXK].rearrange("p (h k) -> p h k", h=NA_HEADS)


def build_mix(nc, dram, keep, psum):
    jobs = mix_jobs()
    at = {job[:3]: n for n, job in enumerate(jobs)}
    emptied = evac_counts(jobs)
    weights = weight_order()
    WSLOTS = RING_SLOTS
    HALVES = 3
    RING = 4
    AHEAD = 2
    INTER_AT = 2
    with ExitStack() as ctx:
        def sb(name, shape, dt=F32):
            return ctx.enter_context(nc.sbuf_tensor(name, shape, dt))

        def sem(name):
            return ctx.enter_context(nc.semaphore(name))

        ident, hg_out = keep["ident"], keep["hg_out"]
        naq, nak, nav = keep["naq"], keep["nak"], keep["nav"]
        mq, mk, mv = keep["mq"], keep["mk"], keep["mv"]
        xn = sb("xn", [P, NT, D])
        mem_sb = sb("mem_sb", [P, MT, D])
        h_hi = sb("h_hi", [P, KD, T], F32R)
        h_lo = sb("h_lo", [P, KD, T], F32R)
        mT = sb("mT", [P, KD, MEM])
        wring = keep["ring"][:].rearrange("p (s k c) -> p s k c", s=WSLOTS, k=KD)
        w_hi = sb("w_hi1", [P, HALVES, KD // 2, P], F32R)
        w_lo = sb("w_lo1", [P, HALVES, KD // 2, P], F32R)
        gain_a = sb("gain_a", [P, KD])
        gain_m = sb("gain_m", [P, KD])
        gain_o = sb("gain_o", [P, HPS])
        bound = sb("bound", [P, 2, HPS, 2])
        lb = sb("lb", [P, 2, HPS])
        lb1 = sb("lb1", [P, 2, HPS])
        lbt = sb("lbt", [P, 2, HPS])
        nvT = sb("nvT", [P, T])
        masks = sb("masks", [P, LEVELS + 1, P])
        halves = sb("halves", [P, P])
        ss = sb("ss", [P, NT + MT])
        std = sb("std", [P, NT + MT])
        rstd = sb("rstd", [P, NT + MT])
        eps = sb("eps", [P, 1])
        q = sb("hgq", [P, HPS, T])
        kk = sb("hgk", [P, 2, HPS, T])
        v = sb("hgv", [P, NT, HG_HEADS * HD])
        arr = sb("arr", [P, 2, HPS, NT, P + 1])
        ebt = sb("ebt", [P, 2, HPS, NT])
        inter = sb("inter", [P, HPS, 4, T])
        ext = sb("ext", [P, 6, P])
        dec = sb("dec", [P, 2, 2, T])
        qk = xn[:].rearrange("p r (s t) -> p r s t", s=2)
        lf = inter[:, 0, :, :].rearrange("p (d h) t -> p d h t", d=2)
        m_flat = mT[:].rearrange("p k m -> p (k m)")
        gz = m_flat[:, 0:2 * T].rearrange("p (h t) -> p h t", h=HPS)
        tmp = m_flat[:, 2 * T:4 * T].rearrange("p (h t) -> p h t", h=2)
        Am = sb("Am", [P, 2, NT * (T + P)])
        oT = mem_sb[:, 0, :].rearrange("p (h t) -> p h t", h=HPS)
        osq = mem_sb[:, 1, :].rearrange("p (h t) -> p h t", h=HPS)
        squares = inter[:].rearrange("p h c (a t) -> p (h c a) t", a=1).rearrange("p (n b) t -> p n (b t)", b=2)
        ksum = hg_out
        orst = tmp
        sil = keep["ring"][:, 3 * D:3 * D + HPS * T].rearrange("p (h t) -> p h t", h=HPS)
        QF, KF, QB, KB = range(4)

        s_const, s_mem, s_bias = sem("const_in"), sem("mem_in"), sem("bias_in")
        s_x = [sem(f"x_in{i}") for i in range(NT)]
        s_late = sem("late_const_in")
        s_w = [sem(f"w_in{i}") for i in range(WSLOTS)]
        s_sq, s_std, s_rstd, s_xn = sem("sumsq"), sem("std"), sem("rstd"), sem("xn_ready")
        pe_done, act_ev, dve_ev = sem("pe_done"), sem("act_emptied"), sem("dve_emptied")
        s_lb, s_gate, s_lf, s_k, s_scan, s_ksum = (sem("lb"), sem("gate"), sem("logf"), sem("k_ready"),
                                                   sem("scan"), sem("ksum"))
        s_dec, s_exp, s_qk = sem("decay_in"), sem("decay_exp"), sem("qk_ready")
        s_ebt, s_idec, s_iexp, s_inter, s_ext = (sem("ebt"), sem("inter_in"), sem("inter_exp"),
                                                 sem("inter_ready"), sem("ext_ready"))
        s_diag, s_osq, s_sil, s_fin = sem("diag"), sem("osq"), sem("sil"), sem("hg_fin")
        ev = {"act": act_ev, "dve": dve_ev}
        s_hhi, s_whi, s_wlo, s_half = sem("h_hi_r"), sem("w_hi_r"), sem("w_lo_r"), sem("half_used")
        block = ctx.enter_context(nc.Block())

        def bank(n):
            return psum[:, n % BANKS, :]

        def await_emptied(eng, key):
            who, count = emptied[at[key]]
            eng.wait_ge(ev[who], count)

        def level_step(hp, lv):
            return hp * LEVELS + lv

        def prepare(stage, hp, lv):
            s = level_step(hp, lv) + AHEAD
            if lv < LEVELS and s < HPS * LEVELS:
                stage(*divmod(s, LEVELS))

        def halves_of(ap, lv):
            h = 64 >> lv
            return ap.rearrange("p n (b s j) -> p n b s j", s=2, j=h)

        def mid_of(d, hp, lv):
            h = 64 >> lv
            m = arr[:, d, hp, :, h:P + 1:2 * h]
            return m.unsqueeze(3).to_broadcast([P, NT, P // (2 * h), h])

        z_jobs = [job[:3] for job in jobs if job[0] in ("e", "q", "iz", "mq", "naq", "nak", "nav", "g")]
        z_slot = [n for n, (kind, _) in enumerate(weights) if kind == "z"]
        kv_job = {n: at[("mk", 0, 0)] if ct < 2 else at[("mv", 0, 0)] for n, (kind, ct) in enumerate(weights) if kind == "kv"}
        assert len(z_jobs) == len(z_slot)

        def split_next(split, job):
            if job[:3] in z_jobs:
                p = z_jobs.index(job[:3]) + 1
                if p < len(z_jobs):
                    split(2 * p)
                    split(2 * p + 1)

        def await_slot(eng, h):
            if h >= HALVES:
                p, second = divmod(h - HALVES, 2)
                if second:
                    eng.wait_ge(pe_done, at[z_jobs[p]] + 1)
                else:
                    eng.wait_ge(s_half, p + 1)

        def half_raw(h):
            k = (h % 2) * (KD // 2)
            return wring[:, z_slot[h // 2] % WSLOTS, k:k + KD // 2, :]

        @block.sync
        def _(sp):
            for i in range(NT):
                sp.dma_start(xn[:, i, :], dram["x"][i * P:(i + 1) * P, :]).then_inc(s_x[i], 16)
            for i in range(MT):
                sp.dma_start(mem_sb[:, i, :], dram["mem"][i * P:(i + 1) * P, :]).then_inc(s_mem, 16)
            for n, (kind, ct) in enumerate(weights):
                last = n - WSLOTS
                if last in kv_job:
                    sp.wait_ge(pe_done, kv_job[last] + 1)
                elif last >= 0:
                    sp.wait_ge(s_wlo, 2 * (z_slot.index(last) + 1))
                src = dram["w_in"][ct] if kind == "z" else dram["w_kv"][ct]
                sp.dma_start(wring[:, n % WSLOTS, :, :], src).then_inc(s_w[n % WSLOTS], 16)
            sp.wait_ge(s_wlo, 2 * len(z_jobs))
            bias = bias_table(keep)
            for cq in range(WIN):
                sp.dma_start(bias[cq * ROWS:(cq + 1) * ROWS, :, :],
                             dram["na_rpb"][:, :, (WIN - 1 - cq) * ROWS:(WIN - 1 - cq) * ROWS + MAXK]).then_inc(s_bias, 16)
            sp.wait_ge(s_bias, 16 * WIN)

        consts = [(ident[:], "ident"), (gain_a[:], "attn_norm_g"), (gain_m[:], "mem_norm_g"),
                  (bound[:], "hg_lower_bound")]
        late_consts = [(masks[:], "level_masks"), (halves[:], "head_mean"), (gain_o[:], "hg_out_norm_g")]

        @block.scalar
        def _(act):
            for dst, name in consts:
                act.dma_start(dst, dram[name]).then_inc(s_const, 16)
            act.wait_ge(s_rstd, 1)
            act.activation(std[:, 0:1], eps[:, 0:1], ACT.Sqrt).then_inc(s_sq, 1)
            for i in range(NT):
                act.wait_ge(s_x[i], 16)
                act.activation(squares[:, i, :], xn[:, i, :], ACT.Square, accum_out=ss[:, i:i + 1]).then_inc(s_sq, 1)
            act.wait_ge(s_sq, NT + 1)
            act.activation(std[:, 0:NT], ss[:, 0:NT], ACT.Sqrt, bias=eps[:, 0:1], scale=1.0 / D).then_inc(s_std, 1)
            act.wait_ge(s_mem, 16 * MT)
            for i in range(MT):
                act.activation(dec[:, i, :, :].rearrange("p a t -> p (a t)"), mem_sb[:, i, :], ACT.Square,
                               accum_out=ss[:, NT + i:NT + i + 1]).then_inc(s_sq, 1)
            act.wait_ge(s_sq, NT + MT + 1)
            act.activation(std[:, NT:], ss[:, NT:], ACT.Sqrt, bias=eps[:, 0:1], scale=1.0 / D).then_inc(s_std, 1)
            for dst, name in late_consts:
                act.dma_start(dst, dram[name]).then_inc(s_late, 16)
            act.wait_ge(s_const, 16 * len(consts))

            def empty(key):
                n = at[key]
                act.wait_ge(pe_done, n + 1)
                src = bank(n)
                kind, a, b = key
                if kind == "mT":
                    return act.activation(mT[:, a, :], src[:, 0:MEM], ACT.Identity, scale=gain_m[:, a:a + 1])
                if kind == "e":
                    return act.activation(kk[:, a, b, :], src, ACT.Exp, scale=-1.0)
                if kind == "q":
                    return act.copy(q[:, a, :], src)
                if kind == "iz":
                    if a:
                        act.wait_ge(pe_done, at[("iT", 0, 0)] + 1)
                    return act.copy(nvT[:], src)
                if kind == "iT":
                    return act.copy(v[:, :, a * P:(a + 1) * P], src.rearrange("p (n c) -> p n c", n=NT))
                if kind == "mk":
                    return act.copy(mk[:], src.rearrange("p (n c) -> p n c", n=2))
                if kind == "mv":
                    return act.copy(mv[:], src.rearrange("p (n c) -> p n c", n=2))
                if kind == "mq":
                    return act.copy(mq[:, a, :], src)
                if kind in ("naq", "nak", "nav"):
                    if kind == "nav":
                        act.wait_ge(pe_done, at[("navT", a - 1, 0) if a else ("iT", 1, 0)] + 1)
                    dst = {"naq": naq[:, a, :], "nak": nak[:, a, :], "nav": nvT[:]}[kind]
                    return act.copy(dst.rearrange("p (c r) -> p r c", r=ROWS),
                                    src.rearrange("p (r c) -> p r c", r=ROWS))
                if kind == "navT":
                    return act.copy(nav[:, :, a * P:(a + 1) * P], src.rearrange("p (n c) -> p n c", n=NT))
                if kind == "g":
                    return act.copy(gz[:, a, :], src)
                if kind == "x":
                    m = b
                    row = Am[:, a % 2, m * T:(m + 1) * T]
                    if a >= 2:
                        await_emptied(act, ("o", 0, 0))
                    if 0 < m < NT - 1:
                        act.copy(row[:, 0:m * P], src[:, 0:m * P])
                    if m < NT - 1:
                        return act.copy(row[:, (m + 1) * P:], src[:, (m + 1) * P:])
                    return act.copy(row[:, 0:m * P], src[:, 0:m * P])
                if kind == "ms":
                    if a == 0:
                        act.wait_ge(s_diag, 2 * LEVELS * HPS)
                    return act.activation(orst[:, a, :], src, ACT.Sqrt, bias=eps[:, 0:1])

            def log_f():
                act.wait_ge(s_gate, 6)
                act.activation(lf, kk[:], ACT.Ln).then_inc(s_lf, 1)

            def level_exps(hp, lv):
                s = level_step(hp, lv)
                act.wait_ge(s_dec, 4 * (s + 1))
                act.activation(dec[:, s % 2, :, :], dec[:, s % 2, :, :], ACT.Exp).then_inc(s_exp, 1)

            def inter_exps(hp):
                act.wait_ge(s_idec, 2 * (hp + 1))
                if hp == 0:
                    act.activation(ebt[:], arr[:, :, :, :, P], ACT.Exp).then_inc(s_ebt, 1)
                act.activation(inter[:, hp, 1:3, :], inter[:, hp, 1:3, :], ACT.Exp).then_inc(s_iexp, 1)
                act.activation(inter[:, hp, QF, :].rearrange("p (n t) -> p n t", n=NT),
                               arr[:, 0, hp, :, 1:P + 1], ACT.Exp).then_inc(s_iexp, 1)
                act.activation(inter[:, hp, KB, :].rearrange("p (n t) -> p n t", n=NT),
                               arr[:, 1, hp, :, 0:P], ACT.Exp).then_inc(s_iexp, 1)

            def split_w(h):
                n = z_slot[h // 2]
                act.wait_ge(s_w[n % WSLOTS], 16 * (n // WSLOTS + 1))
                await_slot(act, h)
                act.copy(w_hi[:, h % HALVES, :, :], half_raw(h)).then_inc(s_whi, 1)

            early_jobs = [job for job in jobs if job[0] in ("hT", "mT")]
            split_w(0)
            split_w(1)
            for job in early_jobs:
                if job[0] == "hT":
                    k = job[1]
                    act.wait_ge(pe_done, at[job[:3]] + 1)
                    act.activation(h_hi[:, k, :], bank(at[job[:3]]), ACT.Identity, scale=gain_a[:, k:k + 1]).then_inc(s_hhi, 1)
                if job[3] == "act":
                    empty(job[:3]).then_inc(act_ev, 1)
            act.wait_ge(s_lb, 1)
            act.activation(lbt[:], lbt[:], ACT.Exp).then_inc(s_std, 1)

            for job in jobs[len(early_jobs):]:
                split_next(split_w, job)
                if job[3] == "act":
                    empty(job[:3]).then_inc(act_ev, 1)
                if job[:3] == ("iz", 1, 0):
                    log_f()
                if job[:3] == ("iT", 1, 0):
                    for s in range(AHEAD):
                        level_exps(*divmod(s, LEVELS))
                if job[0] == "lev" and job[2] % 2 == 1:
                    hp, lv = job[2] // 2, job[1]
                    prepare(level_exps, hp, lv)
                    if lv + 1 == INTER_AT:
                        inter_exps(hp)
                if job[:3] == ("g", 1, 0):
                    await_emptied(act, ("g", 1, 0))
                    act.activation(sil, gz, ACT.Exp, scale=-1.0).then_inc(s_sil, 1)

        @block.gpsimd
        def _(pool):
            pool.memset(arr[:, :, :, :, 0:1], 0.0).then_inc(s_scan, 1)

            def level_products(hp, lv):
                s = level_step(hp, lv)
                pool.wait_ge(s_exp, s + 1)
                if s >= RING:
                    pool.wait_ge(pe_done, at[("lev", (s - RING) % LEVELS, 2 * ((s - RING) // LEVELS) + 1)] + 1)
                pool.tensor_tensor(qk[:, s % RING, 0, :], q[:, hp, :], dec[:, s % 2, 0, :], ALU.mult).then_inc(s_qk, 1)
                for side in range(2):
                    pick = lambda ap: halves_of(ap.rearrange("p (n t) -> p n t", n=NT), lv)[:, :, :, side, :]
                    pool.tensor_tensor(pick(qk[:, s % RING, 1, :]), pick(kk[:, side, hp, :]),
                                       pick(dec[:, s % 2, 1, :]), ALU.mult).then_inc(s_qk, 1)

            def inter_products(hp, d):
                pool.wait_ge(s_iexp, 3 * (hp + 1))
                for kind, src in (((QF, q[:, hp, :]), (KF, kk[:, 0, hp, :])), ((QB, q[:, hp, :]), (KB, kk[:, 1, hp, :])))[d]:
                    pool.tensor_tensor(inter[:, hp, kind, :], inter[:, hp, kind, :], src, ALU.mult).then_inc(s_inter, 1)

            def far_queries(hp):
                pool.wait_ge(s_inter, 4 * (hp + 1))
                pool.wait_ge(s_ebt, 1)
                if hp:
                    pool.wait_ge(pe_done, at[("x", 1, NT - 1)] + 1)
                qf = inter[:, hp, QF, :].rearrange("p (n t) -> p n t", n=NT)
                qb = inter[:, hp, QB, :].rearrange("p (n t) -> p n t", n=NT)
                pool.tensor_scalar(ext[:, 0, :], qf[:, 2, :], ebt[:, 0, hp, 1:2], None, ALU.mult).then_inc(s_ext, 1)
                pool.tensor_scalar(ext[:, 1, :], qf[:, 3, :], ebt[:, 0, hp, 2:3], None, ALU.mult).then_inc(s_ext, 1)
                pool.tensor_scalar(ext[:, 3, :], qb[:, 0, :], ebt[:, 1, hp, 1:2], None, ALU.mult).then_inc(s_ext, 1)
                pool.tensor_scalar(ext[:, 4, :], qb[:, 1, :], ebt[:, 1, hp, 2:3], None, ALU.mult).then_inc(s_ext, 1)
                pool.wait_ge(s_ext, 6 * hp + 4)
                pool.tensor_scalar(ext[:, 2, :], ext[:, 1, :], ebt[:, 0, hp, 1:2], None, ALU.mult).then_inc(s_ext, 1)
                pool.tensor_scalar(ext[:, 5, :], ext[:, 3, :], ebt[:, 1, hp, 2:3], None, ALU.mult).then_inc(s_ext, 1)

            def rest_w(h):
                pool.wait_ge(s_whi, h + 1)
                pool.tensor_tensor(w_lo[:, h % HALVES, :, :], half_raw(h), w_hi[:, h % HALVES, :, :].bitcast(F32),
                                   ALU.subtract).then_inc(s_wlo, 1)

            rest_w(0)
            rest_w(1)
            for job in jobs:
                split_next(rest_w, job)
                if job[:3] == ("iT", 1, 0):
                    pool.wait_ge(s_k, 1)
                    await_emptied(pool, ("q", 1, 0))
                    for s in range(AHEAD):
                        level_products(*divmod(s, LEVELS))
                if job[0] == "lev" and job[2] % 2 == 1:
                    hp, lv = job[2] // 2, job[1]
                    prepare(level_products, hp, lv)
                    if INTER_AT <= lv < INTER_AT + 2:
                        inter_products(hp, lv - INTER_AT)
                    if lv == INTER_AT + 2:
                        far_queries(hp)

        @block.vector
        def _(dve):
            dve.memset(eps[:], EPS).then_inc(s_rstd, 1)
            for part, rows in enumerate((range(NT), range(NT, NT + MT))):
                c = slice(rows[0], rows[-1] + 1)
                dve.wait_ge(s_std, part + 1)
                dve.reciprocal(rstd[:, c], std[:, c]).then_inc(s_rstd, 1)
                dve.wait_ge(s_rstd, part + 2)
                for i in rows:
                    if i < NT:
                        dve.tensor_scalar(xn[:, i, :], xn[:, i, :], rstd[:, i:i + 1], None, ALU.mult).then_inc(s_xn, 1)
                    else:
                        m = mem_sb[:, i - NT, :]
                        dve.tensor_scalar(m, m, rstd[:, i:i + 1], None, ALU.mult).then_inc(s_xn, 1)
            dve.wait_ge(s_const, 16 * len(consts))
            diag_n = Tally(s_diag)

            def diag(h):
                return Am[:, h % 2, :].rearrange("p (n t) -> p n t", n=NT)[:, :, 0:P]

            def empty(key):
                n = at[key]
                dve.wait_ge(pe_done, n + 1)
                src = bank(n)
                kind, a, b = key
                if kind == "hT":
                    dve.wait_ge(s_hhi, a + 1)
                    dve.scalar_tensor_tensor(h_lo[:, a, :], src, gain_a[:, a:a + 1], h_hi[:, a, :].bitcast(F32),
                                             ALU.mult, ALU.subtract).then_inc(dve_ev, 1)
                if kind == "mT":
                    dve.tensor_scalar(mT[:, a, :], src[:, 0:MEM], gain_m[:, a:a + 1], None, ALU.mult).then_inc(dve_ev, 1)
                if kind == "lev":
                    lv, h = a, b
                    if lv == 0 and h == 0:
                        dve.wait_ge(s_late, 16 * len(late_consts))
                    mask = masks[:, lv, :].unsqueeze(1).to_broadcast([P, NT, P])
                    s4 = src.rearrange("p (n t) -> p n t", n=NT)
                    if lv == 0:
                        if h >= 2:
                            dve.wait_ge(pe_done, at[("o", 0, 0)] + 1)
                        dve.tensor_tensor(diag(h), s4, mask, ALU.mult).then_inc(dve_ev, 1)
                    else:
                        t4 = tmp[:, h % 2, :].rearrange("p (n t) -> p n t", n=NT)
                        if diag_n.n >= 2:
                            dve.wait_ge(s_diag, diag_n.n - 1)
                        dve.tensor_tensor(t4, s4, mask, ALU.mult).then_inc(dve_ev, 1)
                        dve.wait_ge(dve_ev, emptied[n][1])
                        if diag_n.n >= 2:
                            dve.wait_ge(s_diag, diag_n.n - 1)
                        diag_n.inc(dve.tensor_tensor(diag(h), diag(h), t4, ALU.add))
                if kind == "o":
                    dve.tensor_copy(oT[:, a, :], src).then_inc(dve_ev, 1)
                    dve.wait_ge(dve_ev, emptied[n][1])
                    dve.tensor_tensor(osq[:, a, :], oT[:, a, :], oT[:, a, :], ALU.mult).then_inc(s_osq, 1)

            fin = Tally(s_fin)

            def silu_gate(hp):
                dve.wait_ge(s_sil, 1)
                fin.inc(dve.tensor_scalar(sil[:, hp, :], sil[:, hp, :], 1.0, None, ALU.add))
                dve.wait_ge(s_fin, fin.n)
                fin.inc(dve.reciprocal(sil[:, hp, :], sil[:, hp, :]))
                dve.wait_ge(s_fin, fin.n)
                fin.inc(dve.tensor_tensor(sil[:, hp, :], sil[:, hp, :], gz[:, hp, :], ALU.mult))

            def head_norm(hp):
                await_emptied(dve, ("ms", hp, 0))
                dve.wait_ge(s_late, 16 * len(late_consts))
                fin.inc(dve.reciprocal(orst[:, hp, :], orst[:, hp, :]))
                dve.wait_ge(s_fin, fin.n)
                fin.inc(dve.tensor_tensor(oT[:, hp, :], oT[:, hp, :], orst[:, hp, :], ALU.mult))
                dve.wait_ge(s_fin, fin.n)
                fin.inc(dve.scalar_tensor_tensor(hg_out[:, hp, :], oT[:, hp, :], gain_o[:, hp:hp + 1], sil[:, hp, :],
                                                 ALU.mult, ALU.mult))

            def decays(hp, lv):
                s = level_step(hp, lv)
                if s >= 2:
                    dve.wait_ge(s_qk, 3 * (s - 1))
                X = [arr[:, d, hp, :, 1 - d:P + 1 - d] for d in range(2)]
                dq = halves_of(dec[:, s % 2, 0, :].rearrange("p (n t) -> p n t", n=NT), lv)
                dk = halves_of(dec[:, s % 2, 1, :].rearrange("p (n t) -> p n t", n=NT), lv)
                xf, xb = halves_of(X[0], lv), halves_of(X[1], lv)
                mf, mb = mid_of(0, hp, lv), mid_of(1, hp, lv)
                for dst, a, b in ((dq[:, :, :, 1, :], xf[:, :, :, 1, :], mf), (dq[:, :, :, 0, :], mb, xb[:, :, :, 0, :]),
                                  (dk[:, :, :, 0, :], mf, xf[:, :, :, 0, :]), (dk[:, :, :, 1, :], xb[:, :, :, 1, :], mb)):
                    dve.tensor_tensor(dst, a, b, ALU.subtract).then_inc(s_dec, 1)

            def inter_decays(hp):
                for kind, d in ((KF, 0), (QB, 1)):
                    tot = arr[:, d, hp, :, P:P + 1].to_broadcast([P, NT, P])
                    dve.tensor_tensor(inter[:, hp, kind, :].rearrange("p (n t) -> p n t", n=NT), tot,
                                      arr[:, d, hp, :, 1 - d:P + 1 - d], ALU.subtract).then_inc(s_idec, 1)

            dve.tensor_tensor(lbt[:], bound[:, :, :, 1], bound[:, :, :, 0], ALU.subtract).then_inc(s_lb, 1)

            for job in jobs:
                if job == next(j for j in jobs if j[0] == "e"):
                    dve.wait_ge(s_std, 3)
                    dve.tensor_scalar(lb1[:], lbt[:], 1.0, None, ALU.add).then_inc(s_lb, 1)
                    dve.wait_ge(s_lb, 2)
                    dve.reciprocal(lb[:], lb1[:]).then_inc(s_lb, 1)
                    dve.wait_ge(s_lb, 3)
                    dve.tensor_scalar(lb1[:], lb[:], -1.0, 1.0, ALU.mult, ALU.add).then_inc(s_lb, 1)
                if job[3] == "dve":
                    empty(job[:3])
                if job[:3] == ("lev", LEVELS - 1, 2 * (HPS - 1)):
                    silu_gate(0)
                if job[:3] == ("ms", 1, 0):
                    head_norm(1)
                if job[:3] == ("lev", LEVELS, 2 * (HPS - 1) + 1):
                    silu_gate(1)
                    head_norm(0)
                if job[:3] == ("iT", 1, 0):
                    await_emptied(dve, ("e", 1, 1))
                    dve.tensor_scalar(kk[:], kk[:], 1.0, None, ALU.add).then_inc(s_gate, 1)
                    dve.wait_ge(s_gate, 1)
                    dve.reciprocal(kk[:], kk[:]).then_inc(s_gate, 1)
                    dve.wait_ge(s_gate, 2)
                    dve.wait_ge(s_lb, 4)
                    for d in range(2):
                        for hp in range(HPS):
                            dve.tensor_scalar(kk[:, d, hp, :], kk[:, d, hp, :], lb1[:, d, hp:hp + 1], lb[:, d, hp:hp + 1],
                                              ALU.mult, ALU.add).then_inc(s_gate, 1)
                    dve.wait_ge(s_gate, 6)
                    dve.wait_ge(s_lf, 1)
                    dve.tensor_scalar(kk[:], kk[:], -1.0, 1.0, ALU.mult, ALU.add).then_inc(s_k, 1)
                    dve.wait_ge(s_scan, 1)
                    for d in range(2):
                        for hp in range(HPS):
                            for n in range(NT):
                                seg = lf[:, d, hp, n * P:(n + 1) * P]
                                dve.tensor_tensor_scan(arr[:, d, hp, n, 1:P + 1], seg, seg, 0.0,
                                                       ALU.add, ALU.bypass).then_inc(s_scan, 1)
                    dve.wait_ge(s_k, 1)
                    dve.tensor_tensor(ksum[:], kk[:, 0, :, :], kk[:, 1, :, :], ALU.add).then_inc(s_ksum, 1)
                    dve.wait_ge(s_scan, 1 + 4 * NT)
                    for s in range(AHEAD):
                        decays(*divmod(s, LEVELS))
                if job[0] == "lev" and job[2] % 2 == 0:
                    hp, lv = job[2] // 2, job[1]
                    prepare(decays, hp, lv)
                    if lv + 1 == INTER_AT:
                        inter_decays(hp)

        @block.tensor
        def _(pe):
            wpos = [0]

            def weight_slots(k):
                slots = []
                for _ in range(k):
                    n = sorted(kv_job)[wpos[0]]
                    pe.wait_ge(s_w[n % WSLOTS], 16 * (n // WSLOTS + 1))
                    slots.append(n % WSLOTS)
                    wpos[0] += 1
                return slots

            def project(out, p):
                for second in range(2):
                    h = 2 * p + second
                    pe.wait_ge(s_wlo, h + 1)
                    for j in range(KD // 2):
                        k = second * (KD // 2) + j
                        for a, b in ((w_hi, h_hi), (w_hi, h_lo), (w_lo, h_hi)):
                            last = pe.matmul(out, a[:, h % HALVES, j, :], b[:, k, :],
                                             start=(k == 0 and a is w_hi and b is h_hi), stop=(k == KD - 1 and a is w_lo))
                    if not second:
                        last.then_inc(s_half, 1)
                return last

            def run(n, key):
                kind, a, b = key
                out = bank(n)
                if kind == "hT":
                    for i in range(NT):
                        last = pe.transpose(out[:, i * P:(i + 1) * P], xn[:, i, a * P:(a + 1) * P], ident[:])
                elif kind == "mT":
                    if a == 0:
                        pe.wait_ge(s_xn, NT + MT)
                    for i in range(MT):
                        last = pe.transpose(out[:, i * P:(i + 1) * P], mem_sb[:, i, a * P:(a + 1) * P], ident[:])
                elif key in z_jobs:
                    last = project(out, z_jobs.index(key))
                elif kind == "mk":
                    for j, slot in enumerate(weight_slots(2)):
                        for k in range(KD):
                            last = pe.matmul(out[:, j * MEM:(j + 1) * MEM], wring[:, slot, k, :], mT[:, k, :],
                                             start=(k == 0), stop=(k == KD - 1))
                elif kind == "mv":
                    slots = weight_slots(2)
                    for m in range(MT):
                        for j, slot in enumerate(slots):
                            c = slice(m * MEM + j * P, m * MEM + (j + 1) * P)
                            for k in range(KD):
                                last = pe.matmul(out[:, c], mT[:, k, m * P:(m + 1) * P], wring[:, slot, k, :],
                                                 start=(k == 0), stop=(k == KD - 1))
                elif kind in ("navT", "iT"):
                    await_emptied(pe, ("nav" if kind == "navT" else "iz", a, 0))
                    for t in range(NT):
                        last = pe.transpose(out[:, t * P:(t + 1) * P], nvT[:, t * P:(t + 1) * P], ident[:])
                elif kind == "lev":
                    lv, h = a, b
                    hp, r = h // 2, slice(HD * (h % 2), HD * (h % 2) + HD)
                    if lv < LEVELS:
                        s = level_step(hp, lv)
                        pe.wait_ge(s_qk, 3 * (s + 1))
                        kt, qt = qk[r, s % RING, 1, :], qk[r, s % RING, 0, :]
                    else:
                        pe.wait_ge(s_ksum, 1)
                        kt, qt = ksum[r, hp, :], q[r, hp, :]
                    for t in range(NT):
                        c = slice(t * P, (t + 1) * P)
                        last = pe.matmul(out[:, c], kt[:, c], qt[:, c], start=True, stop=True)
                elif kind == "x":
                    h, m = a, b
                    hp, r = h // 2, slice(HD * (h % 2), HD * (h % 2) + HD)
                    if m == 0:
                        pe.wait_ge(s_ext, 6 * (hp + 1))
                    for t in range(NT):
                        if t == m:
                            continue
                        far = abs(t - m)
                        kt = inter[r, hp, KF if t > m else KB, m * P:(m + 1) * P]
                        if far == 1:
                            qt = inter[r, hp, QF if t > m else QB, t * P:(t + 1) * P]
                        elif far == 2:
                            qt = ext[r, (t - 2) if t > m else (3 + t), :]
                        else:
                            qt = ext[r, 2 if t > m else 5, :]
                        last = pe.matmul(out[:, t * P:(t + 1) * P], kt, qt, start=True, stop=True)
                elif kind == "o":
                    hp = a
                    await_emptied(pe, ("x", 2 * hp + 1, NT - 1))
                    pe.wait_ge(s_diag, 2 * LEVELS * (hp + 1))
                    for s in range(2):
                        h = 2 * hp + s
                        for m in range(NT):
                            last = pe.matmul(out[s * HD:(s + 1) * HD, :], v[:, m, h * HD:(h + 1) * HD],
                                             Am[:, s, m * T:(m + 1) * T], start=(m == 0), stop=(m == NT - 1))
                elif kind == "ms":
                    pe.wait_ge(s_osq, a + 1)
                    pe.wait_ge(s_late, 16 * len(late_consts))
                    last = pe.matmul(out, halves[:], osq[:, a, :], start=True, stop=True)
                return last

            pe.wait_ge(s_const, 16 * len(consts))
            pe.wait_ge(s_xn, NT)
            first_z = at[("e", 0, 0)]
            for n, job in enumerate(jobs):
                if n >= BANKS:
                    who, count = emptied[n - BANKS]
                    pe.wait_ge(ev[who], count)
                if n == first_z:
                    await_emptied(pe, ("hT", KD - 1, 0))
                if job[:3] == ("mk", 0, 0):
                    await_emptied(pe, ("mT", KD - 1, 0))
                    await_emptied(pe, ("mT", KD - 2, 0))
                run(n, job[:3]).then_inc(pe_done, 1)


def build_attention(nc, dram, keep, psum):
    PAIRS_NA, PAIRS = NA_HEADS // 2, (NA_HEADS + MEM_HEADS) // 2
    UNITS = PAIRS * 2 * NT
    NA_UNITS = PAIRS_NA * 2 * NT
    S_SLOTS, T_SLOTS, T_LAG, V_LAG = 5, 4, 4, 6
    with ExitStack() as ctx:
        def sb(name, shape, dt=F32):
            return ctx.enter_context(nc.sbuf_tensor(name, shape, dt))

        def sem(name):
            return ctx.enter_context(nc.semaphore(name))

        ident, x_sb, hg_out = keep["ident"], keep["x"], keep["hg_out"]
        h2hi, h2lo = keep["h2hi"], keep["h2lo"]
        naq, nak, nav = keep["naq"], keep["nak"], keep["nav"]
        mq, mk, mv = keep["mq"], keep["mk"], keep["mv"]
        mixT = sb("mixT", [P, PAIRS, T])
        bias = bias_table(keep)
        wmask = sb("wmask", [P, NT, MAXK])
        bm = sb("bias_masked", [P, 2, NT, MAXK])
        prob = sb("prob", [P, S_SLOTS, MAXK])
        probT = sb("probT", [P, T_SLOTS, MAXK])
        nmax = sb("nmax", [P, UNITS])
        total = sb("total", [P, UNITS])
        inv = sb("inv", [P, UNITS])
        w_out = sb("w_out", [P, KD, D])
        h2 = keep["ring"][:, 0:NT * D].rearrange("p (n d) -> p n d", n=NT)
        ss = sb("ss2", [P, NT])
        std = sb("std2", [P, NT])
        rstd = sb("rstd2", [P, NT])
        eps = sb("eps2", [P, 1])
        gain = sb("gain_f", [P, KD])

        s_mask, s_x = sem("mask_in"), sem("x_again")
        s_in, s_wo, s_u0 = sem("gain_in"), sem("wout_in"), sem("u_first_in")
        s_score, s_scaled, s_max, s_exp, s_inv, s_prob = (sem("score"), sem("scaled"), sem("nmax_ready"),
                                                          sem("exp_done"), sem("inv_ready"), sem("prob_ready"))
        s_turned, s_probT, s_pv, s_out, s_bm = (sem("turned"), sem("probT_ready"), sem("pv"), sem("mix_ready"),
                                                sem("bm_ready"))
        s_proj, s_x2, s_sq, s_std, s_rstd, s_h2 = (sem("proj"), sem("x2"), sem("sumsq2"), sem("std2_r"),
                                                   sem("rstd2_r"), sem("h2_ready"))
        s_hT, s_hi, s_lo = sem("h2T_pe"), sem("h2hi_r"), sem("h2lo_r")
        block = ctx.enter_context(nc.Block())

        def unit(u):
            pair, side, g = u // (2 * NT), (u // NT) % 2, u % NT
            return pair, side, g, (key_tiles(g) if pair < PAIRS_NA else [0, 1])

        def width(u):
            return P * len(unit(u)[3])

        def rows(side):
            return slice(side * HD, side * HD + HD)

        @block.sync
        def _(sp):
            sp.dma_start(wmask[:], dram["window_masks"]).then_inc(s_mask, 16)
            sp.dma_start(x_sb[:], dram["x"].rearrange("(n p) d -> p n d", p=P)).then_inc(s_x, 16)
            sp.dma_start(gain[:], dram["ffn_norm_g"]).then_inc(s_in, 16)
            sp.dma_start(w_out[:], dram["w_out"].rearrange("(k p) n -> p k n", p=P)).then_inc(s_wo, 16)
            for n in range(USLOTS):
                sp.dma_start(keep["u_raw"][:, n, :, :], dram["peer_u"][2 * GROUP + n]).then_inc(s_u0, 16)
            sp.wait_ge(s_u0, 16 * USLOTS)

        def masked_bias(eng, h):
            eng.tensor_tensor(bm[:, h % 2, :, :], wmask[:], bias[:, h, :].unsqueeze(1).to_broadcast([P, NT, MAXK]),
                              ALU.add).then_inc(s_bm, 1)

        @block.gpsimd
        def _(pool):
            pool.wait_ge(s_bm, 1)
            masked_bias(pool, 1)
            for h in range(2, NA_HEADS):
                pool.wait_ge(s_scaled, NT * (h - 1))
                masked_bias(pool, h)

        def turned_h2(i, k):
            return psum[:, 4 + 2 * (i % 2) + k // 4, (k % 4) * P:(k % 4 + 1) * P]

        def h2_parts(eng, i):
            for k in range(KD):
                if k % 4 == 0 and eng is nc.scalar:
                    eng.wait_ge(s_hT, 2 * i + k // 4 + 1)
                src, c = turned_h2(i, k), slice(i * P, (i + 1) * P)
                if eng is nc.scalar:
                    eng.activation(h2hi[:, k, c], src, ACT.Identity, scale=gain[:, k:k + 1]).then_inc(s_hi, 1)
                else:
                    eng.wait_ge(s_hi, i * KD + (k // 4 + 1) * 4)
                    eng.scalar_tensor_tensor(h2lo[:, k, c], src, gain[:, k:k + 1], h2hi[:, k, c].bitcast(F32),
                                             ALU.mult, ALU.subtract).then_inc(s_lo, 1)

        @block.scalar
        def _(act):
            def exps(u):
                w = width(u)
                act.wait_ge(s_max, u + 1)
                act.activation(prob[:, u % S_SLOTS, 0:w], prob[:, u % S_SLOTS, 0:w], ACT.Exp, bias=nmax[:, u:u + 1],
                               accum_out=total[:, u:u + 1]).then_inc(s_exp, 1)

            def move_probT(u):
                w = width(u)
                act.wait_ge(s_turned, u + 1)
                if u >= T_SLOTS:
                    act.wait_ge(s_pv, u - T_SLOTS + 1)
                act.copy(probT[:, u % T_SLOTS, 0:w], psum[:, 3 + u % 3, 0:w]).then_inc(s_probT, 1)

            def normalise(u):
                w = width(u)
                act.wait_ge(s_inv, u + 1)
                act.activation(prob[:, u % S_SLOTS, 0:w], prob[:, u % S_SLOTS, 0:w], ACT.Identity,
                               scale=inv[:, u:u + 1]).then_inc(s_prob, 1)

            for u in range(UNITS + T_LAG):
                if u < UNITS:
                    exps(u)
                if NA_UNITS < u <= UNITS:
                    normalise(u - 1)
                if u >= T_LAG:
                    move_probT(u - T_LAG)
            act.wait_ge(s_in, 16)
            for i in range(NT):
                if i:
                    h2_parts(act, i - 1)
                act.wait_ge(s_x2, 2 * (i + 1) + 1)
                act.activation(h2[:, i, :], x_sb[:, i, :], ACT.Square, accum_out=ss[:, i:i + 1]).then_inc(s_sq, 1)
                act.wait_ge(s_sq, i + 1)
                act.activation(std[:, i:i + 1], ss[:, i:i + 1], ACT.Sqrt, bias=eps[:, 0:1], scale=1.0 / D).then_inc(s_std, 1)
            h2_parts(act, NT - 1)

        @block.vector
        def _(dve):
            dve.memset(eps[:], EPS).then_inc(s_x2, 1)
            dve.wait_ge(s_mask, 16)
            masked_bias(dve, 0)

            def scaled_max(u):
                pair, side, g, keys = unit(u)
                w = width(u)
                dve.wait_ge(s_score, u + 1)
                if u >= S_SLOTS:
                    dve.wait_ge(s_turned, u - S_SLOTS + 1)
                dst = prob[:, u % S_SLOTS, 0:w]
                if pair < PAIRS_NA:
                    h = 2 * pair + side
                    dve.wait_ge(s_bm, h + 1)
                    off = (keys[0] - g + 1) * P
                    dve.scalar_tensor_tensor(dst, psum[:, u % 3, 0:w], SCALE, bm[:, h % 2, g, off:off + w],
                                             ALU.mult, ALU.add).then_inc(s_scaled, 1)
                else:
                    dve.tensor_scalar(dst, psum[:, u % 3, 0:w], SCALE, None, ALU.mult).then_inc(s_scaled, 1)
                dve.wait_ge(s_scaled, u + 1)
                dve.tensor_reduce(nmax[:, u:u + 1], dst, AX.X, ALU.max, negate=True).then_inc(s_max, 1)

            def invert(u):
                dve.wait_ge(s_exp, u + 1)
                dve.reciprocal(inv[:, u:u + 1], total[:, u:u + 1]).then_inc(s_inv, 1)

            def normalise(u):
                w = width(u)
                dve.wait_ge(s_inv, u + 1)
                dve.tensor_scalar(prob[:, u % S_SLOTS, 0:w], prob[:, u % S_SLOTS, 0:w], inv[:, u:u + 1], None,
                                  ALU.mult).then_inc(s_prob, 1)

            def move_out(pair):
                dve.wait_ge(s_pv, 2 * NT * (pair + 1))
                src = psum[:, 6 + pair % 2, :]
                if pair < PAIRS_NA:
                    dve.tensor_copy(mixT[:, pair, :].rearrange("p (r c) -> p r c", r=ROWS),
                                    src.rearrange("p (c r) -> p r c", r=ROWS)).then_inc(s_out, 1)
                else:
                    dve.tensor_copy(mixT[:, pair, :], src).then_inc(s_out, 1)

            for u in range(UNITS + V_LAG + 1):
                if u < UNITS:
                    scaled_max(u)
                if 1 <= u <= UNITS:
                    invert(u - 1)
                    if u <= NA_UNITS:
                        normalise(u - 1)
                done = u - V_LAG
                if done >= 1 and done % (2 * NT) == 0:
                    move_out(done // (2 * NT) - 1)
            dve.wait_ge(s_x, 16)
            for i in range(NT):
                for n in (2 * i, 2 * i + 1):
                    half = slice((n % 2) * BANK, (n % 2) * BANK + BANK)
                    dve.wait_ge(s_proj, n + 1)
                    dve.tensor_tensor(x_sb[:, i, half], psum[:, n % 4, :], x_sb[:, i, half], ALU.add).then_inc(s_x2, 1)
                if i:
                    h2_parts(dve, i - 1)
                dve.wait_ge(s_std, i + 1)
                dve.reciprocal(rstd[:, i:i + 1], std[:, i:i + 1]).then_inc(s_rstd, 1)
                dve.wait_ge(s_rstd, i + 1)
                dve.tensor_scalar(h2[:, i, :], x_sb[:, i, :], rstd[:, i:i + 1], None, ALU.mult).then_inc(s_h2, 1)
            h2_parts(dve, NT - 1)

        @block.tensor
        def _(pe):
            def scores(u):
                pair, side, g, keys = unit(u)
                w, r = width(u), rows(side)
                if u >= 3:
                    pe.wait_ge(s_scaled, u - 2)
                if pair < PAIRS_NA:
                    q, k = naq[r, pair, g * P:(g + 1) * P], nak[r, pair, keys[0] * P:keys[0] * P + w]
                else:
                    q, k = mq[r, pair - PAIRS_NA, g * P:(g + 1) * P], mk[r, pair - PAIRS_NA, :]
                pe.matmul(psum[:, u % 3, 0:w], q, k, start=True, stop=True).then_inc(s_score, 1)

            def turn(u):
                pe.wait_ge(s_prob, u + 1)
                if u >= 3:
                    pe.wait_ge(s_probT, u - 2)
                for j in range(len(unit(u)[3])):
                    last = pe.transpose(psum[:, 3 + u % 3, j * P:(j + 1) * P], prob[:, u % S_SLOTS, j * P:(j + 1) * P], ident[:])
                last.then_inc(s_turned, 1)

            def values(u):
                pair, side, g, keys = unit(u)
                pe.wait_ge(s_probT, u + 1)
                if u % (2 * NT) == 0 and pair >= 2:
                    pe.wait_ge(s_out, pair - 1)
                for j, kt in enumerate(keys):
                    if pair < PAIRS_NA:
                        h = 2 * pair + side
                        v = nav[:, kt, h * HD:(h + 1) * HD]
                    else:
                        h = 2 * (pair - PAIRS_NA) + side
                        v = mv[:, kt, h * HD:(h + 1) * HD]
                    last = pe.matmul(psum[rows(side), 6 + pair % 2, g * P:(g + 1) * P], v, probT[:, u % T_SLOTS, j * P:(j + 1) * P],
                                     start=(j == 0), stop=(j == len(keys) - 1))
                last.then_inc(s_pv, 1)

            for u in range(UNITS + V_LAG):
                if u < UNITS:
                    scores(u)
                if T_LAG <= u < UNITS + T_LAG:
                    turn(u - T_LAG)
                if u >= V_LAG:
                    values(u - V_LAG)
            pe.wait_ge(s_wo, 16)
            pe.wait_ge(s_out, PAIRS)
            pe.wait_ge(s_probT, UNITS)

            def turn_h2(i):
                pe.wait_ge(s_h2, i + 1)
                if i >= 2:
                    pe.wait_ge(s_lo, (i - 1) * KD)
                for k in range(KD):
                    last = pe.transpose(turned_h2(i, k), h2[:, i, k * P:(k + 1) * P], ident[:])
                    if k % 4 == 3:
                        last.then_inc(s_hT, 1)

            for n in range(2 * NT):
                i, half = n // 2, slice((n % 2) * BANK, (n % 2) * BANK + BANK)
                if n >= 4:
                    pe.wait_ge(s_x2, n - 4 + 2)
                for k in range(KD):
                    src = hg_out[:, k - 4, :] if k in (4, 5) else mixT[:, k if k < 4 else k - 2, :]
                    last = pe.matmul(psum[:, n % 4, :], src[:, i * P:(i + 1) * P], w_out[:, k, half],
                                     start=(k == 0), stop=(k == KD - 1))
                last.then_inc(s_proj, 1)
                if n % 2 == 0 and n:
                    turn_h2(i - 1)
            turn_h2(NT - 1)


def build_routing(nc, dram, keep, psum):
    HC = 2 * PH
    WSLOTS, SSLOTS = 3, 4
    with ExitStack() as ctx:
        def sb(name, shape, dt=F32):
            return ctx.enter_context(nc.sbuf_tensor(name, shape, dt))

        def sem(name):
            return ctx.enter_context(nc.semaphore(name))

        ident, chosen, acts = keep["ident"], keep["chosen"], keep["acts"]
        h2hi, h2lo, iota = keep["h2hi"], keep["h2lo"], keep["iota"]
        u_raw, u_hi, u_lo, gel = keep["u_raw"], keep["u_hi"], keep["u_lo"], keep["gel"]
        w_raw = sb("wq_raw", [P, WSLOTS, KD, P])
        w_hi = sb("wq_hi", [P, 2, KD, P], F32R)
        w_lo = sb("wq_lo", [P, 2, KD, P], F32R)
        keysT = sb("keysT", [P, HC, NKEYS])
        query = sb("query", [P, 2, T])
        scores = sb("scores", [P, SSLOTS, NT, NKEYS])
        top = sb("top", [P, HC, NT, TOPK])
        top_i = sb("top_i", [P, HC, NT, TOPK], U32)
        top_f = sb("top_f", [P, HC, NT, TOPK])
        sums = sb("sums", [P, 2, NT, TOPK * TOPK])
        best = sb("best", [P, PH, NT, TOPK])
        place = sb("place", [P, PH, NT, TOPK], U32)
        place_ab = sb("place_ab", [P, 2, 2, NT, TOPK], U32)
        ab = sb("ab", [P, 2, 2, NT, TOPK])
        pick = sb("pick", [P, 2, 2, NT, TOPK * TOPK])
        found = sb("found", [P, 3, NT, PH, TOPK])
        gsum = sb("gsum", [P, PH, NT])
        ginv = sb("ginv", [P, PH, NT])

        s_in = sem("keys_in")
        s_w = [sem(f"wq_in{i}") for i in range(WSLOTS)]
        s_whi, s_wlo = sem("wq_hi_r"), sem("wq_lo_r")
        s_u = [sem(f"u3_in{i}") for i in range(USLOTS)]
        s_uhi, s_ulo, s_act, s_gel = sem("u3_hi_r"), sem("u3_lo_r"), sem("act3_pe"), sem("gel3_r")
        s_ast = [sem("acts3_out0"), sem("acts3_out1")]
        s_q, s_qsb, s_s, s_ssb = sem("query_pe"), sem("query_sb"), sem("scores_pe"), sem("scores_sb")
        s_top, s_ab, s_eq, s_pick, s_red, s_cast = (sem("top_steps"), sem("ab_ready"), sem("eq_ready"),
                                                    sem("pick_ready"), sem("picked"), sem("top_cast"))
        s_gin, s_gexp, s_g, s_turn, s_out = (sem("gate_in"), sem("gate_exp"), sem("gate_steps"), sem("chosen_pe"),
                                             sem("chosen_sb"))
        block = ctx.enter_context(nc.Block())

        @block.sync
        def _(sp):
            for n in range(EARLY_ROUTING + 4):
                if n < HC:
                    if n >= WSLOTS:
                        sp.wait_ge(s_wlo, n - WSLOTS + 1)
                    sp.dma_start(w_raw[:, n % WSLOTS, :, :], dram["w_query"][n]).then_inc(s_w[n % WSLOTS], 16)
                if USLOTS <= n < EARLY_ROUTING + USLOTS:
                    sp.wait_ge(s_ulo, n - USLOTS + 1)
                    sp.dma_start(u_raw[:, n % USLOTS, :, :], dram["peer_u"][2 * GROUP + n]).then_inc(s_u[n % USLOTS], 16)
                if n >= 4:
                    m = n - 4
                    sp.wait_ge(s_gel, m + 1)
                    sp.dma_start(acts[m], gel[:, m % 2, :]).then_inc(s_ast[m % 2], 16)
            for i in range(2):
                sp.wait_ge(s_ast[i], 16 * (EARLY_ROUTING // 2))
            for i in range(USLOTS):
                sp.wait_ge(s_u[i], 16 * (EARLY_ROUTING // USLOTS))

        @block.scalar
        def _(act):
            def split_w(n):
                act.wait_ge(s_w[n % WSLOTS], 16 * (n // WSLOTS + 1))
                if n >= 2:
                    act.wait_ge(s_q, n - 1)
                act.copy(w_hi[:, n % 2, :, :], w_raw[:, n % WSLOTS, :, :]).then_inc(s_whi, 1)

            def split_u(n):
                if n >= USLOTS:
                    act.wait_ge(s_u[n % USLOTS], 16 * (n // USLOTS))
                if n >= 2:
                    act.wait_ge(s_act, n - 1)
                act.copy(u_hi[:, n % 2, :, :], u_raw[:, n % USLOTS, :, :]).then_inc(s_uhi, 1)

            act.dma_start(keysT[:], dram["sub_keys"]).then_inc(s_in, 16)
            act.dma_start(iota[:], dram["iota"]).then_inc(s_in, 16)
            split_u(0)
            split_u(1)
            split_w(0)
            split_w(1)
            for n in range(EARLY_ROUTING + 1):
                if n == EARLY_ROUTING:
                    act.wait_ge(s_gin, 1)
                    act.activation(best[:], best[:], ACT.Exp).then_inc(s_gexp, 1)
                if n:
                    m = n - 1
                    act.wait_ge(s_act, m + 1)
                    if m >= 2:
                        act.wait_ge(s_ast[m % 2], 16 * (m // 2))
                    act.activation(gel[:, m % 2, :], psum[:, 6 + m % 2, :], ACT.Gelu).then_inc(s_gel, 1)
                if n < HC:
                    act.wait_ge(s_q, n + 1)
                    if n >= 2:
                        act.wait_ge(s_s, n - 1)
                    act.copy(query[:, n % 2, :], psum[:, n % 2, :]).then_inc(s_qsb, 1)
                    if n + 2 < HC:
                        split_w(n + 2)
                if n < EARLY_ROUTING:
                    split_u(n + 2)
                if 1 <= n <= HC:
                    act.wait_ge(s_s, n)
                    if n > SSLOTS:
                        act.wait_ge(s_cast, n - SSLOTS)
                    act.copy(scores[:, (n - 1) % SSLOTS, :, :],
                             psum[:, 2 + (n - 1) % 2, :].rearrange("p (t k) -> p t k", t=NT)).then_inc(s_ssb, 1)
            for j in range(3):
                act.wait_ge(s_turn, j + 1)
                act.copy(chosen[:, j, :], psum[:, CHOSEN_BANKS[j], :]).then_inc(s_out, 1)

        def key_numbers(eng, h):
            for c in range(2):
                dst = pick[:, h % 2, c, :, :].rearrange("p n (s a) -> p n s a", a=TOPK)
                eng.wait_ge(s_eq, 2 * h + c + 1)
                eng.wait_ge(s_cast, 2 * h + c + 1)
                eng.tensor_tensor(dst, dst, top_f[:, 2 * h + c, :, :].unsqueeze(2).to_broadcast([P, NT, TOPK, TOPK]),
                                  ALU.mult).then_inc(s_pick, 1)

        def rest_u(eng, n):
            if n >= 2:
                eng.wait_ge(s_act, n - 1)
            eng.wait_ge(s_uhi, n + 1)
            if n == 2:
                eng.wait_ge(s_ulo, 2)
            eng.tensor_tensor(u_lo[:, n % 2, :, :], u_raw[:, n % USLOTS, :, :], u_hi[:, n % 2, :, :].bitcast(F32),
                              ALU.subtract).then_inc(s_ulo, 1)

        @block.gpsimd
        def _(pool):
            def rest_w(n):
                if n >= 2:
                    pool.wait_ge(s_q, n - 1)
                pool.wait_ge(s_whi, n + 1)
                pool.tensor_tensor(w_lo[:, n % 2, :, :], w_raw[:, n % WSLOTS, :, :], w_hi[:, n % 2, :, :].bitcast(F32),
                                   ALU.subtract).then_inc(s_wlo, 1)

            rest_w(0)
            rest_w(1)
            for n in range(EARLY_ROUTING):
                if n + 2 < HC:
                    rest_w(n + 2)
                if n + 2 <= EARLY_ROUTING:
                    rest_u(pool, n + 2)
                if n >= PICK_LAG and n % 2 == PICK_LAG % 2 and (n - PICK_LAG) // 2 < PH - 1:
                    key_numbers(pool, (n - PICK_LAG) // 2)
            rest_u(pool, EARLY_ROUTING + 1)

        @block.vector
        def _(dve):
            steps = Tally(s_top)
            rest_u(dve, 0)
            rest_u(dve, 1)
            small = iota[:, 0:TOPK].unsqueeze(1).unsqueeze(1).to_broadcast([P, NT, TOPK, TOPK])
            dve.wait_ge(s_in, 32)

            def top16(data, values, places):
                n = len(data)
                lo, hi = slice(0, 8), slice(8, 16)
                back = lambda: dve.wait_ge(s_top, steps.n - n + 1)
                for i in range(n):
                    steps.inc(dve.max(values(i)[:, lo], data[i]))
                for i in range(n):
                    back()
                    steps.inc(dve.max_index(places(i)[:, lo], values(i)[:, lo], data[i]))
                for i in range(n):
                    back()
                    steps.inc(dve.match_replace(data[i], values(i)[:, lo], data[i], NEG))
                for i in range(n):
                    back()
                    steps.inc(dve.max(values(i)[:, hi], data[i]))
                for i in range(n):
                    back()
                    steps.inc(dve.max_index(places(i)[:, hi], values(i)[:, hi], data[i]))

            def reduce_picks(h):
                dve.wait_ge(s_pick, 2 * (h + 1))
                for c in range(2):
                    dve.tensor_reduce(found[:, c, :, h, :], pick[:, h % 2, c, :, :].rearrange("p n (s a) -> p n s a", a=TOPK),
                                      AX.X, ALU.add).then_inc(s_red, 1)

            for n in range(HC):
                h = n // 2
                dve.wait_ge(s_ssb, n + 1)
                top16([scores[:, n % SSLOTS, t, :] for t in range(NT)], lambda t: top[:, n, t, :], lambda t: top_i[:, n, t, :])
                dve.wait_ge(s_top, steps.n)
                dve.tensor_copy(top_f[:, n, :, :], top_i[:, n, :, :]).then_inc(s_cast, 1)
                if n % 2:
                    s4 = sums[:, h % 2, :, :].rearrange("p n (a b) -> p n a b", b=TOPK)
                    steps.inc(dve.tensor_tensor(s4, top[:, n - 1, :, :].unsqueeze(3).to_broadcast([P, NT, TOPK, TOPK]),
                                                top[:, n, :, :].unsqueeze(2).to_broadcast([P, NT, TOPK, TOPK]), ALU.add))
                    dve.wait_ge(s_top, steps.n)
                    top16([sums[:, h % 2, t, :] for t in range(NT)], lambda t: best[:, h, t, :], lambda t: place[:, h, t, :])
                    dve.wait_ge(s_top, steps.n)
                    if h >= 2:
                        dve.wait_ge(s_eq, 2 * (h - 1))
                    steps.inc(dve.tensor_scalar(place_ab[:, h % 2, 0, :, :], place[:, h, :, :], 4, None, ALU.logical_shift_right))
                    steps.inc(dve.tensor_scalar(place_ab[:, h % 2, 1, :, :], place[:, h, :, :], 15, None, ALU.bitwise_and))
                    dve.wait_ge(s_top, steps.n)
                    dve.wait_ge(s_cast, n + 1)
                    dve.tensor_copy(ab[:, h % 2, :, :, :], place_ab[:, h % 2, :, :, :]).then_inc(s_ab, 1)
                    dve.wait_ge(s_ab, h + 1)
                    if h >= 2:
                        dve.wait_ge(s_red, 2 * (h - 1))
                    for c in range(2):
                        dst = pick[:, h % 2, c, :, :].rearrange("p n (s a) -> p n s a", a=TOPK)
                        src = ab[:, h % 2, c, :, :].unsqueeze(3).to_broadcast([P, NT, TOPK, TOPK])
                        dve.tensor_tensor(dst, src, small, ALU.is_equal).then_inc(s_eq, 1)
                    if h:
                        reduce_picks(h - 1)
            key_numbers(dve, PH - 1)
            steps.inc(dve.tensor_copy(gsum[:], best[:, :, :, 0]))
            dve.wait_ge(s_top, steps.n)
            dve.tensor_tensor(best[:], best[:], gsum[:].unsqueeze(3).to_broadcast([P, PH, NT, TOPK]), ALU.subtract).then_inc(s_gin, 1)
            reduce_picks(PH - 1)
            dve.wait_ge(s_gexp, 1)
            dve.tensor_reduce(gsum[:], best[:], AX.X, ALU.add).then_inc(s_g, 1)
            dve.wait_ge(s_g, 1)
            dve.reciprocal(ginv[:], gsum[:]).then_inc(s_g, 1)
            dve.wait_ge(s_g, 2)
            dve.tensor_tensor(found[:, 2, :, :, :].rearrange("p n h s -> p h n s"), best[:],
                              ginv[:].unsqueeze(3).to_broadcast([P, PH, NT, TOPK]), ALU.mult).then_inc(s_g, 1)

        @block.tensor
        def _(pe):
            for n in range(EARLY_ROUTING):
                pe.wait_ge(s_ulo, n + 1)
                if n >= 2:
                    pe.wait_ge(s_gel, n - 1)
                for k in range(KD):
                    for a, b in ((u_hi, h2hi), (u_hi, h2lo), (u_lo, h2hi)):
                        last = pe.matmul(psum[:, 6 + n % 2, :], a[:, n % 2, k, :], b[:, k, :],
                                         start=(k == 0 and a is u_hi and b is h2hi), stop=(k == KD - 1 and a is u_lo))
                last.then_inc(s_act, 1)
                if n < HC:
                    pe.wait_ge(s_wlo, n + 1)
                    if n >= 2:
                        pe.wait_ge(s_qsb, n - 1)
                    for k in range(KD):
                        for a, b in ((w_hi, h2hi), (w_hi, h2lo), (w_lo, h2hi)):
                            last = pe.matmul(psum[:, n % 2, :], a[:, n % 2, k, :], b[:, k, :],
                                             start=(k == 0 and a is w_hi and b is h2hi), stop=(k == KD - 1 and a is w_lo))
                    last.then_inc(s_q, 1)
                if 1 <= n <= HC:
                    m = n - 1
                    pe.wait_ge(s_in, 32)
                    pe.wait_ge(s_qsb, n)
                    if m >= 2:
                        pe.wait_ge(s_ssb, m - 1)
                    for t in range(NT):
                        last = pe.matmul(psum[:, 2 + m % 2, t * P:(t + 1) * P], query[:, m % 2, t * P:(t + 1) * P],
                                         keysT[:, m, :], start=True, stop=True)
                    last.then_inc(s_s, 1)
            pe.wait_ge(s_red, 2 * PH)
            for j in range(3):
                if j == 2:
                    pe.wait_ge(s_g, 3)
                for t in range(NT):
                    last = pe.transpose(psum[:, CHOSEN_BANKS[j], t * P:(t + 1) * P],
                                        found[:, j, t, :, :].rearrange("p h s -> p (h s)"), ident[:])
                last.then_inc(s_turn, 1)


def build_gates(nc, dram, keep, psum):
    BATCH, BATCHES = 16, 2 * CHUNK // 16
    QUADS = BATCH // 4
    HALF = BATCHES // 2
    ITERS = T // (2 * CHUNK)
    PER = BATCHES // 2
    assert EARLY_GATES == PER * ITERS and PER == USLOTS
    with ExitStack() as ctx:
        def sb(name, shape, dt=F32):
            return ctx.enter_context(nc.sbuf_tensor(name, shape, dt))

        def sem(name):
            return ctx.enter_context(nc.semaphore(name))

        chosen, gates, acts, h2hi, h2lo = keep["chosen"], keep["gates"], keep["acts"], keep["h2hi"], keep["h2lo"]
        iota, u_raw, u_hi, u_lo, gel = keep["iota"], keep["u_raw"], keep["u_hi"], keep["u_lo"], keep["gel"]
        hot_j = sb("hot_j", [P, 2, BATCH, P])
        hot_i = sb("hot_i", [P, 2, BATCH, P])
        chunk = sb("chunk", [P, 2, P, CHUNK])
        s_hot_i, s_gated, s_hot_j = sem("hot_i_r"), sem("gated_r"), sem("hot_j_r")
        s_prod, s_moved = sem("gate_prod"), sem("gate_moved")
        s_st = keep["gates_out"]
        s_u = [sem(f"u4_in{i}") for i in range(USLOTS)]
        s_uhi, s_ulo, s_act, s_gel = sem("u4_hi_r"), sem("u4_lo_r"), sem("act4_pe"), sem("gel4_r")
        s_ast = [sem("acts4_out0"), sem("acts4_out1")]
        block = ctx.enter_context(nc.Block())

        def wait(eng, s, value):
            if not (isinstance(value, int) and value <= 0):
                eng.wait_ge(s, value)

        def over_chunks(eng, body):
            body(0)
            with eng.Fori(1, ITERS) as it:
                body(it)

        @block.sync
        def _(sp):
            def load(turn, e, source):
                m = turn * USLOTS + e
                sp.wait_ge(s_act, m - USLOTS + 1)
                sp.dma_start(u_raw[:, e, :, :],
                             dram["peer_u"][bass.ds(source, 1), :, :, :].rearrange("a p k j -> p (a k) j")).then_inc(s_u[e], 16)

            def store(turn, e):
                m = turn * USLOTS + e
                sp.wait_ge(s_gel, m + 1)
                sp.dma_start(acts[bass.ds(EARLY_ROUTING + m, 1), :, :].rearrange("a j t -> j (a t)"),
                             gel[:, e % 2, :]).then_inc(s_ast[e % 2], 16)

            with sp.Fori(0, ITERS - 1) as it:
                for e in range(PER):
                    load(it + 1, e, 2 * GROUP + EARLY_ROUTING + (it + 1) * USLOTS + e)
                    store(it, e)
            for e in range(PER):
                load(ITERS, e, e)
                store(ITERS - 1, e)
            for i in range(2):
                sp.wait_ge(s_ast[i], 16 * (EARLY_GATES // 2))
            for i in range(USLOTS):
                sp.wait_ge(s_u[i], 16 * ITERS)

        @block.vector
        def _(dve):
            def one_hots(eng_it, b):
                batch = eng_it * BATCHES + b
                wait(dve, s_prod, (batch - 1) * QUADS)
                tokens = bass.ds(batch * BATCH, BATCH)
                for hot, row, ready in ((hot_i, 0, s_hot_i), (hot_j, 1, s_hot_j)):
                    dve.tensor_tensor(hot[:, b % 2, :, :], iota[:].unsqueeze(1).to_broadcast([P, BATCH, P]),
                                      chosen[:, row, tokens].unsqueeze(2).to_broadcast([P, BATCH, P]),
                                      ALU.is_equal).then_inc(ready, 1)

            def rest_u(turn, e):
                m = turn * USLOTS + e
                dve.wait_ge(s_act, m - 1)
                dve.wait_ge(s_uhi, m - 1)
                dve.tensor_tensor(u_lo[:, e % 2, :, :], u_raw[:, e % USLOTS, :, :], u_hi[:, e % 2, :, :].bitcast(F32),
                                  ALU.subtract).then_inc(s_ulo, 1)

            def body(it):
                for b in range(BATCHES):
                    one_hots(it, b)
                    if b % 2:
                        e = b // 2 + 2
                        if e < PER:
                            rest_u(it, e)
                        else:
                            rest_u(it + 1, e - PER)

            over_chunks(dve, body)

        @block.gpsimd
        def _(pool):
            with pool.Fori(0, ITERS) as it:
                for b in range(BATCHES):
                    batch = it * BATCHES + b
                    pool.wait_ge(s_hot_i, batch + 1)
                    pool.tensor_tensor(hot_i[:, b % 2, :, :], hot_i[:, b % 2, :, :],
                                       chosen[:, 2, bass.ds(batch * BATCH, BATCH)].unsqueeze(2).to_broadcast([P, BATCH, P]),
                                       ALU.mult).then_inc(s_gated, 1)

        @block.tensor
        def _(pe):
            def activations(turn, e):
                m = turn * USLOTS + e
                wait(pe, s_ulo, m - 1)
                wait(pe, s_gel, m - 1)
                for k in range(KD):
                    for a, b in ((u_hi, h2hi), (u_hi, h2lo), (u_lo, h2hi)):
                        last = pe.matmul(psum[:, 6 + e % 2, :], a[:, e % 2, k, :], b[:, k, :],
                                         start=(k == 0 and a is u_hi and b is h2hi), stop=(k == KD - 1 and a is u_lo))
                last.then_inc(s_act, 1)

            def body(it):
                for b in range(BATCHES):
                    batch = it * BATCHES + b
                    if b % 2 == 0:
                        activations(it, b // 2)
                    pe.wait_ge(s_gated, batch + 1)
                    pe.wait_ge(s_hot_j, batch + 1)
                    for q in range(QUADS):
                        wait(pe, s_moved, (batch - 1) * QUADS + q + 1)
                        for s in range(4):
                            last = pe.matmul(psum[:, q, s * P:(s + 1) * P], hot_j[:, b % 2, q * 4 + s, :],
                                             hot_i[:, b % 2, q * 4 + s, :], start=True, stop=True)
                        last.then_inc(s_prod, 1)

            over_chunks(pe, body)

        @block.scalar
        def _(act):
            def split_u(turn, e):
                m = turn * USLOTS + e
                wait(act, s_u[e], 16 * turn)
                act.wait_ge(s_act, m - 1)
                act.copy(u_hi[:, e % 2, :, :], u_raw[:, e, :, :]).then_inc(s_uhi, 1)

            def gelu(turn, e):
                m = turn * USLOTS + e
                act.wait_ge(s_act, m + 1)
                wait(act, s_ast[e % 2], (turn * (USLOTS // 2) + e // 2) * 16)
                act.activation(gel[:, e % 2, :], psum[:, 6 + e % 2, :], ACT.Gelu).then_inc(s_gel, 1)

            def body(it):
                for b in range(BATCHES):
                    batch, half = it * BATCHES + b, b // HALF
                    if b % 2 == 0:
                        e = b // 2
                        gelu(it, e)
                        if e + 2 < PER:
                            split_u(it, e + 2)
                        else:
                            split_u(it + 1, e + 2 - PER)
                    if b % HALF == 0:
                        wait(act, s_st[half], it * 16)
                    for q in range(QUADS):
                        act.wait_ge(s_prod, batch * QUADS + q + 1)
                        start = (b % HALF) * BATCH + q * 4
                        act.copy(chunk[:, half, :, start:start + 4],
                                 psum[:, q, :].rearrange("p (s i) -> p i s", s=4)).then_inc(s_moved, 1)
                    if b % HALF == HALF - 1:
                        act.wait_ge(s_moved, (batch + 1) * QUADS)
                        act.dma_start(gates[bass.ds(it * 2 + half, 1), :, :, :].rearrange("c j i t -> j (c i) t"),
                                      chunk[:, half, :, :]).then_inc(s_st[half], 16)

            over_chunks(act, body)


def build_experts(nc, dram, keep, psum):
    TILES, E = NKEYS, GROUP
    GROUPS = TILES // E
    PAIRS, EARLY_PAIRS = GROUPS // 2, EARLY // (2 * E)
    UR, VR, GR, SR = USLOTS, 2, 4, 4
    with ExitStack() as ctx:
        def sb(name, shape, dt=F32):
            return ctx.enter_context(nc.sbuf_tensor(name, shape, dt))

        def sem(name):
            return ctx.enter_context(nc.semaphore(name))

        x_sb, h2hi, h2lo, gates, acts = keep["x"], keep["h2hi"], keep["h2lo"], keep["gates"], keep["acts"]
        s_gates = keep["gates_out"]
        u_raw, u_hi, u_lo, gel = keep["u_raw"], keep["u_hi"], keep["u_lo"], keep["gel"]
        eps = sb("eps4", [P, 1])
        v_raw = sb("v_raw", [P, VR, D])
        g_sb = sb("g_sb", [P, GR, T])
        v_hi = sb("v_hi", [P, 2 * E, D], F32R)
        v_lo = sb("v_lo", [P, 2 * E, D], F32R)
        wgt = sb("wgt", [P, 2, T])
        w_hi = sb("w_hi", [P, 2 * E, T], F32R)
        w_lo = sb("w_lo", [P, 2 * E, T], F32R)
        fgain = v_raw[:, 0, :]
        ss = sb("ss4", [P, NT])
        std = sb("std4", [P, NT])
        rstd = sb("rstd4", [P, NT])

        s_u = [sem(f"u_in{i}") for i in range(UR)]
        s_v = [sem(f"v_in{i}") for i in range(VR)]
        s_g = [sem(f"g_in{i}") for i in range(GR)]
        s_uhi, s_ulo, s_vhi, s_vlo = sem("u_hi_r"), sem("u_lo_r"), sem("v_hi_r"), sem("v_lo_r")
        s_act, s_gel, s_wgt, s_whi, s_wlo = sem("act_pe"), sem("gel_r"), sem("wgt_r"), sem("w_hi_r"), sem("w_lo_r")
        s_outp, s_acc = sem("out_pe"), sem("acc_r")
        s_fg, s_sq, s_std, s_rstd, s_fin, s_store = (sem("fgain_in"), sem("sumsq4"), sem("std4_r"), sem("rstd4_r"),
                                                     sem("final_r"), sem("stored"))
        block = ctx.enter_context(nc.Block())

        def wait(eng, s, value):
            if not (isinstance(value, int) and value <= 0):
                eng.wait_ge(s, value)

        def over_pairs(eng, body):
            body(0, "first")
            with eng.Fori(1, 1 + EARLY_PAIRS) as it:
                body(it * 2, "early")
            body((1 + EARLY_PAIRS) * 2, "again")
            with eng.Fori(2 + EARLY_PAIRS, PAIRS - 1) as it:
                body(it * 2, "own")
            body((PAIRS - 1) * 2, "last")

        def own(g, e, kind):
            return g * E + e - (0 if kind == "first" else EARLY)


        @block.sync
        def _(sp):
            def load_u(g, e, kind):
                n = g * E + e
                tile = bass.ds(n, 1)
                wait(sp, s_wgt, n - UR + 1)
                if kind == "early":
                    sp.dma_start(u_raw[:, e % UR, 0:T // P, :],
                                 acts[bass.ds(n - 2 * E, 1), :, :].rearrange("a j (b c) -> j (a b) c", c=P)).then_inc(s_u[e % UR], 16)
                else:
                    sp.dma_start(u_raw[:, e % UR, :, :],
                                 dram["peer_u"][tile, :, :, :].rearrange("a p k j -> p (a k) j")).then_inc(s_u[e % UR], 16)

            def load_g(g, e):
                n = g * E + e
                wait(sp, s_wgt, n - GR + 1)
                sp.dma_start(g_sb[:, e % GR, :].rearrange("p (c t) -> p c t", t=CHUNK),
                             gates[:, :, bass.ds(n, 1), :].rearrange("c j a t -> j c (a t)")).then_inc(s_g[e % GR], 16)

            def loads(g, kind):
                if kind == "first":
                    for s in s_gates:
                        sp.wait_ge(s, 16 * (T // (2 * CHUNK)))
                for e in range(2 * E):
                    if not (kind == "first" and e < UR):
                        load_u(g, e, kind)
                    load_g(g, e)

            over_pairs(sp, loads)
            sp.wait_ge(s_vlo, TILES)
            sp.dma_start(fgain, dram["final_norm_g"].to_broadcast([P, D])).then_inc(s_fg, 16)
            for i in range(NT):
                sp.wait_ge(s_fin, 2 * i + 2)
                sp.dma_start(dram["out"][i * P:(i + 1) * P, :], x_sb[:, i, :]).then_inc(s_store, 16)
            sp.wait_ge(s_store, 16 * NT)

        @block.gpsimd
        def _(pool):
            for n in range(VR):
                pool.dma_start(v_raw[:, n, :], dram["peer_v"][n]).then_inc(s_v[n], 16)
            with pool.Fori(1, TILES // VR) as it:
                for e in range(VR):
                    n = it * VR + e
                    pool.wait_ge(s_vlo, n - VR + 1)
                    pool.dma_start(v_raw[:, e, :], dram["peer_v"][bass.ds(n, 1), :, :].rearrange("a j d -> j (a d)")).then_inc(s_v[e], 16)

        def arrived(eng, sems, g, e, slots):
            eng.wait_ge(sems[e % slots], (g * (E // slots) + e // slots + 1) * 16)

        def look_ahead(split, g, e, kind):
            if e < 2 * E - 2:
                split(g, e + 2, kind)
            elif kind in ("again", "own"):
                split(g + 2, e + 2 - 2 * E, kind)

        @block.scalar
        def _(act):
            def split_u(g, e, kind):
                wait(act, s_u[e % UR], (g * (E // UR) + e // UR) * 16)
                wait(act, s_act, own(g, e, kind) - 1)
                act.copy(u_hi[:, e % 2, :, :], u_raw[:, e % UR, :, :]).then_inc(s_uhi, 1)

            def activate(g, e, kind):
                act.wait_ge(s_act, own(g, e, kind) + 1)
                look_ahead(split_u, g, e, kind)
                wait(act, s_wgt, g * E + e - 1)
                act.activation(gel[:, e % 2, :], psum[:, e % SR, :], ACT.Gelu).then_inc(s_gel, 1)

            def body(g, kind):
                if kind == "again":
                    split_u(g, 0, kind)
                    split_u(g, 1, kind)
                if kind == "first":
                    activate(g, 0, kind)
                    activate(g, 1, kind)
                for half in range(2):
                    for e in range(half * E, half * E + E):
                        n = g * E + e
                        if kind != "early" and not (kind == "first" and e < 2):
                            activate(g, e, kind)
                        act.wait_ge(s_wgt, n + 1)
                        wait(act, s_outp, (g + half - 1) * 8)
                        act.copy(w_hi[:, e, :], wgt[:, e % 2, :]).then_inc(s_whi, 1)
                    for e in range(half * E, half * E + E):
                        arrived(act, s_v, g, e, VR)
                        act.copy(v_hi[:, e, :], v_raw[:, e % VR, :]).then_inc(s_vhi, 1)

            over_pairs(act, body)
            for i in range(NT):
                act.wait_ge(s_acc, GROUPS * 8 - (8 - 2 * (i + 1)))
                act.activation(gel[:].rearrange("p a t -> p (a t)"), x_sb[:, i, :], ACT.Square, accum_out=ss[:, i:i + 1]).then_inc(s_sq, 1)
                act.wait_ge(s_sq, i + 1)
                if i == 0:
                    act.wait_ge(s_rstd, 1)
                act.activation(std[:, i:i + 1], ss[:, i:i + 1], ACT.Sqrt, bias=eps[:, 0:1], scale=1.0 / D).then_inc(s_std, 1)

        @block.vector
        def _(dve):
            dve.memset(eps[:], EPS).then_inc(s_rstd, 1)

            def rest_u(g, e, kind):
                dve.wait_ge(s_uhi, own(g, e, kind) - 1)
                dve.tensor_tensor(u_lo[:, e % 2, :, :], u_raw[:, e % UR, :, :], u_hi[:, e % 2, :, :].bitcast(F32),
                                  ALU.subtract).then_inc(s_ulo, 1)

            def rest_v(g, e):
                dve.wait_ge(s_vhi, g * E + e + 1)
                dve.tensor_tensor(v_lo[:, e, :], v_raw[:, e % VR, :], v_hi[:, e, :].bitcast(F32), ALU.subtract).then_inc(s_vlo, 1)

            def accumulate(g, m):
                dve.wait_ge(s_outp, g * 8 + m + 1)
                dst = x_sb[:, m // 2, (m % 2) * BANK:(m % 2 + 1) * BANK]
                dve.tensor_tensor(dst, psum[:, SR + m % 4, :], dst, ALU.add).then_inc(s_acc, 1)

            def body(g, kind):
                if kind == "again":
                    rest_u(g, 0, kind)
                    rest_u(g, 1, kind)
                if kind == "first":
                    look_ahead(rest_u, g, 0, kind)
                    look_ahead(rest_u, g, 1, kind)
                for half in range(2):
                    for e in range(half * E, half * E + E):
                        n = g * E + e
                        if kind == "early":
                            dve.wait_ge(s_u[e % UR], (g * (E // UR) + e // UR) * 16)
                            activated = u_raw[:, e % UR, 0:T // P, :].rearrange("p a b -> p (a b)")
                        else:
                            if not (kind == "first" and e < 2):
                                look_ahead(rest_u, g, e, kind)
                            dve.wait_ge(s_gel, own(g, e, kind) + 1)
                            activated = gel[:, e % 2, :]
                        arrived(dve, s_g, g, e, GR)
                        wait(dve, s_wlo, n - 1)
                        dve.tensor_tensor(wgt[:, e % 2, :], activated, g_sb[:, e % GR, :], ALU.mult).then_inc(s_wgt, 1)
                        dve.wait_ge(s_whi, n + 1)
                        dve.tensor_tensor(w_lo[:, e, :], wgt[:, e % 2, :], w_hi[:, e, :].bitcast(F32), ALU.subtract).then_inc(s_wlo, 1)
                    for m in range(8):
                        if not (kind == "first" and half == 0):
                            accumulate(g + half - 1, m)
                        if m % 2 == 0:
                            rest_v(g, half * E + m // 2)

            over_pairs(dve, body)
            for m in range(8):
                accumulate(GROUPS - 1, m)
            dve.wait_ge(s_fg, 16)
            for i in range(NT):
                dve.wait_ge(s_std, i + 1)
                dve.reciprocal(rstd[:, i:i + 1], std[:, i:i + 1]).then_inc(s_rstd, 1)
                dve.wait_ge(s_rstd, i + 2)
                dve.wait_ge(s_acc, GROUPS * 8)
                for half in range(2):
                    c = slice(half * BANK, (half + 1) * BANK)
                    dve.scalar_tensor_tensor(x_sb[:, i, c], x_sb[:, i, c], rstd[:, i:i + 1], fgain[:, c],
                                             ALU.mult, ALU.mult).then_inc(s_fin, 1)

        @block.tensor
        def _(pe):
            def activations(g, e, kind):
                wait(pe, s_ulo, own(g, e, kind) - 1)
                wait(pe, s_gel, own(g, e, kind) - SR + 1)
                for k in range(KD):
                    for a, b in ((u_hi, h2hi), (u_hi, h2lo), (u_lo, h2hi)):
                        last = pe.matmul(psum[:, e % SR, :], a[:, e % 2, k, :], b[:, k, :],
                                         start=(k == 0 and a is u_hi and b is h2hi), stop=(k == KD - 1 and a is u_lo))
                last.then_inc(s_act, 1)

            def outputs(g, half):
                pe.wait_ge(s_wlo, (g + 1) * E)
                pe.wait_ge(s_vlo, (g + 1) * E)
                for m in range(8):
                    t, c = slice((m // 2) * P, (m // 2 + 1) * P), slice((m % 2) * BANK, (m % 2 + 1) * BANK)
                    wait(pe, s_acc, g * 8 + m - 3)
                    for e in range(half * E, half * E + E):
                        for a, b in ((w_hi, v_hi), (w_hi, v_lo), (w_lo, v_hi)):
                            last = pe.matmul(psum[:, SR + m % 4, :], a[:, e, t], b[:, e, c],
                                             start=(e == half * E and a is w_hi and b is v_hi),
                                             stop=(e == half * E + E - 1 and a is w_lo))
                    last.then_inc(s_outp, 1)

            def body(g, kind):
                for half in range(2):
                    if kind != "early":
                        for e in range(E):
                            activations(g, half * E + e, kind)
                    if not (kind == "first" and half == 0):
                        outputs(g + half - 1, 1 - half)

            over_pairs(pe, body)
            outputs(GROUPS - 1, 1)


def _level_masks():
    s, t = np.arange(P)[:, None], np.arange(P)[None, :]
    out = np.zeros((P, LEVELS + 1, P), np.float32)
    for lv in range(LEVELS):
        h = 64 >> lv
        out[:, lv] = (s // (2 * h) == t // (2 * h)) & (s // h != t // h)
    out[:, LEVELS] = s == t
    return out


def _window_masks():
    out = np.full((P, NT, 3, P), MASKED, np.float32)
    q = np.arange(P)
    for g in range(NT):
        cq = g * WIN + q // ROWS
        c0 = np.clip(cq - WIN // 2, 0, GRID_W - WIN)
        for j in range(3):
            ck = (g - 1 + j) * WIN + np.arange(P) // ROWS
            inside = (ck[None, :] >= c0[:, None]) & (ck[None, :] < c0[:, None] + WIN)
            out[:, g, j][inside] = 0.0
    return out


def _pairwise_rpb(rpb):
    pad = np.pad(rpb, ((0, 0), (0, 0), (WIN, WIN))).transpose(0, 2, 1)
    return np.stack([pad[:, :, ROWS - 1 - r:2 * ROWS - 1 - r] for r in range(ROWS)]).reshape(ROWS, NA_HEADS, -1)


def _tiles(w):
    return w.reshape(KD, P, -1, P).transpose(2, 1, 0, 3)


def _columns(g):
    return g.reshape(-1, P).T


def build(nc, dram):
    gates = nc.dram_tensor("gates", [T // CHUNK, NKEYS, NKEYS, CHUNK], F32).ap()
    acts = nc.dram_tensor("acts", [EARLY, NKEYS, T], F32).ap()
    with ExitStack() as ctx:
        def sb(where, name, shape, dt=F32, side=None):
            return where.enter_context(nc.sbuf_tensor(name, shape, dt, side=side))

        psum = ctx.enter_context(nc.psum_tensor("psum", [P, BANKS, BANK], F32))
        keep = {"gates": gates, "acts": acts, "ident": sb(ctx, "ident", [P, P])}
        keep["gates_out"] = [ctx.enter_context(nc.semaphore(f"gates_out{i}")) for i in range(2)]
        with ExitStack() as mixing:
            keep["ring"] = sb(mixing, "wring", [P, RING_SLOTS * KD * P])
            keep["hg_out"] = sb(mixing, "hg_out", [P, HPS, T])
            keep["naq"] = sb(mixing, "naq", [P, 4, T])
            keep["nak"] = sb(mixing, "nak", [P, 4, T])
            keep["nav"] = sb(mixing, "nav", [P, NT, NA_HEADS * HD])
            keep["mq"] = sb(mixing, "mq", [P, 2, T])
            keep["mk"] = sb(mixing, "mk", [P, 2, MEM])
            keep["mv"] = sb(mixing, "mv", [P, MT, MEM_HEADS * HD])
            build_mix(nc, dram, keep, psum)
            keep["x"] = sb(ctx, "x_sb", [P, NT, D], side="right")
            keep["h2hi"] = sb(ctx, "h2hi", [P, KD, T], F32R, side="right")
            keep["h2lo"] = sb(ctx, "h2lo", [P, KD, T], F32R, side="right")
            keep["u_raw"] = sb(ctx, "u_raw", [P, USLOTS, KD, P], side="right")
            build_attention(nc, dram, keep, psum)
        keep["iota"] = sb(ctx, "iota", [P, P])
        keep["u_hi"] = sb(ctx, "u_hi", [P, 2, KD, P], F32R)
        keep["u_lo"] = sb(ctx, "u_lo", [P, 2, KD, P], F32R)
        keep["gel"] = sb(ctx, "gel", [P, 2, T])
        with ExitStack() as routed:
            keep["chosen"] = sb(routed, "chosen", [P, 3, T])
            build_routing(nc, dram, keep, psum)
            build_gates(nc, dram, keep, psum)
        build_experts(nc, dram, keep, psum)


def kernel(x, mem, attn_norm_g, w_in, na_rpb, hg_lower_bound, hg_out_norm_g, mem_norm_g, w_mem_kv, w_out,
           ffn_norm_g, peer_w_query, peer_sub_keys, peer_u, peer_v, final_norm_g):
    import concourse.bacc as bacc
    from concourse.bass_utils import run_bass_kernel_spmd

    head_mean = np.zeros((P, P), np.float32)
    for s in range(2):
        head_mean[s * HD:(s + 1) * HD, s * HD:(s + 1) * HD] = 1.0 / HD
    a = np.asarray
    arrays = {
        "x": a(x)[0], "mem": a(mem)[0],
        "w_in": _tiles(a(w_in)[0]), "w_kv": _tiles(a(w_mem_kv)[0]), "w_query": _tiles(a(peer_w_query)[0]),
        "attn_norm_g": _columns(a(attn_norm_g)[0]), "mem_norm_g": _columns(a(mem_norm_g)[0]),
        "ffn_norm_g": _columns(a(ffn_norm_g)[0]), "hg_out_norm_g": _columns(a(hg_out_norm_g)[0]),
        "hg_lower_bound": a(hg_lower_bound).reshape(2, 2, HPS, P).transpose(3, 0, 2, 1),
        "na_rpb": _pairwise_rpb(a(na_rpb)[0]), "w_out": a(w_out)[0],
        "sub_keys": a(peer_sub_keys)[0].reshape(2 * PH, NKEYS, P).transpose(2, 0, 1),
        "peer_u": a(peer_u)[0].reshape(NKEYS, NKEYS, KD, P).transpose(0, 3, 2, 1),
        "peer_v": a(peer_v)[0].reshape(NKEYS, NKEYS, D), "final_norm_g": a(final_norm_g).reshape(1, D),
        "ident": np.eye(P, dtype=np.float32), "head_mean": head_mean, "level_masks": _level_masks(),
        "window_masks": _window_masks().reshape(P, NT, 3 * P),
        "iota": np.broadcast_to(np.arange(P, dtype=np.float32), (P, P)),
    }
    arrays = {f"in_{k}": np.ascontiguousarray(v) for k, v in arrays.items()}
    nc = bacc.Bacc("TRN2", target_bir_lowering=False, num_devices=1)
    dram = {k[3:]: nc.dram_tensor(k, v.shape, F32, kind="ExternalInput").ap() for k, v in arrays.items()}
    dram["out"] = nc.dram_tensor("out", (T, D), F32, kind="ExternalOutput").ap()
    build(nc, dram)
    r = run_bass_kernel_spmd(nc, [arrays], core_ids=[0])
    return r.results[0]["out"].reshape(1, T, D)
```
